# Optimizing a Trainium2 kernel written in Bass

```python
import jax, jax.numpy as jnp
from jax import lax
import numpy as np
import math
import jax
import jax.numpy as jnp

D_MODEL = 1024
BATCH = 1
SEQ = 256
DEPTH = 2

HGRN_HEADS = 4
HGRN_HEAD_DIM = 128
HGRN_WIDTH = HGRN_HEADS * HGRN_HEAD_DIM
HGRN_CHUNK = 64
SB_HEADS = 8
SB_HEAD_DIM = 64
SB_WIDTH = SB_HEADS * SB_HEAD_DIM
SB_BLOCK = 128
FFN_DIM = 3584
N_EXPERTS = 8
TOP_K = 2
RMS_EPS = 1e-6
IN_WIDTH = 4 * HGRN_WIDTH + 3 * SB_WIDTH + 2 * D_MODEL


def _split_points():
    sizes = [HGRN_WIDTH] * 4 + [SB_WIDTH] * 3 + [D_MODEL] * 2
    pts, acc = [], 0
    for s in sizes[:-1]:
        acc += s
        pts.append(acc)
    return pts

def rms_norm(x, g):
    x32 = x.astype(jnp.float32)
    y = x32 * lax.rsqrt(jnp.mean(x32 * x32, axis=-1, keepdims=True) + RMS_EPS)
    return (y * g.astype(jnp.float32)).astype(x.dtype)

def hgrn2_chunkwise(q, k, v, log_f):
    B, S, H, Dk = q.shape
    Dv = v.shape[-1]
    n = S // HGRN_CHUNK

    def to_chunks(t):
        return t.reshape(B, n, HGRN_CHUNK, H, t.shape[-1]).transpose(1, 0, 3, 2, 4)

    causal = jnp.tril(jnp.ones((HGRN_CHUNK, HGRN_CHUNK), dtype=bool))[:, :, None]

    def step(s_prev, inp):
        qb, kb, vb, fb = inp
        b = jnp.cumsum(fb, axis=2)
        diff = b[:, :, :, None, :] - b[:, :, None, :, :]
        decay = jnp.exp(jnp.where(causal, diff, -jnp.inf))
        scores = jnp.einsum('bhtd,bhtsd,bhsd->bhts', qb, decay, kb)
        o = (jnp.einsum('bhts,bhsv->bhtv', scores, vb)
             + jnp.einsum('bhtd,bhdv->bhtv', qb * jnp.exp(b), s_prev))
        b_last = b[:, :, -1:, :]
        s_new = (jnp.exp(b_last[:, :, 0, :])[..., None] * s_prev
                 + jnp.einsum('bhsd,bhsv->bhdv', kb * jnp.exp(b_last - b), vb))
        return s_new, o

    s0 = jnp.zeros((B, H, Dk, Dv), jnp.float32)
    _, o = lax.scan(step, s0, (to_chunks(q), to_chunks(k), to_chunks(v), to_chunks(log_f)))
    return o.transpose(1, 0, 3, 2, 4).reshape(B, S, H, Dv)

def stick_breaking_attention(q, k, v):
    B, S, H, d = q.shape
    scale = d ** -0.5
    outs = []
    for blk in range(S // SB_BLOCK):
        t0 = blk * SB_BLOCK
        kl = t0 + SB_BLOCK
        z = jnp.einsum('bthd,bshd->bhts', q[:, t0:kl], k[:, :kl]).astype(jnp.float32) * scale
        t_idx = t0 + jnp.arange(SB_BLOCK)[:, None]
        s_idx = jnp.arange(kl)[None, :]
        strict = s_idx < t_idx
        log_keep = jnp.where(strict, jax.nn.log_sigmoid(-z), 0.0)
        after = lax.cumsum(log_keep, axis=3, reverse=True) - log_keep
        w = jnp.where(strict, jnp.exp(jax.nn.log_sigmoid(z) + after), 0.0)
        outs.append(jnp.einsum('bhts,bshd->bthd', w, v[:, :kl].astype(jnp.float32)))
    return jnp.concatenate(outs, axis=1)

def hybrid_mixer(h, w_in, lb, out_norm, w_branch_a, w_branch_b, w_out):
    B, S, _ = h.shape
    proj = jnp.einsum('bsd,dn->bsn', h, w_in)
    hq, hf, hi, hog, sq, sk, sv, ga, gb = jnp.split(proj, _split_points(), axis=-1)

    def hh(t):
        return t.reshape(B, S, HGRN_HEADS, HGRN_HEAD_DIM).astype(jnp.float32)
    lb = lb.reshape(HGRN_HEADS, HGRN_HEAD_DIM)
    zf = hh(hf)
    log_f = jnp.logaddexp(jnp.log(lb), jnp.log1p(-lb) + jax.nn.log_sigmoid(zf))
    k_in = (1.0 - lb) * jax.nn.sigmoid(-zf)
    o_a = hgrn2_chunkwise(jax.nn.silu(hh(hq)), k_in, hh(hi), log_f)
    o_a = rms_norm(o_a, out_norm) * jax.nn.silu(hh(hog))
    o_a = o_a.reshape(B, S, HGRN_WIDTH).astype(h.dtype)

    def sh(t):
        return t.reshape(B, S, SB_HEADS, SB_HEAD_DIM)
    o_b = stick_breaking_attention(sh(sq), sh(sk), sh(sv)).reshape(B, S, SB_WIDTH).astype(h.dtype)

    y = (jax.nn.sigmoid(ga) * jnp.einsum('bsn,nd->bsd', o_a, w_branch_a)
         + jax.nn.sigmoid(gb) * jnp.einsum('bsn,nd->bsd', o_b, w_branch_b))
    return jnp.einsum('bsd,de->bse', y, w_out)

def swiglu(h, w_gate, w_up, w_down):
    a = jnp.einsum('...d,df->...f', h, w_gate)
    u = jnp.einsum('...d,df->...f', h, w_up)
    return jnp.einsum('...f,fd->...d', jax.nn.silu(a) * u, w_down)

def moe_swiglu(h, w_router, w_gate, w_up, w_down):
    B, S, D = h.shape
    t = h.reshape(B * S, D)
    logits = jnp.einsum('td,de->te', t, w_router).astype(jnp.float32)
    top_val, top_idx = lax.top_k(logits, TOP_K)
    top_w = jax.nn.softmax(top_val, axis=-1)
    combine = jnp.einsum('tk,tke->te', top_w, jax.nn.one_hot(top_idx, N_EXPERTS, dtype=jnp.float32))
    y = jnp.zeros((B * S, D), jnp.float32)
    for e in range(N_EXPERTS):
        y = y + combine[:, e:e + 1] * swiglu(t, w_gate[e], w_up[e], w_down[e]).astype(jnp.float32)
    return y.astype(h.dtype).reshape(B, S, D)

def first_inputs(seed: int = 0) -> dict:
    key = jax.random.key(seed)
    ks = jax.random.split(key, 20)
    f32 = jnp.float32
    n_dense = (DEPTH + 1) // 2
    n_moe = DEPTH // 2
    res = (2 * DEPTH) ** -0.5

    def nrm(k, shape, fan_in, extra=1.0):
        return jax.random.normal(k, shape, f32) * (fan_in ** -0.5) * extra

    def gain(k, shape):
        return 1.0 + 0.02 * jax.random.normal(k, shape, f32)

    return {
        'x': jax.random.normal(ks[0], (BATCH, SEQ, D_MODEL), f32),
        'mix_norm': gain(ks[1], (DEPTH, D_MODEL)),
        'w_in': nrm(ks[2], (DEPTH, D_MODEL, IN_WIDTH), D_MODEL),
        'hgrn_lb_logits': 0.5 * jax.random.normal(ks[3], (DEPTH, HGRN_WIDTH), f32),
        'hgrn_out_norm': gain(ks[4], (DEPTH, HGRN_HEAD_DIM)),
        'w_branch_hgrn': nrm(ks[5], (DEPTH, HGRN_WIDTH, D_MODEL), HGRN_WIDTH),
        'w_branch_sb': nrm(ks[6], (DEPTH, SB_WIDTH, D_MODEL), SB_WIDTH),
        'w_out': nrm(ks[7], (DEPTH, D_MODEL, D_MODEL), D_MODEL, res),
        'ffn_norm': gain(ks[8], (DEPTH, D_MODEL)),
        'dense_w_gate': nrm(ks[9], (n_dense, D_MODEL, FFN_DIM), D_MODEL),
        'dense_w_up': nrm(ks[10], (n_dense, D_MODEL, FFN_DIM), D_MODEL),
        'dense_w_down': nrm(ks[11], (n_dense, FFN_DIM, D_MODEL), FFN_DIM, res),
        'moe_router': nrm(ks[12], (n_moe, D_MODEL, N_EXPERTS), D_MODEL),
        'moe_w_gate': nrm(ks[13], (n_moe, N_EXPERTS, D_MODEL, FFN_DIM), D_MODEL),
        'moe_w_up': nrm(ks[14], (n_moe, N_EXPERTS, D_MODEL, FFN_DIM), D_MODEL),
        'moe_w_down': nrm(ks[15], (n_moe, N_EXPERTS, FFN_DIM, D_MODEL), FFN_DIM, res),
        'final_norm': gain(ks[16], (D_MODEL,)),
    }

def first_block(x, mix_norm, w_in, hgrn_lb_logits, hgrn_out_norm, w_branch_hgrn, w_branch_sb, w_out,
              ffn_norm, dense_w_gate, dense_w_up, dense_w_down, moe_router, moe_w_gate, moe_w_up,
              moe_w_down, final_norm):
    lb_all = jnp.cumsum(jax.nn.softmax(hgrn_lb_logits.astype(jnp.float32), axis=0), axis=0)
    lb_all = lb_all - lb_all[0:1]
    for layer in range(DEPTH):
        h = rms_norm(x, mix_norm[layer])
        x = x + hybrid_mixer(h, w_in[layer], lb_all[layer], hgrn_out_norm[layer],
                             w_branch_hgrn[layer], w_branch_sb[layer], w_out[layer])
        h = rms_norm(x, ffn_norm[layer])
        j = layer // 2
        if layer % 2 == 0:
            x = x + swiglu(h, dense_w_gate[j], dense_w_up[j], dense_w_down[j])
        else:
            x = x + moe_swiglu(h, moe_router[j], moe_w_gate[j], moe_w_up[j], moe_w_down[j])
    return rms_norm(x, final_norm)


GRID_W = 64
CTX_LEN = 256
HEAD_DIM = 64
MIX_WIDTH = D_MODEL
GROUP_WIDTH = MIX_WIDTH // 2
N_Q_HEADS = GROUP_WIDTH // HEAD_DIM
N_KV_HEADS = N_Q_HEADS // 4
KV_WIDTH = N_KV_HEADS * HEAD_DIM
HYENA_WIDTH = GROUP_WIDTH
HYENA_ORDER = 2
HYENA_SHORT_CONV = 3
HYENA_EMB = 33
HYENA_HIDDEN = 64
HYENA_DECAY_TARGET = 1e-2
HYENA_SHORT_DECAY_PCT = 0.3
HYENA_LONG_DECAY_PCT = 1.5
Q_BLOCK = 128
WINDOW = 128
NA_ROWS = 8
NA_COLS = 16
ROPE_THETA = 10000.0
EPS = 1e-6
NEG_INF = -1e30
N_EVEN = (DEPTH + 1) // 2
N_ODD = DEPTH // 2
EVEN_SPLITS = (GROUP_WIDTH, KV_WIDTH, KV_WIDTH, (HYENA_ORDER + 1) * HYENA_WIDTH, GROUP_WIDTH, HYENA_WIDTH)
ODD_SPLITS = (GROUP_WIDTH, KV_WIDTH, KV_WIDTH, GROUP_WIDTH, GROUP_WIDTH, GROUP_WIDTH, GROUP_WIDTH, GROUP_WIDTH)
IN_WIDTH_2 = sum(EVEN_SPLITS)


def rms_norm_2(x, g):
    xf = x.astype(jnp.float32)
    y = xf * lax.rsqrt(jnp.mean(xf * xf, axis=-1, keepdims=True) + EPS)
    return (y * g.astype(jnp.float32)).astype(x.dtype)

def adaln(cond, w, b):
    m = jnp.matmul(jax.nn.silu(cond), w) + b
    return jnp.split(m, 3, axis=-1)

def modulated_norm(x, g, shift, scale):
    return rms_norm_2(x, g) * (1 + scale) + shift

def split_cols(p, sizes):
    idx = [int(v) for v in np.cumsum(sizes)[:-1]]
    return jnp.split(p, idx, axis=-1)

def heads(t, n):
    return t.reshape(t.shape[0], t.shape[1], n, HEAD_DIM)

def axial_rope_tables(n_tokens):
    t = jnp.arange(n_tokens, dtype=jnp.int32)
    row = (t // GRID_W).astype(jnp.float32)
    col = (t % GRID_W).astype(jnp.float32)
    n_pairs = HEAD_DIM // 4
    inv = ROPE_THETA ** (-jnp.arange(n_pairs, dtype=jnp.float32) / n_pairs)
    ang = jnp.concatenate([row[:, None] * inv, col[:, None] * inv], axis=-1)
    return jnp.cos(ang), jnp.sin(ang)

def apply_rope(x, cos, sin):
    b, n, h, dh = x.shape
    xf = x.astype(jnp.float32).reshape(b, n, h, dh // 2, 2)
    x0, x1 = xf[..., 0], xf[..., 1]
    cs, sn = cos[None, :, None, :], sin[None, :, None, :]
    out = jnp.stack([x0 * cs - x1 * sn, x0 * sn + x1 * cs], axis=-1)
    return out.reshape(b, n, h, dh).astype(x.dtype)

def context_attention(q_ctx, k_ctx, v_ctx, sink_logit=None):
    b, n, h, dh = q_ctx.shape
    kv = k_ctx.shape[2]
    g = h // kv
    qg = q_ctx.reshape(b, n, kv, g, dh)
    sc = jnp.einsum('bqkgd,bckd->bkgqc', qg, k_ctx).astype(jnp.float32) * dh ** -0.5
    if sink_logit is not None:
        sink = jnp.broadcast_to(sink_logit.astype(jnp.float32).reshape(1, kv, g, 1, 1), sc.shape[:-1] + (1,))
        p = jax.nn.softmax(jnp.concatenate([sc, sink], axis=-1), axis=-1)[..., :-1]
    else:
        p = jax.nn.softmax(sc, axis=-1)
    o = jnp.einsum('bkgqc,bckd->bqkgd', p.astype(v_ctx.dtype), v_ctx)
    return o.reshape(b, n, h * dh)

def global_gqa(q, k, v, k_ctx, v_ctx):
    b, s, h, dh = q.shape
    kv = k.shape[2]
    g = h // kv
    nb = s // Q_BLOCK
    k_all = jnp.concatenate([k_ctx, k], axis=1)
    v_all = jnp.concatenate([v_ctx, v], axis=1)
    scale = dh ** -0.5
    qb = q.reshape(b, nb, Q_BLOCK, kv, g, dh).swapaxes(0, 1)

    def one_block(q_blk):
        sc = jnp.einsum('bqkgd,bnkd->bkgqn', q_blk, k_all).astype(jnp.float32) * scale
        p = jax.nn.softmax(sc, axis=-1).astype(v_all.dtype)
        return jnp.einsum('bkgqn,bnkd->bqkgd', p, v_all)

    o = lax.map(one_block, qb)
    return o.swapaxes(0, 1).reshape(b, s, h * dh)

def windowed_gqa(q, k, v, k_ctx, v_ctx, sink_logit):
    b, s, h, dh = q.shape
    kv = k.shape[2]
    g = h // kv
    nb = s // Q_BLOCK
    side = WINDOW // Q_BLOCK
    span = (2 * side + 1) * Q_BLOCK
    n_ctx = k_ctx.shape[1]
    pad = ((0, 0), (side * Q_BLOCK, side * Q_BLOCK), (0, 0), (0, 0))
    kp = jnp.pad(k, pad).reshape(b, nb + 2 * side, Q_BLOCK, kv, dh)
    vp = jnp.pad(v, pad).reshape(b, nb + 2 * side, Q_BLOCK, kv, dh)
    kb = jnp.concatenate([kp[:, j:j + nb] for j in range(2 * side + 1)], axis=2)
    vb = jnp.concatenate([vp[:, j:j + nb] for j in range(2 * side + 1)], axis=2)
    qb = q.reshape(b, nb, Q_BLOCK, kv, g, dh)
    a = jnp.arange(Q_BLOCK)[:, None]
    j = jnp.arange(span)[None, :]
    band = jnp.abs(j - side * Q_BLOCK - a) <= WINDOW
    kpos = jnp.arange(nb)[:, None] * Q_BLOCK - side * Q_BLOCK + jnp.arange(span)[None, :]
    valid = band[None] & ((kpos >= 0) & (kpos < s))[:, None, :]
    sink = sink_logit.astype(jnp.float32).reshape(kv, g, 1, 1)
    scale = dh ** -0.5

    def one_block(args):
        q_blk, k_blk, v_blk, m = args
        s_loc = jnp.einsum('bqkgd,bjkd->bkgqj', q_blk, k_blk).astype(jnp.float32) * scale
        s_loc = jnp.where(m, s_loc, NEG_INF)
        s_ctx = jnp.einsum('bqkgd,bckd->bkgqc', q_blk, k_ctx).astype(jnp.float32) * scale
        s_sink = jnp.broadcast_to(sink, s_loc.shape[:-1] + (1,))
        p = jax.nn.softmax(jnp.concatenate([s_loc, s_ctx, s_sink], axis=-1), axis=-1)
        p_loc = p[..., :span].astype(v.dtype)
        p_ctx = p[..., span:span + n_ctx].astype(v.dtype)
        return (jnp.einsum('bkgqj,bjkd->bqkgd', p_loc, v_blk)
                + jnp.einsum('bkgqc,bckd->bqkgd', p_ctx, v_ctx))

    xs = (qb.swapaxes(0, 1), kb.swapaxes(0, 1), vb.swapaxes(0, 1), valid)
    o = lax.map(one_block, xs)
    return o.swapaxes(0, 1).reshape(b, s, h * dh)

def neighbourhood_attention(q, k, v, k_ctx, v_ctx, rpb):
    b, s, h, dh = q.shape
    rows = s // GRID_W
    kr = min(NA_ROWS, rows)
    kw = min(NA_COLS, GRID_W)
    nk = kr * kw
    t = jnp.arange(s, dtype=jnp.int32)
    r = t // GRID_W
    col = t % GRID_W
    r0 = jnp.clip(r - kr // 2, 0, rows - kr)
    c0 = jnp.clip(col - kw // 2, 0, GRID_W - kw)
    key_r = r0[:, None, None] + jnp.arange(kr, dtype=jnp.int32)[None, :, None]
    key_c = c0[:, None, None] + jnp.arange(kw, dtype=jnp.int32)[None, None, :]
    key_idx = (key_r * GRID_W + key_c).reshape(s, nk)
    rel_idx = ((key_r - r[:, None, None] + NA_ROWS - 1) * (2 * NA_COLS - 1)
               + (key_c - col[:, None, None] + NA_COLS - 1)).reshape(s, nk)
    nb = s // Q_BLOCK
    rpb_flat = rpb.reshape(h, -1).astype(jnp.float32)
    scale = dh ** -0.5
    n_ctx = k_ctx.shape[1]

    def one_block(args):
        q_blk, idx, ridx = args
        kg = jnp.take(k, idx.reshape(-1), axis=1).reshape(b, Q_BLOCK, nk, h, dh)
        vg = jnp.take(v, idx.reshape(-1), axis=1).reshape(b, Q_BLOCK, nk, h, dh)
        s_loc = (jnp.einsum('bqhd,bqnhd->bhqn', q_blk, kg).astype(jnp.float32) * scale
                 + jnp.take(rpb_flat, ridx, axis=1)[None])
        s_ctx = jnp.einsum('bqhd,bchd->bhqc', q_blk, k_ctx).astype(jnp.float32) * scale
        p = jax.nn.softmax(jnp.concatenate([s_loc, s_ctx], axis=-1), axis=-1)
        p_loc = p[..., :nk].astype(v.dtype)
        p_ctx = p[..., nk:nk + n_ctx].astype(v.dtype)
        return (jnp.einsum('bhqn,bqnhd->bqhd', p_loc, vg)
                + jnp.einsum('bhqc,bchd->bqhd', p_ctx, v_ctx))

    xs = (q.reshape(b, nb, Q_BLOCK, h, dh).swapaxes(0, 1),
          key_idx.reshape(nb, Q_BLOCK, nk), rel_idx.reshape(nb, Q_BLOCK, nk))
    o = lax.map(one_block, xs)
    return o.swapaxes(0, 1).reshape(b, s, h * dh)

def hyena_positional_features(n):
    t = jnp.linspace(0.0, 1.0, n, dtype=jnp.float32)[:, None]
    bands = (HYENA_EMB - 1) // 2
    w = 2.0 * math.pi * jnp.arange(n, dtype=jnp.float32)[:, None] / n
    f = jnp.linspace(1e-4, bands - 1, bands, dtype=jnp.float32)[None, :]
    return jnp.concatenate([t, jnp.cos(f * w), -jnp.sin(f * w)], axis=-1)

def hyena_filters(n, w1, b1, w2, b2, freq, w3):
    f32 = jnp.float32
    z = hyena_positional_features(n)
    fr = freq.astype(f32)
    hdn = jnp.sin(fr * (z @ w1.astype(f32) + b1.astype(f32)))
    hdn = jnp.sin(fr * (hdn @ w2.astype(f32) + b2.astype(f32)))
    filt = hdn @ w3.astype(f32)
    t = jnp.linspace(0.0, 1.0, n, dtype=f32)[:, None]
    deltas = jnp.linspace(math.log(HYENA_DECAY_TARGET) / HYENA_LONG_DECAY_PCT,
                          math.log(HYENA_DECAY_TARGET) / HYENA_SHORT_DECAY_PCT, HYENA_WIDTH, dtype=f32)
    decay = jnp.exp(-t * jnp.abs(deltas))
    return filt.reshape(n, HYENA_ORDER, 2, HYENA_WIDTH) * decay[:, None, None, :]

def bidir_long_conv(z, h_fwd, h_bwd, d_skip):
    n = z.shape[1]
    taps = jnp.concatenate([h_fwd, jnp.zeros_like(h_fwd[:1]), h_bwd[:0:-1]], axis=0)
    taps = taps * lax.rsqrt(jnp.sum(taps * taps, axis=0, keepdims=True) + EPS)
    zf = jnp.fft.rfft(z.astype(jnp.float32), n=2 * n, axis=1)
    tf = jnp.fft.rfft(taps, n=2 * n, axis=0)
    y = jnp.fft.irfft(zf * tf[None], n=2 * n, axis=1)[:, :n]
    return (y + z.astype(jnp.float32) * d_skip.astype(jnp.float32)).astype(z.dtype)

def centred_depthwise_conv(u, w, bias):
    pad = w.shape[0] // 2
    y = lax.conv_general_dilated(u, w[:, None, :].astype(u.dtype), window_strides=(1,),
                                 padding=[(pad, pad)], dimension_numbers=('NWC', 'WIO', 'NWC'),
                                 feature_group_count=u.shape[-1])
    return y + bias

def hyena_branch(u, conv_w, conv_b, w1, b1, w2, b2, freq, w3, d_skip):
    n = u.shape[1]
    filt = hyena_filters(n, w1, b1, w2, b2, freq, w3)
    uc = centred_depthwise_conv(u, conv_w, conv_b)
    parts = jnp.split(uc, HYENA_ORDER + 1, axis=-1)
    z = parts[0]
    for o in range(HYENA_ORDER):
        z = parts[o + 1] * bidir_long_conv(z, filt[:, o, 0], filt[:, o, 1], d_skip[o])
    return z

def even_mixer(p, p_ctx, q_norm, k_norm, conv_w, conv_b, w1, b1, w2, b2, freq, w3, d_skip, cos, sin, need_ctx):
    aq, ak, av, hu, ag, hg = split_cols(p, EVEN_SPLITS)
    caq, cak, cav, chu, cag, chg = split_cols(p_ctx, EVEN_SPLITS)
    q = apply_rope(rms_norm_2(heads(aq, N_Q_HEADS), q_norm), cos, sin)
    k = apply_rope(rms_norm_2(heads(ak, N_KV_HEADS), k_norm), cos, sin)
    v = heads(av, N_KV_HEADS)
    k_c = rms_norm_2(heads(cak, N_KV_HEADS), k_norm)
    v_c = heads(cav, N_KV_HEADS)
    y_a = global_gqa(q, k, v, k_c, v_c)
    y_b = hyena_branch(hu, conv_w, conv_b, w1, b1, w2, b2, freq, w3, d_skip)
    y = jnp.concatenate([y_a * jax.nn.silu(ag), y_b * jax.nn.silu(hg)], axis=-1)
    if not need_ctx:
        return y, None
    q_c = rms_norm_2(heads(caq, N_Q_HEADS), q_norm)
    y_ca = context_attention(q_c, k_c, v_c)
    y_cb = hyena_branch(chu, conv_w, conv_b, w1, b1, w2, b2, freq, w3, d_skip)
    y_c = jnp.concatenate([y_ca * jax.nn.silu(cag), y_cb * jax.nn.silu(chg)], axis=-1)
    return y, y_c

def odd_mixer(p, p_ctx, wq_norm, wk_norm, sink, nq_norm, nk_norm, rpb, cos, sin, need_ctx):
    wq, wk, wv, nq, nk_, nv, wg, ng = split_cols(p, ODD_SPLITS)
    cwq, cwk, cwv, cnq, cnk, cnv, cwg, cng = split_cols(p_ctx, ODD_SPLITS)
    q_w = apply_rope(rms_norm_2(heads(wq, N_Q_HEADS), wq_norm), cos, sin)
    k_w = apply_rope(rms_norm_2(heads(wk, N_KV_HEADS), wk_norm), cos, sin)
    v_w = heads(wv, N_KV_HEADS)
    kc_w = rms_norm_2(heads(cwk, N_KV_HEADS), wk_norm)
    vc_w = heads(cwv, N_KV_HEADS)
    y_w = windowed_gqa(q_w, k_w, v_w, kc_w, vc_w, sink)
    q_n = rms_norm_2(heads(nq, N_Q_HEADS), nq_norm)
    k_n = rms_norm_2(heads(nk_, N_Q_HEADS), nk_norm)
    v_n = heads(nv, N_Q_HEADS)
    kc_n = rms_norm_2(heads(cnk, N_Q_HEADS), nk_norm)
    vc_n = heads(cnv, N_Q_HEADS)
    y_n = neighbourhood_attention(q_n, k_n, v_n, kc_n, vc_n, rpb)
    y = jnp.concatenate([y_w * jax.nn.silu(wg), y_n * jax.nn.silu(ng)], axis=-1)
    if not need_ctx:
        return y, None
    y_cw = context_attention(rms_norm_2(heads(cwq, N_Q_HEADS), wq_norm), kc_w, vc_w, sink)
    y_cn = context_attention(rms_norm_2(heads(cnq, N_Q_HEADS), nq_norm), kc_n, vc_n)
    y_c = jnp.concatenate([y_cw * jax.nn.silu(cwg), y_cn * jax.nn.silu(cng)], axis=-1)
    return y, y_c

def second_inputs(seed: int = 0) -> dict:
    key = jax.random.key(seed)
    keys = iter(jax.random.split(key, 32))

    def nrm(shape, std):
        return std * jax.random.normal(next(keys), shape, jnp.float32)

    n_filter_out = HYENA_ORDER * 2 * HYENA_WIDTH
    n_hy_in = (HYENA_ORDER + 1) * HYENA_WIDTH
    return {
        'x': nrm((BATCH, SEQ, D_MODEL), 1.0),
        'c': nrm((BATCH, D_MODEL), 1.0),
        'ctx': nrm((BATCH, CTX_LEN, D_MODEL), 1.0),
        'c_ctx': nrm((D_MODEL,), 1.0),
        'norm_g': 1.0 + nrm((DEPTH, D_MODEL), 0.1),
        'w_ada': nrm((DEPTH, D_MODEL, 3 * D_MODEL), D_MODEL ** -0.5),
        'b_ada': nrm((DEPTH, 3 * D_MODEL), 0.01),
        'w_in': nrm((DEPTH, D_MODEL, IN_WIDTH_2), D_MODEL ** -0.5),
        'w_out': nrm((DEPTH, MIX_WIDTH, D_MODEL), MIX_WIDTH ** -0.5),
        'glob_q_norm': 1.0 + nrm((N_EVEN, HEAD_DIM), 0.1),
        'glob_k_norm': 1.0 + nrm((N_EVEN, HEAD_DIM), 0.1),
        'hy_conv_w': nrm((N_EVEN, HYENA_SHORT_CONV, n_hy_in), HYENA_SHORT_CONV ** -0.5),
        'hy_conv_b': nrm((N_EVEN, n_hy_in), 0.01),
        'hy_w1': nrm((N_EVEN, HYENA_EMB, HYENA_HIDDEN), HYENA_EMB ** -0.5),
        'hy_b1': nrm((N_EVEN, HYENA_HIDDEN), 0.01),
        'hy_w2': nrm((N_EVEN, HYENA_HIDDEN, HYENA_HIDDEN), HYENA_HIDDEN ** -0.5),
        'hy_b2': nrm((N_EVEN, HYENA_HIDDEN), 0.01),
        'hy_freq': 1.0 + nrm((N_EVEN, HYENA_HIDDEN), 0.1),
        'hy_w3': nrm((N_EVEN, HYENA_HIDDEN, n_filter_out), HYENA_HIDDEN ** -0.5),
        'hy_skip': nrm((N_EVEN, HYENA_ORDER, HYENA_WIDTH), 0.5),
        'win_q_norm': 1.0 + nrm((N_ODD, HEAD_DIM), 0.1),
        'win_k_norm': 1.0 + nrm((N_ODD, HEAD_DIM), 0.1),
        'win_sink': nrm((N_ODD, N_Q_HEADS), 0.5),
        'nat_q_norm': 1.0 + nrm((N_ODD, HEAD_DIM), 0.1),
        'nat_k_norm': 1.0 + nrm((N_ODD, HEAD_DIM), 0.1),
        'nat_rpb': nrm((N_ODD, N_Q_HEADS, 2 * NA_ROWS - 1, 2 * NA_COLS - 1), 0.1),
    }

def second_block(x, c, ctx, c_ctx, norm_g, w_ada, b_ada, w_in, w_out,
              glob_q_norm, glob_k_norm, hy_conv_w, hy_conv_b, hy_w1, hy_b1, hy_w2, hy_b2,
              hy_freq, hy_w3, hy_skip, win_q_norm, win_k_norm, win_sink,
              nat_q_norm, nat_k_norm, nat_rpb):
    cos, sin = axial_rope_tables(x.shape[1])
    x_ctx = ctx
    for layer in range(DEPTH):
        need_ctx = layer < DEPTH - 1
        shift, scale, gate = adaln(c, w_ada[layer], b_ada[layer])
        c_shift, c_scale, c_gate = adaln(c_ctx, w_ada[layer], b_ada[layer])
        h = modulated_norm(x, norm_g[layer], shift[:, None], scale[:, None])
        h_ctx = modulated_norm(x_ctx, norm_g[layer], c_shift, c_scale)
        p = jnp.matmul(h, w_in[layer])
        p_ctx = jnp.matmul(h_ctx, w_in[layer])
        i = layer // 2
        if layer % 2 == 0:
            y, y_ctx = even_mixer(p, p_ctx, glob_q_norm[i], glob_k_norm[i], hy_conv_w[i], hy_conv_b[i],
                                  hy_w1[i], hy_b1[i], hy_w2[i], hy_b2[i], hy_freq[i], hy_w3[i], hy_skip[i],
                                  cos, sin, need_ctx)
        else:
            y, y_ctx = odd_mixer(p, p_ctx, win_q_norm[i], win_k_norm[i], win_sink[i],
                                 nat_q_norm[i], nat_k_norm[i], nat_rpb[i], cos, sin, need_ctx)
        x = x + gate[:, None] * jnp.matmul(y, w_out[layer])
        if need_ctx:
            x_ctx = x_ctx + c_gate * jnp.matmul(y_ctx, w_out[layer])
    return x


def setup_inputs(seed=0):
    out = dict(first_inputs(seed))
    for name, value in second_inputs(seed + 1).items():
        if name != "x":
            out[name + "_2"] = value
    return out


def reference(
    x, mix_norm, w_in, hgrn_lb_logits, hgrn_out_norm, w_branch_hgrn, w_branch_sb, w_out,
    ffn_norm, dense_w_gate, dense_w_up, dense_w_down, moe_router, moe_w_gate, moe_w_up,
    moe_w_down, final_norm, c_2, ctx_2, c_ctx_2, norm_g_2, w_ada_2, b_ada_2, w_in_2, w_out_2,
    glob_q_norm_2, glob_k_norm_2, hy_conv_w_2, hy_conv_b_2, hy_w1_2, hy_b1_2, hy_w2_2, hy_b2_2,
    hy_freq_2, hy_w3_2, hy_skip_2, win_q_norm_2, win_k_norm_2, win_sink_2, nat_q_norm_2,
    nat_k_norm_2, nat_rpb_2,
):
    x = first_block(
        x, mix_norm, w_in, hgrn_lb_logits, hgrn_out_norm, w_branch_hgrn, w_branch_sb, w_out,
        ffn_norm, dense_w_gate, dense_w_up, dense_w_down, moe_router, moe_w_gate, moe_w_up,
        moe_w_down, final_norm,
    )
    return second_block(
        x, c_2, ctx_2, c_ctx_2, norm_g_2, w_ada_2, b_ada_2, w_in_2, w_out_2, glob_q_norm_2,
        glob_k_norm_2, hy_conv_w_2, hy_conv_b_2, hy_w1_2, hy_b1_2, hy_w2_2, hy_b2_2, hy_freq_2,
        hy_w3_2, hy_skip_2, win_q_norm_2, win_k_norm_2, win_sink_2, nat_q_norm_2, nat_k_norm_2,
        nat_rpb_2,
    )


_drawn_inputs = setup_inputs


def setup_inputs(seed=0):
    import zlib

    import numpy as np

    out = dict(_drawn_inputs(seed))
    spreads = {}
    factors = {'hgrn_lb_logits': 2.962,
     'hgrn_out_norm': 2.982,
     'glob_q_norm_2': 8.0,
     'glob_k_norm_2': 8.0,
     'hy_conv_b_2': 2.693,
     'win_q_norm_2': 8.0,
     'win_k_norm_2': 8.0,
     'win_sink_2': 8.0,
     'nat_q_norm_2': 8.0,
     'nat_k_norm_2': 8.0,
     'nat_rpb_2': 38.292}
    for name, (base, spread) in spreads.items():
        noise = np.random.default_rng([zlib.crc32(name.encode()), seed]).standard_normal(out[name].shape)
        drawn = base * np.exp(spread * noise) if base else spread * noise
        out[name] = jnp.asarray(drawn.astype(out[name].dtype))
    for name, factor in factors.items():
        out[name] = (out[name] * factor).astype(out[name].dtype)
    return out
```

```python
from contextlib import ExitStack

import numpy as np

import concourse.bass as bass
from concourse import mybir

F32 = mybir.dt.float32
BF16 = mybir.dt.bfloat16
I32 = mybir.dt.int32
ACT = mybir.ActivationFunctionType
ALU = mybir.AluOpType
AX = mybir.AxisListType

P = 128
D = 1024
KD = D // P
S = 256
F = 3584
E = 8
PW = 2048
RING = 6
EPS = 1e-6
PI = float(np.pi)

IN1 = 22
IN2 = 13
ADA = 12
OUTP = 4
FSTEP = F // 256
FFN = 3 * FSTEP
LAYER1 = IN1 + OUTP + OUTP
BLOCK1 = LAYER1 + FFN + LAYER1 + E * FFN
LAYER2 = ADA + IN2 + OUTP
PANELS = BLOCK1 + 2 * LAYER2

HQ, HF, HOG, SQ, SK, GA, GB = 0, 4, 8, 12, 16, 20, 28
HI, SV = 18, 20
C_Q, C_K, C_V, C_HU, C_G, C_HG = 0, 4, 5, 6, 18, 22
C_NQ, C_NK, C_NV = 6, 10, 14

(K_ID, K_ONE, K_1024, K_128, K_BD, K_SWAP, K_TRI, K_NEG, K_LEV, K_STRICT, K_COS, K_SIN, K_WIN, K_NBR,
 K_LOW) = np.cumsum([0, 128, 128, 128, 128, 128, 128, 128, 128, 896, 128, 256, 256, 512, 256]).tolist()
K_EPS = K_LOW + 64
K_N = K_EPS + 1
S_MIX, S_FFN, S_FIN, S_NG, S_ON, S_LB, S_QK, S_CW, S_CB, S_SINK, S_ADA, S_ROUT, S_COND, S_HYP = np.cumsum(
    [0, 16, 16, 8, 16, 2, 8, 6, 36, 12, 8, 48, 64, 16]).tolist()
S_N = S_HYP + 3


def constants():
    c = np.zeros((P, K_N), np.float32)
    i, j = np.arange(P)[:, None], np.arange(P)[None, :]
    c[:, K_ID:K_ID + P] = i == j
    c[:, K_ONE:K_ONE + P] = 1.0
    c[:, K_1024:K_1024 + P] = 1.0 / D
    c[:, K_128:K_128 + P] = 1.0 / P
    c[:, K_BD:K_BD + P] = (i // 64 == j // 64) / 64.0
    c[:, K_SWAP:K_SWAP + P] = ((j % 2 == 1) & (i == j - 1)) * 1.0 - ((j % 2 == 0) & (i == j + 1)) * 1.0
    c[:, K_TRI:K_TRI + P] = -1.0 * (i >= j)
    c[:, K_NEG:K_NEG + P] = -1.0
    for lv in range(7):
        c[:, K_LEV + lv * P:K_LEV + (lv + 1) * P] = ((i >> lv) % 2 == 0) & ((j >> lv) == (i >> lv) + 1)
    c[:, K_STRICT:K_STRICT + P] = i < j
    t = np.arange(S)
    inv = 10000.0 ** (-np.arange(16, dtype=np.float32) / np.float32(16))
    ang = np.concatenate([(t // 64).astype(np.float32)[:, None] * inv, (t % 64).astype(np.float32)[:, None] * inv], -1)
    pair = (np.arange(P) % 64) // 2
    c[:, K_COS:K_COS + S] = np.cos(ang.astype(np.float32)).T[pair]
    c[:, K_SIN:K_SIN + S] = np.sin(ang.astype(np.float32)).T[pair]
    for qt in range(2):
        q = qt * P + np.arange(P)[:, None]
        c[:, K_WIN + qt * S:K_WIN + (qt + 1) * S] = np.where(np.abs(t[None, :] - q) <= 128, 0.0, -1e30)
    c0 = np.clip(np.arange(P) % 64 - 8, 0, 48)[:, None]
    kc = 63 - (t % 64)[None, :]
    c[:, K_NBR:K_NBR + S] = np.where((kc >= c0) & (kc < c0 + 16), 0.0, -1e30)
    low = (np.arange(8)[None, :] < np.arange(8)[:, None]) * 1.0
    c[:, K_LOW:K_LOW + 64] = low.reshape(1, 64)
    c[:, K_EPS] = EPS
    return c


def dft_tables():
    t = np.arange(S, dtype=np.float64)
    a = np.pi * np.outer(t, 2 * t + 1) / 512.0
    rows = lambda m: m.reshape(2, P, S).transpose(1, 0, 2).reshape(P, 2 * S)
    return np.concatenate([rows(np.cos(a)), rows(np.sin(a)), rows(np.cos(a).T / 256), rows(np.sin(a).T / 256)],
                          1).astype(np.float32)


def decay_table():
    t = np.linspace(0.0, 1.0, S, dtype=np.float32)[:, None]
    deltas = np.linspace(np.log(1e-2) / 1.5, np.log(1e-2) / 0.3, 512, dtype=np.float32)
    d = np.exp(-t * np.abs(deltas)).astype(np.float32)
    return d.reshape(2, P, 512).transpose(1, 0, 2).reshape(P, 1024)


def position_table():
    t = np.linspace(0.0, 1.0, S, dtype=np.float32)[:, None]
    w = (2.0 * np.pi * np.arange(S, dtype=np.float32)[:, None] / S).astype(np.float32)
    f = np.linspace(1e-4, 15, 16, dtype=np.float32)[None, :]
    return np.concatenate([t, np.cos(f * w), -np.sin(f * w)], -1).T.astype(np.float32)


def two_blocks(nc, panels, x_in, ctx_in, consts_in, small_in, dft_in, decay_in, pos_in, w1_in, w2_in, w3_in,
               skip_in, rpb_in, out):
    stack = ExitStack()
    with stack:
        def sb(name, words, parts=P, dt=F32):
            return stack.enter_context(nc.sbuf_tensor(name, [parts, words], dt))

        sems = {}

        def sem(name):
            if name not in sems:
                sems[name] = stack.enter_context(nc.semaphore(name))
            return sems[name]

        seen = {}

        def nth(eng, name, k=1):
            key = (eng.engine, name)
            seen[key] = seen.get(key, 0) + k
            return seen[key]

        ring = sb("ring", RING * PW)
        xT = sb("xT", KD * S)
        cT = sb("cT", KD * S)
        hT = sb("hT", KD * 512)
        proj = sb("proj", 26 * 512)
        yT = sb("yT", KD * 512)
        arena = sb("arena", 9728)
        cst = sb("cst", K_N)
        sml = sb("sml", S_N)
        rstd = sb("rstd", 512)
        ada = sb("ada", 48)
        ada_a = sb("ada_a", 16)
        cond = sb("cond", 16)
        lbs = sb("lbs", 32)
        stat = sb("stat", 16)
        rt = sb("rt", 400)
        zrow = sb("zrow", 640, dt=BF16)
        ps = stack.enter_context(nc.psum_tensor("ps", [P, 8, 512], F32))

        h3 = hT[:, :].rearrange("p (k n) -> p k n", k=KD)
        y3 = yT[:, :].rearrange("p (k n) -> p k n", k=KD)
        x3 = xT[:, :].rearrange("p (k n) -> p k n", k=KD)
        c3 = cT[:, :].rearrange("p (k n) -> p k n", k=KD)
        ones1 = cst[:, K_ONE:K_ONE + 1]
        eps1 = cst[:, K_EPS:K_EPS + 1]

        def K(at, n=P):
            return cst[:, at:at + n]

        def bank(b, n=1):
            return ps[:, b:b + n, :].rearrange("p b n -> p (b n)")

        def slot(p, a, b):
            s = p % RING
            return ring[:, s * PW + a:s * PW + b]

        def qk_chunks(layer):
            if layer == 0:
                return [(C_Q + c, 512, 0, True) for c in range(4)] + [(C_K, 512, 1, True)]
            return ([(C_Q + c, S, 2, True) for c in range(4)] + [(C_K, 512, 3, True)]
                    + [(C_NQ + c, S, 4, False) for c in range(4)] + [(C_NK + c, 512, 5, False) for c in range(4)])

        def attention_units(layer):
            us = []

            def gqa(c, half, qt, stream, kind):
                r = slice(half * 64, half * 64 + 64)
                first = 0 if stream == 0 else 2
                us.append(dict(
                    half=half, keys=512 if stream == 0 else 256, kind=kind,
                    q=proj[r, (C_Q + c) * 512 + stream * S + qt * P:][:, 0:P],
                    k=proj[r, C_K * 512 + stream * S:(C_K + 1) * 512],
                    v=lambda n: proj[:, C_V * 512 + (first + n) * P + half * 64:][:, 0:64],
                    mask=K(K_WIN + qt * S, S).rearrange("p (r c) -> p r c", r=4),
                    sink=sml[:, S_SINK + c + 4 * half:S_SINK + c + 4 * half + 1],
                    gate=proj[r, (C_G + c) * 512 + stream * S + qt * P:][:, 0:P],
                    y=yT[r, c * 512 + stream * S + qt * P:][:, 0:P]))

            def neighbour(h, qt):
                half, c = h % 2, h // 2
                r = slice(half * 64, half * 64 + 64)
                us.append(dict(
                    half=half, keys=512, kind="neighbour",
                    q=proj[r, (C_NQ + c) * 512 + qt * P:][:, 0:P], k=proj[r, (C_NK + c) * 512:(C_NK + c + 1) * 512],
                    v=lambda n: proj[:, (C_NV + 2 * (h // 4)) * 512 + n * S + (h % 4) * 64:][:, 0:64],
                    mask=arena[:, (h * 2 + qt) * S:(h * 2 + qt + 1) * S].rearrange("p (r c) -> p r c", r=4)[:, :, ::-1],
                    gate=proj[r, (C_HG + c) * 512 + qt * P:][:, 0:P],
                    y=yT[r, (4 + c) * 512 + qt * P:][:, 0:P]))

            if layer == 0:
                for c in range(4):
                    for half in range(2):
                        for stream in range(2):
                            for qt in range(2):
                                gqa(c, half, qt, stream, "plain")
            else:
                for c in range(4):
                    for half in range(2):
                        for qt in range(2):
                            gqa(c, half, qt, 0, "window")
                for h in range(8):
                    for qt in range(2):
                        neighbour(h, qt)
            return us

        def qk_root(i):
            return arena[:, 7424:7936] if i % 2 else rstd[:, :]

        def scores_sb(i):
            return arena[:, 4096 + (i % 2) * 520:4096 + (i % 2) * 520 + 520]

        block = stack.enter_context(nc.Block())
        LANDED = [sem(f"panel_landed_{s}") for s in range(RING)]
        DONE = sem("panels_multiplied")

        @block.sync
        def _(sp):
            def load(p, s):
                sp.dma_start(ring[:, s * PW:(s + 1) * PW], panels[bass.ds(p, 1), :, :].rearrange("a p n -> p (a n)")) \
                  .then_inc(LANDED[s], 16)

            for s in range(RING):
                load(s, s)
            full = PANELS // RING
            with sp.Fori(1, full) as r:
                for s in range(RING):
                    sp.wait_ge(DONE, r * RING + (s - RING + 1))
                    load(r * RING + s, s)
            for p in range(full * RING, PANELS):
                sp.wait_ge(DONE, p - RING + 1)
                load(p, p % RING)

        @block.tensor
        def _(pe):
            at = [0]

            def mm(o, w, m, start, stop, skip=False):
                return nc.tensor.matmul(o, w, m, start=start, stop=stop, skip_group_check=skip)

            def landed(p, rounds=0):
                pe.wait_ge(LANDED[p % RING], 16 * (p // RING + 1) + rounds * 16)

            def take():
                p = at[0]
                at[0] += 1
                landed(p)
                return p

            def panel_T(p, b, n, rhs):
                for m in range(2):
                    o = bank(b)[:, m * 256:m * 256 + n] if n <= 256 else bank(b + m)
                    for k in range(KD):
                        last = mm(o, slot(p, k * 256 + m * P, k * 256 + (m + 1) * P), rhs(k), k == 0, k == KD - 1)
                return last

            def norm(streams=1):
                pe.wait_ge(sem("squares_ready"), nth(pe, "squares_ready"))
                for s in range(streams):
                    for k in range(KD):
                        last = mm(bank(0)[:, s * S:(s + 1) * S], K(K_1024), h3[:, k, s * S:(s + 1) * S],
                                  k == 0, k == KD - 1)
                last.then_inc(sem("mean_square_ready"), 1)

            def project1():
                pe.wait_ge(sem("h_ready"), nth(pe, "h_ready", KD))
                for p in range(IN1):
                    q = take()
                    if p >= 8:
                        copied = "proj_even_copied" if p % 2 == 0 else "proj_odd_copied"
                        pe.wait_ge(sem(copied), nth(pe, copied))
                    if p < 18:
                        last = panel_T(q, p % 8, S, lambda k: h3[:, k, 0:S])
                    else:
                        for tb in range(2):
                            for k in range(KD):
                                last = mm(bank(p % 8)[:, tb * S:(tb + 1) * S], h3[:, k, tb * P:(tb + 1) * P],
                                          slot(q, k * 256, (k + 1) * 256), k == 0, k == KD - 1)
                    last.then_inc(DONE, 1)
                seen[(pe.engine, "proj_even_copied")] += 4
                seen[(pe.engine, "proj_odd_copied")] += 4

            def hgrn():
                q = arena[:, 0:1024]
                kk = arena[:, 1024:2048]
                X = [arena[:, 5120:6144], arena[:, 6144:7168]]
                pe.wait_ge(sem("hgrn_qk_ready"), nth(pe, "hgrn_qk_ready"))
                for h in range(8):
                    last = mm(bank(0, 2)[:, h * P:(h + 1) * P], kk[:, h * P:(h + 1) * P], q[:, h * P:(h + 1) * P],
                              True, True)
                last.then_inc(sem("level_scores_ready"), 1)
                for lv in range(8):
                    pe.wait_ge(sem("level_q_ready"), nth(pe, "level_q_ready"))
                    pe.wait_ge(sem("level_k_ready"), nth(pe, "level_k_ready"))
                    x = X[lv % 2]
                    if lv >= 1:
                        pe.wait_ge(sem("level_merged"), nth(pe, "level_merged"))
                    if lv < 7:
                        for h in range(8):
                            xs = x[:, h * P:(h + 1) * P]
                            last = mm(bank(2 - 2 * (lv % 2), 2)[:, h * P:(h + 1) * P], xs, xs, True, True)
                    else:
                        for h in range(4):
                            last = mm(bank(4)[:, h * P:(h + 1) * P], x[:, h * S:h * S + P],
                                      x[:, h * S + P:(h + 1) * S], True, True)
                    last.then_inc(sem("level_scores_ready"), 1)
                pe.wait_ge(sem("hgrn_scores_merged"), nth(pe, "hgrn_scores_merged"))
                pe.wait_ge(sem("level_merged"), nth(pe, "level_merged"))
                sc = arena[:, 7168:8192]
                cross = arena[:, 8192:8704]
                for h in range(4):
                    o = bank(5 + h // 2)[:, (h % 2) * S:(h % 2 + 1) * S]
                    v = lambda tb: proj[:, (HI + h // 2) * 512 + tb * S + (h % 2) * P:][:, 0:P]
                    mm(o[:, 0:P], v(0), sc[:, 2 * h * P:(2 * h + 1) * P], True, True)
                    mm(o[:, P:S], v(1), sc[:, (2 * h + 1) * P:(2 * h + 2) * P], True, False)
                    last = mm(o[:, P:S], v(0), cross[:, h * P:(h + 1) * P], False, True)
                last.then_inc(sem("hgrn_o_ready"), 1)
                pe.wait_ge(sem("hgrn_o_squared"), nth(pe, "hgrn_o_squared"))
                for j in range(2):
                    last = mm(bank(7 if j else 4), K(K_128), arena[:, 3072 + j * 512:3072 + (j + 1) * 512], True, True)
                last.then_inc(sem("hgrn_mean_square_ready"), 1)

            def stick():
                pe.wait_ge(sem("hgrn_done"), nth(pe, "hgrn_done"))
                for g in range(2):
                    L = arena[:, g * 3072:g * 3072 + 1536]
                    W = arena[:, g * 3072 + 1536:(g + 1) * 3072]
                    if g:
                        pe.wait_ge(sem("stick_exponent_ready"), nth(pe, "stick_exponent_ready", 1))
                        seen[(pe.engine, "stick_exponent_ready")] += 1
                    for i in range(4):
                        h = 4 * g + i
                        r = slice((h % 2) * 64, (h % 2) * 64 + 64)
                        kh = proj[r, (SK + h // 2) * S:(SK + h // 2 + 1) * S]
                        qh = proj[r, (SQ + h // 2) * S:(SQ + h // 2 + 1) * S]
                        mm(bank(i)[:, 0:S], kh[:, 0:P], qh, True, False, True)
                        last = mm(bank(i)[:, S:S + P], kh[:, P:S], qh[:, P:S], False, False, True)
                    last.then_inc(sem("stick_z_ready"), 1)
                    pe.wait_ge(sem("stick_softplus_ready"), nth(pe, "stick_softplus_ready"))
                    for i in range(4):
                        l = L[:, i * 384:(i + 1) * 384]
                        mm(bank(i)[:, 0:S], K(K_TRI), l[:, 0:S], False, False, True)
                        mm(bank(i)[:, P:S], K(K_NEG), l[:, S:384], False, False, True)
                        last = mm(bank(i)[:, S:384], K(K_TRI), l[:, S:384], False, True, True)
                    last.then_inc(sem("stick_sums_ready"), 1)
                    pe.wait_ge(sem("stick_weights_ready"), nth(pe, "stick_weights_ready"))
                    for i in range(4):
                        h = 4 * g + i
                        o = bank(4 + g)[(h % 2) * 64:(h % 2) * 64 + 64, (i // 2) * S:(i // 2 + 1) * S]
                        v = lambda tb: proj[:, (SV + h // 4) * 512 + tb * S + (h % 4) * 64:][:, 0:64]
                        w = W[:, i * 384:(i + 1) * 384]
                        mm(o, v(0), w[:, 0:S], True, False)
                        last = mm(o[:, P:S], v(1), w[:, S:384], False, True)
                    last.then_inc(sem("stick_o_ready"), 1)

            def mix_out():
                pe.wait_ge(sem("o_a_ready"), nth(pe, "o_a_ready"))
                pe.wait_ge(sem("o_b_ready"), nth(pe, "o_b_ready", 2))
                for j in range(2):
                    for br in range(2):
                        q = take()
                        for m in range(4):
                            o = bank(4 * j + 2 * br + m // 2)[:, (m % 2) * S:(m % 2 + 1) * S]
                            for k in range(4):
                                last = mm(o, slot(q, k * 512 + m * P, k * 512 + (m + 1) * P),
                                          y3[:, 4 * br + k, 0:S], k == 0, k == 3)
                        last.then_inc(DONE, 1)
                pe.wait_ge(sem("mixed_ready"), nth(pe, "mixed_ready", 2))
                for j in range(OUTP):
                    panel_T(take(), j, S, lambda k: h3[:, k, 0:S]).then_inc(DONE, 1)

            def ffn(p0, e=0):
                hb = [arena[:, 1024:1536], arena[:, 1536:2048]]

                def up(p, f, r):
                    for j in range(2):
                        landed(p + j, r)
                        panel_T(p + j, 2 * j + f % 2, S, lambda k: h3[:, k, 0:S]).then_inc(DONE, 1)

                def down(p, f, r, count):
                    landed(p, r)
                    pe.wait_ge(sem("hidden_ready"), count)
                    for k in range(2):
                        for m in range(KD):
                            last = mm(bank(4 + m // 2)[:, (m % 2) * S:(m % 2 + 1) * S],
                                      slot(p, k * D + m * P, k * D + (m + 1) * P),
                                      hb[f % 2][:, k * S:(k + 1) * S], False, True, True)
                    last.then_inc(DONE, 1)

                h0 = hid[0]
                er = e * (FFN // RING)
                up(p0, 0, er)
                pe.wait_ge(sem("accumulators_free"), e + accs[0])
                for b in range(4):
                    mm(bank(4 + b), zrow[:, 0:P], zrow[:, P:640], True, False, True)
                with pe.Fori(0, FSTEP // 2 - 1) as i:
                    up(p0 + 2, 1, er + i)
                    down(p0 + 4, 0, er + i, e * FSTEP + i * 2 + (h0 + 1))
                    up(p0 + 5, 0, er + i)
                    down(p0 + 7, 1, er + i, e * FSTEP + i * 2 + (h0 + 2))
                up(p0 + 38, 1, er)
                down(p0 + 40, 0, er, e * FSTEP + (h0 + FSTEP - 1))
                down(p0 + 41, 1, er, e * FSTEP + (h0 + FSTEP))

            def router():
                pe.wait_ge(sem("h_ready"), nth(pe, "h_ready", KD))
                for tb in range(2):
                    for k in range(KD):
                        last = mm(bank(1)[:, tb * 8:tb * 8 + 8], h3[:, k, tb * P:(tb + 1) * P],
                                  sml[:, S_ROUT + k * 8:S_ROUT + k * 8 + 8], k == 0, k == KD - 1)
                last.then_inc(sem("logits_ready"), 1)
                pe.wait_ge(sem("combine_diagonals_ready"), nth(pe, "combine_diagonals_ready"))
                for b in range(4):
                    last = mm(bank(4 + b), K(K_ONE), arena[:, 4096 + b * 512:4096 + (b + 1) * 512], True, True)
                last.then_inc(sem("combine_ready"), 1)

            hid, accs = [0], [1]
            pe.wait_ge(sem("inputs_landed"), 64)
            for layer in range(2):
                norm()
                project1()
                hgrn()
                stick()
                mix_out()
                norm()
                if layer == 0:
                    pe.wait_ge(sem("h_ready"), nth(pe, "h_ready", KD))
                    ffn(at[0])
                    at[0] += FFN
                    hid[0] += FSTEP
                    accs[0] += 2
                else:
                    router()
                    with pe.Fori(0, E) as e:
                        ffn(at[0], e)
                    at[0] += E * FFN
            norm()

            def hyena_filters():
                h1 = proj[0:64, 2304:2560]
                h2 = proj[0:64, 2560:2816]
                pe.wait_ge(sem("filter_tables_landed"), nth(pe, "filter_tables_landed", 16 * 7))
                mm(bank(1)[0:64, 0:S], proj[0:33, 2816:2880], proj[0:33, 2048:2304], True, True) \
                    .then_inc(sem("filter_hidden_sum"), 1)
                pe.wait_ge(sem("filter_hidden_ready"), nth(pe, "filter_hidden_ready"))
                mm(bank(1)[0:64, 0:S], proj[0:64, 2880:2944], h1, True, True).then_inc(sem("filter_hidden_sum"), 1)
                pe.wait_ge(sem("filter_hidden_ready"), nth(pe, "filter_hidden_ready"))
                for o in range(2):
                    if o:
                        pe.wait_ge(sem("filter_spectrum_ready"), nth(pe, "filter_spectrum_ready"))
                    for tb in range(2):
                        for d in range(2):
                            last = mm(bank(tb * 2 + d), h2[:, tb * P:(tb + 1) * P],
                                      proj[0:64, (o * 2 + d) * 512:(o * 2 + d + 1) * 512], True, True)
                    last.then_inc(sem("filter_taps_sum"), 1)
                    pe.wait_ge(sem("taps_squared"), nth(pe, "taps_squared"))
                    for j in range(4):
                        last = mm(bank(4), K(K_ONE), proj[:, 9216 + j * 512:9216 + (j + 1) * 512], j == 0, j == 3)
                    last.then_inc(sem("taps_energy_ready"), 1)
                    pe.wait_ge(sem("taps_combined"), nth(pe, "taps_combined"))
                    pe.wait_ge(sem("taps_rnorm_ready"), nth(pe, "taps_rnorm_ready"))
                    for m in range(2):
                        for cs in range(2):
                            for tb in range(2):
                                last = mm(bank(4 + 2 * m + cs),
                                          arena[:, 4096 + cs * 512 + tb * S + m * P:][:, 0:P],
                                          proj[:, 6144 + cs * 1024 + tb * 512:][:, 0:512], tb == 0, tb == 1)
                    last.then_inc(sem("spectrum_sum"), 1)
                pe.wait_ge(sem("filter_spectrum_ready"), nth(pe, "filter_spectrum_ready"))

            def adaln():
                if at[0] == BLOCK1:
                    pe.wait_ge(sem("cond_ready"), nth(pe, "cond_ready"))
                else:
                    pe.wait_ge(sem("ada_done"), nth(pe, "ada_done"))
                for p in range(ADA):
                    q = take()
                    for m in range(2):
                        for k in range(KD):
                            last = mm(bank(7)[:, (2 * p + m) * 2:(2 * p + m) * 2 + 2],
                                      slot(q, k * 256 + m * P, k * 256 + (m + 1) * P),
                                      cond[:, 2 * k:2 * k + 2], k == 0, k == KD - 1)
                    last.then_inc(DONE, 1)

            def project2(layer):
                pe.wait_ge(sem("h_mod_ready"), nth(pe, "h_mod_ready", 2 * KD))
                for p in range(IN2):
                    q = take()
                    b = 2 * (p % 4)
                    if p >= 4:
                        pe.wait_ge(sem("pair_copied"), nth(pe, "pair_copied"))
                    wide = layer == 0 or p in (2, 5, 6)
                    n = 512 if wide else S
                    if layer == 1 and p in (7, 8):
                        for tb in range(4):
                            for k in range(KD):
                                last = mm(bank(b, 2)[:, tb * S:(tb + 1) * S], h3[:, k, tb * P:(tb + 1) * P],
                                          slot(q, k * 256, (k + 1) * 256), k == 0, k == KD - 1)
                    elif p == 2:
                        for k in range(KD):
                            mm(bank(b), slot(q, k * 256, k * 256 + P), h3[:, k, :], k == 0, k == KD - 1)
                        for tb in range(4):
                            for k in range(KD):
                                last = mm(bank(b + 1)[:, tb * P:(tb + 1) * P], h3[:, k, tb * P:(tb + 1) * P],
                                          slot(q, k * 256 + P, (k + 1) * 256), k == 0, k == KD - 1)
                    else:
                        for m in range(2):
                            for k in range(KD):
                                last = mm(bank(b + m)[:, 0:n], slot(q, k * 256 + m * P, k * 256 + (m + 1) * P),
                                          h3[:, k, 0:n], k == 0, k == KD - 1)
                    last.then_inc(DONE, 1)
                pe.wait_ge(sem("pair_copied"), nth(pe, "pair_copied", 4))

            def qk_norm(layer):
                for i, (c, n, g, rope) in enumerate(qk_chunks(layer)):
                    pe.wait_ge(sem("qk_squared"), nth(pe, "qk_squared"))
                    mm(bank(i % 2)[:, 0:n], K(K_BD), arena[:, 6144 + (i % 2) * 512:][:, 0:n], True, True) \
                        .then_inc(sem("qk_mean_square"), 1)
                    pe.wait_ge(sem("qk_normed"), nth(pe, "qk_normed"))
                    if rope:
                        mm(bank(2 + i % 2)[:, 0:S], K(K_SWAP), proj[:, c * 512:c * 512 + S], True, True) \
                            .then_inc(sem("qk_swapped"), 1)
                pe.wait_ge(sem("qk_done"), nth(pe, "qk_done"))

            def hyena():
                nat = proj[:, (C_HU + 4) * 512:(C_HU + 12) * 512]
                for j in range(8):
                    part, tb = j // 4, j % 4
                    if j == 0:
                        pe.wait_ge(sem("short_conv_done"), nth(pe, "short_conv_done"))
                    if j >= 2:
                        pe.wait_ge(sem("natural_copied"), nth(pe, "natural_copied"))
                    for c in range(4):
                        last = nc.tensor.transpose(bank(j % 2)[:, c * P:(c + 1) * P],
                                                   h3[:, part * 4 + c, tb * P:(tb + 1) * P], K(K_ID))
                    last.then_inc(sem("natural_ready"), 1)
                pe.wait_ge(sem("natural_copied"), nth(pe, "natural_copied", 2))
                for o in range(2):
                    for s in range(2):
                        z = nat[:, s * 1024:(s + 1) * 1024]
                        if o == 1 and s == 0:
                            pe.wait_ge(sem("hyena_z_ready"), nth(pe, "hyena_z_ready"))
                        for m in range(2):
                            for cs in range(2):
                                for tb in range(2):
                                    last = mm(bank(2 * m + cs), arena[:, 4096 + cs * 512 + tb * S + m * P:][:, 0:P],
                                              z[:, tb * 512:(tb + 1) * 512], tb == 0, tb == 1)
                        last.then_inc(sem("z_spectrum_ready"), 1)
                        pe.wait_ge(sem("y_spectrum_ready"), nth(pe, "y_spectrum_ready"))
                        Y = hT[:, s * 2048:(s + 1) * 2048]
                        if o == 0:
                            if s:
                                pe.wait_ge(sem("hyena_z_ready"), nth(pe, "hyena_z_ready"))
                            for tb in range(2):
                                for j in range(4):
                                    kc, cs = j // 2, j % 2
                                    last = mm(bank(4 + tb), arena[:, 5120 + cs * 512 + kc * S + tb * P:][:, 0:P],
                                              Y[:, j * 512:(j + 1) * 512], j == 0, j == 3)
                        else:
                            if s:
                                pe.wait_ge(sem("hyena_y_done"), nth(pe, "hyena_y_done"))
                            for c in range(4):
                                for j in range(4):
                                    kc, cs = j // 2, j % 2
                                    last = mm(bank(4 + c // 2)[:, (c % 2) * S:(c % 2 + 1) * S],
                                              Y[:, j * 512 + c * P:j * 512 + (c + 1) * P],
                                              arena[:, 5120 + cs * 512 + kc * S:][:, 0:S], j == 0, j == 3)
                        last.then_inc(sem("hyena_inverse_ready"), 1)
                pe.wait_ge(sem("hyena_y_done"), nth(pe, "hyena_y_done"))

            def attend(layer):
                us = attention_units(layer)
                n = len(us)
                first_pv = pv_count[0]
                for i in range(n + 2):
                    if i < n:
                        u = us[i]
                        if u["kind"] == "plain":
                            last = mm(bank(i % 2)[:, 0:u["keys"]], u["q"], u["k"], True, True)
                        else:
                            mm(bank(i % 2)[:, 0:S], u["q"], u["k"][:, 0:S], True, True)
                            last = mm(bank(6 + i % 2)[:, 0:S], u["q"], u["k"][:, S:512], True, True)
                        last.then_inc(sem("scores_ready"), 1)
                    if 1 <= i <= n:
                        u = us[i - 1]
                        pe.wait_ge(sem("probs_ready"), nth(pe, "probs_ready"))
                        for c in range(u["keys"] // P):
                            last = nc.tensor.transpose(bank(2 + (i - 1) % 2)[:, c * P:(c + 1) * P],
                                                       arena[:, 8192 + ((i - 1) % 2) * 520 + c * P:][:, 0:P], K(K_ID))
                        last.then_inc(sem("probs_turned"), 1)
                    if i >= 2:
                        u = us[i - 2]
                        pe.wait_ge(sem("probsT_ready"), nth(pe, "probsT_ready"))
                        if i >= 4:
                            pe.wait_ge(sem("o_gated"), nth(pe, "o_gated"))
                        o = bank(4 + i % 2)[u["half"] * 64:u["half"] * 64 + 64, 0:P]
                        nch = u["keys"] // P
                        for c in range(nch):
                            last = mm(o, u["v"](c), arena[:, 7168 + (i % 2) * 512 + c * P:][:, 0:P],
                                      c == 0, c == nch - 1)
                        last.then_inc(sem("o_ready"), 1)
                pe.wait_ge(sem("o_gated"), nth(pe, "o_gated", 2))

            def out2(layer):
                n = 512 if layer == 0 else S
                pe.wait_ge(sem("y2_ready"), nth(pe, "y2_ready"))
                for j in range(OUTP):
                    q = take()
                    for m in range(2):
                        for k in range(KD):
                            last = mm(bank(2 * j + m)[:, 0:n], slot(q, k * 256 + m * P, k * 256 + (m + 1) * P),
                                      y3[:, k, 0:n], k == 0, k == KD - 1)
                    last.then_inc(DONE, 1)

            pv_count = [0]
            hyena_filters()
            for layer in range(2):
                adaln()
                norm(2)
                project2(layer)
                qk_norm(layer)
                if layer == 0:
                    hyena()
                attend(layer)
                out2(layer)

        @block.scalar
        def _(act):
            chain = [0]

            def step(ins):
                chain[0] += 1
                ins.then_inc(sem("scalar_steps"), 1)
                act.wait_ge(sem("scalar_steps"), chain[0])

            def f(o, i, fn, **kw):
                return nc.scalar.activation(o, i, fn, **kw)

            panel = [0]

            def multiplied(k):
                panel[0] += k
                act.wait_ge(DONE, panel[0])

            act.dma_start(xT[:, :], x_in).then_inc(sem("inputs_landed"), 16)
            act.dma_start(cst[:, :], consts_in).then_inc(sem("inputs_landed"), 16)
            act.dma_start(sml[:, :], small_in).then_inc(sem("inputs_landed"), 16)
            act.dma_start(cT[:, :], ctx_in).then_inc(sem("inputs_landed"), 16)

            def norm(first=False, streams=1):
                if first:
                    act.wait_ge(sem("inputs_landed"), 64)
                else:
                    act.wait_ge(sem("x_done"), nth(act, "x_done"))
                if streams == 2:
                    step(f(h3[:, :, 0:S], x3, ACT.Square))
                    f(h3[:, :, S:512], c3, ACT.Square).then_inc(sem("squares_ready"), 1)
                else:
                    f(h3[:, :, 0:S], x3, ACT.Square).then_inc(sem("squares_ready"), 1)
                act.wait_ge(sem("mean_square_ready"), nth(act, "mean_square_ready"))
                n = streams * S
                f(rstd[:, 0:n], bank(0)[:, 0:n], ACT.Sqrt, bias=eps1).then_inc(sem("root_ready"), 1)

            def project1():
                for p in range(0, IN1, 2):
                    multiplied(1)
                    o = proj[:, p * 512:(p + 1) * 512]
                    f(o, bank(p % 8), ACT.Copy, scale=0.125 if p * 2 in (SQ, SQ + 2) else 1.0) \
                        .then_inc(sem("proj_even_copied"), 1)
                    panel[0] += 1

            def hgrn(layer):
                q, kk = arena[:, 0:1024], arena[:, 1024:2048]
                e0 = arena[:, 3072:4096]
                E = [e0, arena[:, 4096:5120]]
                act.wait_ge(sem("proj_even_copied"), 11 * (layer + 1))
                act.wait_ge(sem("proj_odd_copied"), 11 * (layer + 1))
                step(f(q, proj[:, HQ * S:(HQ + 4) * S], ACT.Silu))
                f(proj[:, HOG * S:(HOG + 4) * S], proj[:, HOG * S:(HOG + 4) * S], ACT.Silu) \
                    .then_inc(sem("q_silu_ready"), 1)
                f(proj[:, GA * S:(GA + 16) * S], proj[:, GA * S:(GA + 16) * S], ACT.Sigmoid) \
                    .then_inc(sem("gates_ready"), 1)
                act.wait_ge(sem("forget_abs_ready"), nth(act, "forget_abs_ready"))
                step(f(e0, e0, ACT.Exp))
                if layer == 1:
                    step(f(lbs[:, 4:8], lbs[:, 4:8], ACT.Exp))
                    step(f(lbs[:, 4:8], lbs[:, 4:8], ACT.Ln, bias=ones1))
                f(e0, e0, ACT.Ln, bias=ones1).then_inc(sem("forget_log_ready"), 1)
                act.wait_ge(sem("key_exponent_ready"), nth(act, "key_exponent_ready"))
                f(kk, e0, ACT.Exp).then_inc(sem("hgrn_key_ready"), 1)
                if layer == 1:
                    act.wait_ge(sem("forget_abs_ready"), nth(act, "forget_abs_ready"))
                    step(f(e0, e0, ACT.Exp))
                    f(e0, e0, ACT.Ln, bias=ones1).then_inc(sem("forget_log_ready"), 1)
                for lv in range(8):
                    act.wait_ge(sem("level_exponent_ready"), nth(act, "level_exponent_ready"))
                    v = E[lv % 2].rearrange("p (n two b) -> p n two b", two=2, b=1 << lv)
                    f(v[:, :, 1, :], v[:, :, 1, :], ACT.Exp)
                    f(v[:, :, 0, :], v[:, :, 0, :], ACT.Exp, scale=-1.0).then_inc(sem("level_decay_ready"), 1)
                act.wait_ge(sem("level_scores_ready"), nth(act, "level_scores_ready", 9))
                f(arena[:, 8192:8704], bank(4), ACT.Copy).then_inc(sem("cross_copied"), 1)
                act.wait_ge(sem("hgrn_o_ready"), nth(act, "hgrn_o_ready"))
                f(e0, bank(5, 2), ACT.Square).then_inc(sem("hgrn_o_squared"), 1)
                act.wait_ge(sem("hgrn_mean_square_ready"), nth(act, "hgrn_mean_square_ready"))
                f(E[1][:, 0:512], bank(4), ACT.Sqrt, bias=eps1)
                f(E[1][:, 512:1024], bank(7), ACT.Sqrt, bias=eps1).then_inc(sem("hgrn_root_ready"), 1)

            def stick():
                for g in range(2):
                    L = arena[:, g * 3072:g * 3072 + 1536]
                    W = arena[:, g * 3072 + 1536:(g + 1) * 3072]
                    act.wait_ge(sem("stick_z_ready"), nth(act, "stick_z_ready"))
                    step(f(L.rearrange("p (h t) -> p h t", h=4), ps[:, 0:4, 0:384], ACT.Abs))
                    step(f(L, L, ACT.Exp, scale=-1.0))
                    f(L, L, ACT.Ln, bias=ones1).then_inc(sem("stick_log_ready"), 1)
                    act.wait_ge(sem("stick_exponent_ready"), nth(act, "stick_exponent_ready"))
                    f(W, W, ACT.Exp).then_inc(sem("stick_exp_ready"), 1)
                    act.wait_ge(sem("stick_o_ready"), nth(act, "stick_o_ready"))
                    for c in range(2):
                        ins = f(y3[:, 4 + 2 * g + c, 0:S], bank(4 + g)[:, c * S:(c + 1) * S], ACT.Copy)
                        if c == 0:
                            step(ins)
                    ins.then_inc(sem("o_b_ready"), 1)

            def ffn(p0, e=0):
                sg = [arena[:, 0:512], arena[:, 512:1024]]

                def silu(p, f_, more):
                    act.wait_ge(DONE, more + (p + 1))
                    f(sg[f_ % 2], bank(f_ % 2), ACT.Silu).then_inc(sem("gate_silu_ready"), 1)

                silu(p0, 0, e * FFN)
                with act.Fori(0, FSTEP // 2 - 1) as i:
                    silu(p0 + 2, 1, e * FFN + i * 6)
                    silu(p0 + 5, 0, e * FFN + i * 6)
                silu(p0 + 38, 1, e * FFN)

            for layer in range(2):
                norm(first=layer == 0)
                project1()
                hgrn(layer)
                stick()
                panel[0] += 2 * OUTP
                norm()
                if layer == 0:
                    ffn(panel[0])
                    panel[0] += FFN
                else:
                    act.wait_ge(sem("router_max_ready"), nth(act, "router_max_ready"))
                    for tb in range(2):
                        ins = f(rt[:, 16 + 8 * tb:24 + 8 * tb], rt[:, 8 * tb:8 * tb + 8], ACT.Exp,
                                bias=rt[:, 34 + tb:35 + tb])
                        if tb == 0:
                            step(ins)
                    ins.then_inc(sem("router_exp_ready"), 1)
                    act.dma_start(proj[0:64, 0:2048], w3_in).then_inc(sem("filter_tables_landed"), 16)
                    act.dma_start(proj[0:33, 2048:2304], pos_in).then_inc(sem("filter_tables_landed"), 16)
                    act.dma_start(proj[0:33, 2816:2880], w1_in).then_inc(sem("filter_tables_landed"), 16)
                    act.dma_start(proj[0:64, 2880:2944], w2_in).then_inc(sem("filter_tables_landed"), 16)
                    act.dma_start(proj[:, 8192:9216], decay_in).then_inc(sem("filter_tables_landed"), 16)
                    act.dma_start(proj[:, 11776:12800], skip_in.partition_broadcast(P)) \
                       .then_inc(sem("filter_tables_landed"), 16)
                    with act.Fori(0, E) as e:
                        ffn(panel[0], e)
                    panel[0] += E * FFN
            norm()

            act.wait_ge(sem("combine_free"), nth(act, "combine_free"))
            act.dma_start(arena[:, 4096:6144], dft_in).then_inc(sem("filter_tables_landed"), 16)
            f(cond[:, :], sml[:, S_COND:S_COND + 16], ACT.Silu).then_inc(sem("cond_ready"), 1)

            def hyena_filters():
                for _ in range(2):
                    act.wait_ge(sem("filter_phase_ready"), nth(act, "filter_phase_ready"))
                    src = proj[0:64, 2944:3200]
                    dst = proj[0:64, 2304:2560] if _ == 0 else proj[0:64, 2560:2816]
                    f(dst, src, ACT.Sin).then_inc(sem("filter_hidden_ready"), 1)
                for o in range(2):
                    act.wait_ge(sem("taps_ready"), nth(act, "taps_ready"))
                    f(proj[:, 9216:11264], proj[:, 4096:6144], ACT.Square).then_inc(sem("taps_squared"), 1)
                    act.wait_ge(sem("taps_energy_ready"), nth(act, "taps_energy_ready"))
                    f(proj[:, 11264:11776], bank(4), ACT.Sqrt, bias=eps1).then_inc(sem("taps_root_ready"), 1)

            def project2(layer):
                for p in range(IN2):
                    multiplied(1)
                    b = 2 * (p % 4)
                    wide = layer == 0 or p in (2, 5, 6, 7, 8)
                    o = proj[:, 2 * p * 512:(2 * p + 2) * 512]
                    i = bank(b, 2)
                    if not wide:
                        o = o.rearrange("q (a n) -> q a n", a=2)[:, :, 0:S]
                        i = i.rearrange("q (a n) -> q a n", a=2)[:, :, 0:S]
                    f(o, i, ACT.Copy).then_inc(sem("pair_copied"), 1)

            def qk_norm(layer):
                act.wait_ge(sem("pair_copied"), IN2 * (layer + 1))
                for i, (c, n, g, rope) in enumerate(qk_chunks(layer)):
                    f(arena[:, 6144 + (i % 2) * 512:][:, 0:n], proj[:, c * 512:c * 512 + n], ACT.Square) \
                        .then_inc(sem("qk_squared"), 1)
                    if i >= 2:
                        act.wait_ge(sem("qk_normed"), nth(act, "qk_normed"))
                    act.wait_ge(sem("qk_mean_square"), nth(act, "qk_mean_square"))
                    f(qk_root(i)[:, 0:n], bank(i % 2)[:, 0:n], ACT.Sqrt, bias=eps1).then_inc(sem("qk_root_ready"), 1)
                act.wait_ge(sem("qk_normed"), nth(act, "qk_normed", 2))
                gates = proj[:, C_G * 512:(C_G + 8) * 512]
                f(gates, gates, ACT.Silu).then_inc(sem("y_gates_ready"), 1)

            def hyena():
                nat = proj[:, (C_HU + 4) * 512:(C_HU + 12) * 512]
                for j in range(8):
                    act.wait_ge(sem("natural_ready"), nth(act, "natural_ready"))
                    f(nat[:, j * 512:(j + 1) * 512], bank(j % 2), ACT.Copy).then_inc(sem("natural_copied"), 1)

            def attend(layer):
                us = attention_units(layer)
                n = len(us)
                for i in range(n + 1):
                    if i < n:
                        u = us[i]
                        pr = arena[:, 8192 + (i % 2) * 520:][:, 0:520]
                        acc = stat[:, 8 + i % 4:9 + i % 4]
                        nm = stat[:, 4 + i % 4:5 + i % 4]
                        if u["kind"] != "plain":
                            act.wait_ge(sem("scores_ready"), nth(act, "scores_ready"))
                            if i >= 2:
                                act.wait_ge(sem("probs_scaled_exp"), seen[(act.engine, "exp_own")] - 1)
                            scs = scores_sb(i)
                            f(scs[:, S:512], bank(6 + i % 2)[:, 0:S], ACT.Copy, scale=0.125) \
                                .then_inc(sem("context_scores_ready"), 1)
                            act.wait_ge(sem("max_ready"), nth(act, "max_ready"))
                            w = 513 if u["kind"] == "window" else 512
                            f(pr[:, 0:w], scs[:, 0:w], ACT.Exp, bias=nm, accum_out=acc) \
                                .then_inc(sem("probs_scaled_exp"), 1)
                        else:
                            nth(act, "scores_ready")
                            act.wait_ge(sem("max_ready"), nth(act, "max_ready"))
                            f(pr[:, 0:u["keys"]], bank(i % 2)[:, 0:u["keys"]], ACT.Exp, bias=nm, scale=0.125,
                              accum_out=acc).then_inc(sem("probs_scaled_exp"), 1)
                        seen[(act.engine, "exp_own")] = seen.get((act.engine, "exp_own"), 0) + 1
                    if i >= 1:
                        j = i - 1
                        act.wait_ge(sem("probs_turned"), nth(act, "probs_turned"))
                        if j >= 2:
                            act.wait_ge(sem("o_ready"), nth(act, "o_ready"))
                        kk = us[j]["keys"]
                        f(arena[:, 7168 + (j % 2) * 512:][:, 0:kk], bank(2 + j % 2)[:, 0:kk], ACT.Copy) \
                            .then_inc(sem("probsT_ready"), 1)
                act.wait_ge(sem("o_ready"), nth(act, "o_ready", 2))

            hyena_filters()
            for layer in range(2):
                panel[0] += ADA
                if layer == 1:
                    act.wait_ge(sem("y2_ready"), nth(act, "y2_ready"))
                    for h in range(8):
                        for r in range(4):
                            src = bass.AP(rpb_in.tensor, h * 465 + (7 - r) * 31 + 15 - 63, [[1, 64], [31, 4], [1, 64]])
                            dst = arena[(r % 2) * 64:(r % 2) * 64 + 64, (h * 2 + r // 2) * S:(h * 2 + r // 2 + 1) * S]
                            act.dma_start(dst.rearrange("p (a b) -> p a b", a=4), src) \
                               .then_inc(sem("position_bias_landed"), 16)
                norm(streams=2)
                project2(layer)
                qk_norm(layer)
                if layer == 0:
                    hyena()
                attend(layer)
                panel[0] += OUTP
            act.wait_ge(sem("x_done"), nth(act, "x_done", 1))
            act.dma_start(out, xT[:, :]).then_inc(sem("out_stored"), 16)
            act.wait_ge(sem("out_stored"), 16)

        @block.gpsimd
        def _(pool):
            pool.memset(zrow[:, :], 0.0).then_inc(sem("accumulators_free"), 1)
            for layer in range(2):
                k = arena[:, 1024:2048]
                for lv in range(8):
                    pool.wait_ge(sem("level_decay_ready"), nth(pool, "level_decay_ready"))
                    if lv == 0:
                        pool.wait_ge(sem("hgrn_key_ready"), nth(pool, "hgrn_key_ready"))
                    if lv >= 2:
                        pool.wait_ge(sem("level_scores_ready"), nth(pool, "level_scores_ready", 2 if lv == 2 else 1))
                    E = arena[:, 3072 + (lv % 2) * 1024:][:, 0:1024]
                    X = arena[:, 5120 + (lv % 2) * 1024:][:, 0:1024]
                    v = lambda a: a.rearrange("p (n two b) -> p n two b", two=2, b=1 << lv)[:, :, 0, :]
                    pool.tensor_tensor(v(X), v(k), v(E), ALU.mult).then_inc(sem("level_k_ready"), 1)
                seen[(pool.engine, "level_scores_ready")] += 2
            for o in range(2):
                pool.wait_ge(sem("taps_ready"), nth(pool, "taps_ready"))
                if o:
                    pool.wait_ge(sem("spectrum_sum"), nth(pool, "spectrum_sum"))
                a = proj[:, 4096:6144].rearrange("p (tb d n) -> p tb d n", tb=2, d=2)
                hp = proj[:, 6144:7168].rearrange("p (tb n) -> p tb n", tb=2)
                hm = proj[:, 7168:8192].rearrange("p (tb n) -> p tb n", tb=2)
                pool.tensor_tensor(hp, a[:, :, 0, :], a[:, :, 1, :], ALU.add)
                pool.tensor_tensor(hm, a[:, :, 0, :], a[:, :, 1, :], ALU.subtract).then_inc(sem("taps_combined"), 1)

        @block.vector
        def _(dve):
            chain = [0]

            def step(ins):
                chain[0] += 1
                ins.then_inc(sem("vector_steps"), 1)
                dve.wait_ge(sem("vector_steps"), chain[0])

            V = nc.vector
            panel = [0]

            def multiplied(k):
                panel[0] += k
                dve.wait_ge(DONE, panel[0])

            def signal(ins, name):
                ins.then_inc(sem(name), 1)
                made[name] = made.get(name, 0) + 1
                dve.wait_ge(sem(name), made[name])

            made = {}

            def announce(name):
                dve.sem_inc(sem(name), 1)
                made[name] = made.get(name, 0) + 1

            def norm(col, out3=None, name="h_ready"):
                dve.wait_ge(sem("root_ready"), nth(dve, "root_ready"))
                step(V.reciprocal(rstd[:, 0:S], rstd[:, 0:S]))
                for k in range(KD):
                    o = h3[:, k, 0:S] if out3 is None else out3[:, k, :]
                    ins = V.scalar_tensor_tensor(o, x3[:, k, :], sml[:, col + k:col + k + 1], rstd[:, 0:S],
                                                 ALU.mult, ALU.mult)
                    if out3 is None:
                        signal(ins, name)
                    elif k < KD - 1:
                        step(ins)
                    else:
                        signal(ins, name)

            def project1():
                for p in range(1, IN1, 2):
                    multiplied(2)
                    o = proj[:, p * 512:(p + 1) * 512]
                    V.tensor_scalar(o, bank(p % 8), 0.125 if p * 2 in (SQ, SQ + 2) else 1.0, None, ALU.mult) \
                        .then_inc(sem("proj_odd_copied"), 1)

            def hgrn(layer):
                q, kk, b = arena[:, 0:1024], arena[:, 1024:2048], arena[:, 2048:3072]
                e0, lf = arena[:, 3072:4096], arena[:, 4096:5120]
                E = [e0, lf]
                sc, cross = arena[:, 7168:8192], arena[:, 8192:8704]
                z = proj[:, HF * S:(HF + 4) * S]
                heads = lambda a: a.rearrange("p (h t) -> p h t", h=4)
                dve.wait_ge(sem("proj_even_copied"), 11 * (layer + 1))
                dve.wait_ge(sem("proj_odd_copied"), 11 * (layer + 1))
                if layer == 1:
                    step(V.tensor_tensor(lbs[:, 0:4], sml[:, S_LB + 4:S_LB + 8], sml[:, S_LB:S_LB + 4], ALU.subtract))
                    step(V.scalar_tensor_tensor(lbs[:, 4:8], lbs[:, 0:4], -1.0, lbs[:, 0:4], ALU.mult, ALU.min))
                signal(V.scalar_tensor_tensor(e0, z, -1.0, z, ALU.mult, ALU.min), "forget_abs_ready")
                step(V.memset(sc, 0.0))
                dve.wait_ge(sem("forget_log_ready"), nth(dve, "forget_log_ready"))
                step(V.scalar_tensor_tensor(lf, z, 0.0, e0, ALU.min, ALU.subtract))
                if layer == 0:
                    signal(V.tensor_tensor(e0, lf, z, ALU.subtract), "key_exponent_ready")
                else:
                    step(V.scalar_tensor_tensor(lbs[:, 8:12], lbs[:, 0:4], 0.0, lbs[:, 4:8], ALU.min, ALU.subtract))
                    step(V.tensor_tensor(lbs[:, 12:16], lbs[:, 8:12], lbs[:, 0:4], ALU.subtract))
                    rest = lbs[:, 12:16].unsqueeze(2).to_broadcast([P, 4, S])
                    step(V.tensor_tensor(e0, lf, z, ALU.subtract))
                    signal(V.tensor_tensor(heads(e0), heads(e0), rest, ALU.add), "key_exponent_ready")
                    less = lbs[:, 0:4].unsqueeze(2).to_broadcast([P, 4, S])
                    step(V.tensor_tensor(heads(lf), heads(lf), less, ALU.subtract))
                    dve.wait_ge(sem("hgrn_key_ready"), nth(dve, "hgrn_key_ready"))
                    signal(V.scalar_tensor_tensor(e0, lf, -1.0, lf, ALU.mult, ALU.min), "forget_abs_ready")
                    dve.wait_ge(sem("forget_log_ready"), nth(dve, "forget_log_ready"))
                    step(V.scalar_tensor_tensor(lf, lf, 0.0, e0, ALU.max, ALU.add))
                    log_lb = lbs[:, 8:12].unsqueeze(2).to_broadcast([P, 4, S])
                    step(V.tensor_tensor(heads(lf), heads(lf), log_lb, ALU.add))
                for h in range(4):
                    step(V.tensor_tensor_scan(b[:, h * S:(h + 1) * S], ones1.to_broadcast([P, S]),
                                              lf[:, h * S:(h + 1) * S], 0.0, ALU.mult, ALU.add))
                if layer == 0:
                    dve.wait_ge(sem("hgrn_key_ready"), nth(dve, "hgrn_key_ready"))
                dve.wait_ge(sem("q_silu_ready"), nth(dve, "q_silu_ready"))
                announce("hgrn_qk_ready")

                def merge(lv):
                    dve.wait_ge(sem("level_scores_ready"), nth(dve, "level_scores_ready"))
                    if lv == 7:
                        return
                    m = K(K_ID) if lv < 0 else K(K_LEV + lv * P)
                    m = m.bitcast(I32).unsqueeze(1).to_broadcast([P, 8, P])
                    i = bank(0 if lv % 2 else 2, 2).rearrange("p (h t) -> p h t", h=8)
                    signal(V.copy_predicated(sc.rearrange("p (h t) -> p h t", h=8), m, i), "level_merged")

                for lv in range(8):
                    B = 1 << lv
                    if lv >= 2:
                        dve.wait_ge(sem("level_k_ready"), nth(dve, "level_k_ready"))
                    v = lambda a: a.rearrange("p (n m) -> p n m", m=2 * B)
                    signal(V.tensor_tensor(v(E[lv % 2]), v(b), v(b)[:, :, B - 1:B].to_broadcast([P, 512 // B, 2 * B]),
                                           ALU.subtract), "level_exponent_ready")
                    if lv >= 1:
                        merge(lv - 2)
                    dve.wait_ge(sem("level_decay_ready"), nth(dve, "level_decay_ready"))
                    w = lambda a: a.rearrange("p (n two b) -> p n two b", two=2, b=B)[:, :, 1, :]
                    X = arena[:, 5120 + (lv % 2) * 1024:][:, 0:1024]
                    signal(V.tensor_tensor(w(X), w(q), w(E[lv % 2]), ALU.mult), "level_q_ready")
                seen[(dve.engine, "level_k_ready")] += 2
                merge(6)
                merge(7)
                dve.wait_ge(sem("cross_copied"), nth(dve, "cross_copied"))
                announce("hgrn_scores_merged")
                dve.wait_ge(sem("hgrn_root_ready"), nth(dve, "hgrn_root_ready"))
                step(V.reciprocal(lf, lf))
                for j in range(2):
                    t = arena[:, 2048 + j * 512:2048 + (j + 1) * 512]
                    step(V.scalar_tensor_tensor(t, bank(5 + j), sml[:, S_ON + layer:S_ON + layer + 1],
                                                lf[:, j * 512:(j + 1) * 512],
                                                ALU.mult, ALU.mult))
                    g = proj[:, HOG * S + j * 512:HOG * S + (j + 1) * 512]
                    ins = V.tensor_tensor(y3[:, 2 * j:2 * j + 2, 0:S], t.rearrange("p (a n) -> p a n", a=2),
                                          g.rearrange("p (a n) -> p a n", a=2), ALU.mult)
                    if j == 0:
                        step(ins)
                    else:
                        signal(ins, "o_a_ready")
                announce("hgrn_done")

            def stick():
                strict = K(K_STRICT).unsqueeze(1).to_broadcast([P, 4, P])
                for g in range(2):
                    L = arena[:, g * 3072:g * 3072 + 1536]
                    W = arena[:, g * 3072 + 1536:(g + 1) * 3072]
                    v = lambda a: a.rearrange("p (h t) -> p h t", h=4)
                    z = ps[:, 0:4, 0:384]
                    dve.wait_ge(sem("stick_log_ready"), nth(dve, "stick_log_ready"))
                    step(V.scalar_tensor_tensor(v(L), z, 0.0, v(L), ALU.max, ALU.add))
                    step(V.tensor_tensor(v(L)[:, :, 0:P], v(L)[:, :, 0:P], strict, ALU.mult))
                    signal(V.tensor_tensor(v(L)[:, :, S:384], v(L)[:, :, S:384], strict, ALU.mult),
                           "stick_softplus_ready")
                    dve.wait_ge(sem("stick_sums_ready"), nth(dve, "stick_sums_ready"))
                    signal(V.tensor_scalar(v(W), z, 0.0, None, ALU.min), "stick_exponent_ready")
                    dve.wait_ge(sem("stick_exp_ready"), nth(dve, "stick_exp_ready"))
                    step(V.tensor_tensor(v(W)[:, :, 0:P], v(W)[:, :, 0:P], strict, ALU.mult))
                    signal(V.tensor_tensor(v(W)[:, :, S:384], v(W)[:, :, S:384], strict, ALU.mult),
                           "stick_weights_ready")

            def mix_out():
                dve.wait_ge(sem("gates_ready"), nth(dve, "gates_ready"))
                for j in range(2):
                    multiplied(2)
                    ga = proj[:, GA * S + j * 1024:GA * S + (j + 1) * 1024]
                    gb = proj[:, GB * S + j * 1024:GB * S + (j + 1) * 1024]
                    step(V.tensor_tensor(ga, ga, bank(4 * j, 2), ALU.mult))
                    step(V.tensor_tensor(gb, gb, bank(4 * j + 2, 2), ALU.mult))
                    v = lambda a: a.rearrange("p (k n) -> p k n", k=4)
                    signal(V.tensor_tensor(h3[:, 4 * j:4 * j + 4, 0:S], v(ga), v(gb), ALU.add), "mixed_ready")
                for j in range(OUTP):
                    multiplied(1)
                    o = xT[:, j * 512:(j + 1) * 512]
                    ins = V.tensor_tensor(o, o, bank(j), ALU.add)
                    if j < OUTP - 1:
                        step(ins)
                    else:
                        signal(ins, "x_done")

            def ffn(p0, e=0):
                sg = [arena[:, 0:512], arena[:, 512:1024]]
                hb = [arena[:, 1024:1536], arena[:, 1536:2048]]

                def gated(p, f, more, count):
                    dve.wait_ge(DONE, more + (p + 2))
                    dve.wait_ge(sem("gate_silu_ready"), count)
                    V.tensor_tensor(hb[f % 2], sg[f % 2], bank(2 + f % 2), ALU.mult).then_inc(sem("hidden_ready"), 1)

                h0 = hid[0]
                gated(p0, 0, e * FFN, e * FSTEP + (h0 + 1))
                with dve.Fori(0, FSTEP // 2 - 1) as i:
                    gated(p0 + 2, 1, e * FFN + i * 6, e * FSTEP + i * 2 + (h0 + 2))
                    gated(p0 + 5, 0, e * FFN + i * 6, e * FSTEP + i * 2 + (h0 + 3))
                gated(p0 + 38, 1, e * FFN, e * FSTEP + (h0 + FSTEP))
                dve.wait_ge(DONE, e * FFN + (p0 + FFN))

            hid = [0]
            dve.wait_ge(sem("inputs_landed"), 64)
            for layer in range(2):
                norm(S_MIX + layer * KD)
                project1()
                hgrn(layer)
                stick()
                mix_out()
                norm(S_FFN + layer * KD)
                if layer == 0:
                    ffn(panel[0])
                    panel[0] += FFN
                    hid[0] += FSTEP
                    for j in range(4):
                        o = xT[:, j * 512:(j + 1) * 512]
                        ins = V.tensor_tensor(o, o, bank(4 + j), ALU.add)
                        if j < 3:
                            step(ins)
                        else:
                            signal(ins, "x_done")
                    made["accumulators_free"] = 1
                    announce("accumulators_free")

            L = rt[:, 0:16]
            dve.wait_ge(sem("logits_ready"), nth(dve, "logits_ready"))
            step(V.tensor_copy(L, bank(1)[:, 0:16]))
            L3 = L.rearrange("p (t e) -> p t e", t=2)
            step(V.tensor_reduce(rt[:, 32:34], L3, AX.X, ALU.max))
            signal(V.tensor_scalar(rt[:, 34:36], rt[:, 32:34], -1.0, None, ALU.mult), "router_max_ready")
            for tb in range(2):
                l = rt[:, 8 * tb:8 * tb + 8]
                other = l.unsqueeze(1).to_broadcast([P, 8, 8])
                own = l.unsqueeze(2).to_broadcast([P, 8, 8])
                more = rt[:, 64:128].rearrange("p (a b) -> p a b", a=8)
                tie = rt[:, 128:192].rearrange("p (a b) -> p a b", a=8)
                low = K(K_LOW, 64).rearrange("p (a b) -> p a b", a=8)
                step(V.tensor_tensor(more, other, own, ALU.is_gt))
                step(V.tensor_tensor(tie, other, own, ALU.is_equal))
                step(V.tensor_tensor(tie, tie, low, ALU.mult))
                step(V.tensor_tensor(more, more, tie, ALU.add))
                step(V.tensor_reduce(rt[:, 40 + 8 * tb:48 + 8 * tb], more, AX.X, ALU.add))
            step(V.tensor_scalar(rt[:, 40:56], rt[:, 40:56], 1.5, None, ALU.is_lt))
            dve.wait_ge(sem("router_exp_ready"), nth(dve, "router_exp_ready"))
            step(V.tensor_tensor(rt[:, 16:32], rt[:, 16:32], rt[:, 40:56], ALU.mult))
            step(V.tensor_reduce(rt[:, 36:38], rt[:, 16:32].rearrange("p (t e) -> p t e", t=2), AX.X, ALU.add))
            step(V.reciprocal(rt[:, 38:40], rt[:, 36:38]))
            step(V.tensor_tensor(rt[:, 200:216].rearrange("p (t e) -> p t e", t=2),
                                 rt[:, 16:32].rearrange("p (t e) -> p t e", t=2),
                                 rt[:, 38:40].unsqueeze(2).to_broadcast([P, 2, 8]), ALU.mult))
            dg = arena[:, 4096:6144].rearrange("p (e t n) -> p e t n", e=8, t=2)
            for tb in range(2):
                ins = V.tensor_tensor(dg[:, :, tb, :], K(K_ID).unsqueeze(1).to_broadcast([P, 8, P]),
                                      rt[:, 200 + 8 * tb:208 + 8 * tb].unsqueeze(2).to_broadcast([P, 8, P]), ALU.mult)
                if tb == 0:
                    step(ins)
            signal(ins, "combine_diagonals_ready")
            comb = arena[:, 2048:4096]
            dve.wait_ge(sem("combine_ready"), nth(dve, "combine_ready"))
            step(V.tensor_copy(comb, bank(4, 4)))
            announce("accumulators_free")
            tmp = arena[:, 6144:6656]
            with dve.Fori(0, E) as e:
                ffn(panel[0], e)
                w = arena[:, bass.ds(e * S + 2048, S)].unsqueeze(1).to_broadcast([P, 2, S])
                for j in range(4):
                    i = bank(4 + j).rearrange("p (a n) -> p a n", a=2)
                    V.tensor_tensor(arena[:, 6144 + j * 512:6144 + (j + 1) * 512].rearrange("p (a n) -> p a n", a=2),
                                    i, w, ALU.mult).then_inc(sem("expert_weighed"), 1)
                dve.wait_ge(sem("expert_weighed"), e * 4 + 4)
                announce("accumulators_free")
                V.tensor_tensor(xT[:, :], xT[:, :], arena[:, 6144:8192], ALU.add).then_inc(sem("expert_added"), 1)
                dve.wait_ge(sem("expert_added"), e + 1)
            panel[0] += E * FFN
            announce("combine_free")
            announce("x_done")
            norm(S_FIN, out3=x3, name="x_done")

            def hyena_filters():
                dve.wait_ge(sem("filter_tables_landed"), nth(dve, "filter_tables_landed", 16 * 7))
                arg = proj[0:64, 2944:3200]
                turn = proj[0:64, 3200:3456]
                for n in range(2):
                    dve.wait_ge(sem("filter_hidden_sum"), nth(dve, "filter_hidden_sum"))
                    step(V.tensor_scalar(arg, bank(1)[0:64, 0:S], sml[0:64, S_HYP + n:S_HYP + n + 1],
                                         sml[0:64, S_HYP + 2:S_HYP + 3], ALU.add, ALU.mult))
                    step(V.tensor_scalar(turn, arg, 1.0 / (2 * PI), None, ALU.mult))
                    step(V.tensor_scalar(turn, turn, 12582912.0, None, ALU.add))
                    step(V.tensor_scalar(turn, turn, 12582912.0, None, ALU.subtract))
                    for part in (6.28125, 0.0019350051879882812, 3.019916050561733e-07):
                        step(V.scalar_tensor_tensor(arg, turn, -part, arg, ALU.mult, ALU.add))
                    signal(V.tensor_scalar(arg, arg, 3.1415925, -3.1415925, ALU.min, ALU.max), "filter_phase_ready")
                for o in range(2):
                    dve.wait_ge(sem("filter_taps_sum"), nth(dve, "filter_taps_sum"))
                    for tb in range(2):
                        d = proj[:, 8192 + tb * 512:8192 + (tb + 1) * 512].unsqueeze(1).to_broadcast([P, 2, 512])
                        step(V.tensor_tensor(proj[:, 4096 + tb * 1024:4096 + (tb + 1) * 1024]
                                             .rearrange("p (d n) -> p d n", d=2), ps[:, 2 * tb:2 * tb + 2, :], d,
                                             ALU.mult))
                    signal(V.memset(proj[0:1, 4608:5120], 0.0), "taps_ready")
                    dve.wait_ge(sem("taps_root_ready"), nth(dve, "taps_root_ready"))
                    rn = proj[:, 11264:11776]
                    signal(V.reciprocal(rn, rn), "taps_rnorm_ready")
                    dve.wait_ge(sem("spectrum_sum"), nth(dve, "spectrum_sum"))
                    for m in range(2):
                        for cs in range(2):
                            t = arena[:, ((o * 2 + m) * 2 + cs) * 512:][:, 0:512]
                            step(V.tensor_tensor(t, bank(4 + 2 * m + cs), rn, ALU.mult))
                            if cs == 0:
                                step(V.tensor_tensor(t, t, proj[:, 11776 + o * 512:11776 + (o + 1) * 512], ALU.add))
                    announce("filter_spectrum_ready")

            def modulate(layer):
                multiplied(ADA)
                step(V.tensor_tensor(ada[:, :].rearrange("p (c s) -> p c s", s=2),
                                     bank(7)[:, 0:48].rearrange("p (c s) -> p c s", s=2),
                                     sml[:, S_ADA + 24 * layer:S_ADA + 24 * layer + 24].unsqueeze(2)
                                     .to_broadcast([P, 24, 2]), ALU.add))
                g = sml[:, S_NG + layer * KD:S_NG + (layer + 1) * KD].unsqueeze(2).to_broadcast([P, KD, 2])
                step(V.scalar_tensor_tensor(ada_a[:, :].rearrange("p (c s) -> p c s", s=2),
                                            ada[:, 16:32].rearrange("p (c s) -> p c s", s=2), 1.0, g,
                                            ALU.add, ALU.mult))
                dve.wait_ge(sem("root_ready"), nth(dve, "root_ready"))
                step(V.reciprocal(rstd[:, :], rstd[:, :]))
                for k in range(KD):
                    for s, src in enumerate((x3, c3)):
                        o = h3[:, k, s * S:(s + 1) * S]
                        step(V.scalar_tensor_tensor(o, src[:, k, :], ada_a[:, 2 * k + s:2 * k + s + 1],
                                                    rstd[:, s * S:(s + 1) * S], ALU.mult, ALU.mult))
                        signal(V.tensor_scalar(o, o, ada[:, 2 * k + s:2 * k + s + 1], None, ALU.add), "h_mod_ready")

            def qk_norm(layer):
                for i, (c, n, g, rope) in enumerate(qk_chunks(layer)):
                    dve.wait_ge(sem("qk_root_ready"), nth(dve, "qk_root_ready"))
                    r = qk_root(i)[:, 0:n]
                    q = proj[:, c * 512:c * 512 + n]
                    step(V.reciprocal(r, r))
                    signal(V.scalar_tensor_tensor(q, q, sml[:, S_QK + g:S_QK + g + 1], r, ALU.mult, ALU.mult),
                           "qk_normed")
                    if not rope:
                        continue
                    dve.wait_ge(sem("qk_swapped"), nth(dve, "qk_swapped"))
                    t = arena[:, 7168:7168 + S]
                    qx = proj[:, c * 512:c * 512 + S]
                    step(V.tensor_tensor(t, bank(2 + i % 2)[:, 0:S], K(K_SIN, S), ALU.mult))
                    step(V.tensor_tensor(qx, qx, K(K_COS, S), ALU.mult))
                    step(V.tensor_tensor(qx, qx, t, ALU.add))
                announce("qk_done")

            def hyena():
                dve.wait_ge(sem("y_gates_ready"), nth(dve, "y_gates_ready"))
                for j in range(12):
                    src = proj[:, (C_HU + j) * 512:(C_HU + j + 1) * 512].rearrange("p (s t) -> p s t", s=2)
                    dst = hT[:, j * 512:(j + 1) * 512] if j < 8 else proj[:, (C_HU + j - 8) * 512:(C_HU + j - 7) * 512]
                    dst = dst.rearrange("p (s t) -> p s t", s=2)
                    w = lambda n: sml[:, S_CW + 3 * j + n:S_CW + 3 * j + n + 1]
                    step(V.tensor_scalar(dst, src, w(1), sml[:, S_CB + j:S_CB + j + 1], ALU.mult, ALU.add))
                    step(V.scalar_tensor_tensor(dst[:, :, 1:S], src[:, :, 0:S - 1], w(0), dst[:, :, 1:S],
                                                ALU.mult, ALU.add))
                    step(V.scalar_tensor_tensor(dst[:, :, 0:S - 1], src[:, :, 1:S], w(2), dst[:, :, 0:S - 1],
                                                ALU.mult, ALU.add))
                announce("short_conv_done")
                dve.wait_ge(sem("natural_copied"), nth(dve, "natural_copied", 8))
                nat = proj[:, (C_HU + 4) * 512:(C_HU + 12) * 512]
                for o in range(2):
                    for s in range(2):
                        dve.wait_ge(sem("z_spectrum_ready"), nth(dve, "z_spectrum_ready"))
                        Y = hT[:, s * 2048:(s + 1) * 2048]
                        for m in range(2):
                            T = lambda cs: arena[:, ((o * 2 + m) * 2 + cs) * 512:][:, 0:512]
                            A, Bk = bank(2 * m), bank(2 * m + 1)
                            t0 = arena[:, 6144:6656]
                            re, im = Y[:, 2 * m * 512:(2 * m + 1) * 512], Y[:, (2 * m + 1) * 512:(2 * m + 2) * 512]
                            step(V.tensor_tensor(re, A, T(0), ALU.mult))
                            step(V.tensor_tensor(t0, Bk, T(1), ALU.mult))
                            step(V.tensor_tensor(re, re, t0, ALU.subtract))
                            step(V.tensor_tensor(im, A, T(1), ALU.mult))
                            step(V.tensor_tensor(t0, Bk, T(0), ALU.mult))
                            step(V.tensor_tensor(im, im, t0, ALU.add))
                        announce("y_spectrum_ready")
                        dve.wait_ge(sem("hyena_inverse_ready"), nth(dve, "hyena_inverse_ready"))
                        if o == 0:
                            part1 = nat[:, 2048 + s * 1024:2048 + (s + 1) * 1024]
                            signal(V.tensor_tensor(nat[:, s * 1024:(s + 1) * 1024], bank(4, 2), part1, ALU.mult),
                                   "hyena_z_ready")
                        else:
                            p2 = proj[:, C_HU * 512:(C_HU + 4) * 512].rearrange("p (c n) -> p c n", c=4)
                            g = proj[:, C_HG * 512:(C_HG + 4) * 512].rearrange("p (c n) -> p c n", c=4)
                            a = slice(s * S, (s + 1) * S)
                            step(V.tensor_tensor(p2[:, :, a], p2[:, :, a], g[:, :, a], ALU.mult))
                            signal(V.tensor_tensor(y3[:, 4:8, a], bank(4, 2).rearrange("p (c n) -> p c n", c=4),
                                                   p2[:, :, a], ALU.mult), "hyena_y_done")

            def attend(layer):
                us = attention_units(layer)
                n = len(us)
                if layer == 1:
                    dve.wait_ge(sem("y_gates_ready"), nth(dve, "y_gates_ready"))
                    dve.wait_ge(sem("position_bias_landed"), 16 * 32)
                    m = K(K_NBR, S).unsqueeze(1).to_broadcast([P, 16, S])
                    b = arena[:, 0:4096].rearrange("p (a n) -> p a n", a=16)
                    step(V.tensor_tensor(b, b, m, ALU.add))
                for i in range(n + 3):
                    if i < n:
                        u = us[i]
                        dve.wait_ge(sem("scores_ready"), nth(dve, "scores_ready"))
                        mx = stat[:, i % 4:i % 4 + 1]
                        nm = stat[:, 4 + i % 4:5 + i % 4]
                        if u["kind"] == "plain":
                            step(V.tensor_reduce(mx, bank(i % 2)[:, 0:u["keys"]], AX.X, ALU.max))
                            signal(V.tensor_scalar(nm, mx, -0.125, None, ALU.mult), "max_ready")
                        else:
                            sc = scores_sb(i)
                            rows = lambda a: a.rearrange("p (r c) -> p r c", r=4)
                            step(V.scalar_tensor_tensor(rows(sc[:, 0:S]), rows(bank(i % 2)[:, 0:S]), 0.125,
                                                        u["mask"], ALU.mult, ALU.add))
                            w = 512
                            if u["kind"] == "window":
                                step(V.tensor_copy(sc[:, 512:513], u["sink"]))
                                w = 513
                            dve.wait_ge(sem("context_scores_ready"), nth(dve, "context_scores_ready"))
                            step(V.tensor_reduce(mx, sc[:, 0:w], AX.X, ALU.max))
                            signal(V.tensor_scalar(nm, mx, -1.0, None, ALU.mult), "max_ready")
                    if 1 <= i <= n:
                        j = i - 1
                        dve.wait_ge(sem("probs_scaled_exp"), nth(dve, "probs_scaled_exp"))
                        pr = arena[:, 8192 + (j % 2) * 520:][:, 0:us[j]["keys"]]
                        rs = stat[:, 12 + j % 4:13 + j % 4]
                        step(V.reciprocal(rs, stat[:, 8 + j % 4:9 + j % 4]))
                        signal(V.tensor_scalar(pr, pr, rs, None, ALU.mult), "probs_ready")
                    if i >= 3:
                        u = us[i - 3]
                        dve.wait_ge(sem("o_ready"), nth(dve, "o_ready"))
                        o = bank(4 + (i - 3) % 2)[u["half"] * 64:u["half"] * 64 + 64, 0:P]
                        signal(V.tensor_tensor(u["y"], o, u["gate"], ALU.mult), "o_gated")
                announce("y2_ready")

            def out2(layer):
                for j in range(OUTP):
                    multiplied(1)
                    for m in range(2):
                        for s, dst in enumerate((x3, c3)[:2 - layer]):
                            c = 2 * j + m
                            step(V.scalar_tensor_tensor(
                                dst[:, c, :], bank(c)[:, s * S:(s + 1) * S],
                                ada[:, 32 + 2 * c + s:33 + 2 * c + s], dst[:, c, :], ALU.mult, ALU.add))
                announce("x_done")
                announce("ada_done")

            hyena_filters()
            for layer in range(2):
                modulate(layer)
                panel[0] += IN2
                qk_norm(layer)
                if layer == 0:
                    hyena()
                attend(layer)
                out2(layer)


def _columns(w):
    n = w.shape[1] // 256
    return w.reshape(KD, P, n, 256).transpose(2, 1, 0, 3).reshape(n, P, PW)


def _branch(w):
    return w.reshape(4, P, 2, 512).transpose(2, 1, 0, 3).reshape(2, P, PW)


def _rows(w):
    return w.reshape(FSTEP, 2, P, D).transpose(0, 2, 1, 3).reshape(FSTEP, P, PW)


def _chunks(v):
    return v.reshape(-1, P).T


def kernel(**inputs):
    import concourse.bacc as _bacc
    from concourse.bass_utils import run_bass_kernel_spmd as _run

    a = {k: np.asarray(v) for k, v in inputs.items()}
    panels = np.empty((PANELS, P, PW), np.float32)
    at = 0

    def put(block):
        nonlocal at
        panels[at:at + len(block)] = block
        at += len(block)

    def put_ffn(gate, up, down):
        g, u, d = _columns(gate), _columns(up), _rows(down)
        put(g[0:1])
        put(u[0:1])
        for f in range(1, FSTEP):
            put(g[f:f + 1])
            put(u[f:f + 1])
            put(d[f - 1:f])
        put(d[FSTEP - 1:])

    for layer in range(2):
        w = a["w_in"][layer]
        hq, hf, hi, hog, sq, sk, sv, ga, gb = np.split(w, [512, 1024, 1536, 2048, 2560, 3072, 3584, 4608], 1)
        for part in (hq, hf, hog, sq, sk, ga, gb, hi, sv):
            put(_columns(part))
        A, B = _branch(a["w_branch_hgrn"][layer]), _branch(a["w_branch_sb"][layer])
        for j in range(2):
            put(A[j:j + 1])
            put(B[j:j + 1])
        put(_columns(a["w_out"][layer]))
        if layer == 0:
            put_ffn(a["dense_w_gate"][0], a["dense_w_up"][0], a["dense_w_down"][0])
        else:
            for e in range(E):
                put_ffn(a["moe_w_gate"][0, e], a["moe_w_up"][0, e], a["moe_w_down"][0, e])
    heads = np.arange(512).reshape(2, 4, 64).transpose(1, 0, 2).reshape(-1)
    for layer in range(2):
        put(_columns(a["w_ada_2"][layer]))
        cols = np.arange(3328)
        cols[0:512] = heads
        cols[2304:2816] = 2304 + heads
        put(_columns(a["w_in_2"][layer][:, cols]))
        rows = np.arange(1024)
        rows[0:512] = heads
        put(_columns(a["w_out_2"][layer][rows]))
    assert at == PANELS

    small = np.zeros((P, S_N), np.float32)
    small[:, S_MIX:S_MIX + 16] = _chunks(a["mix_norm"])
    small[:, S_FFN:S_FFN + 16] = _chunks(a["ffn_norm"])
    small[:, S_FIN:S_FIN + 8] = _chunks(a["final_norm"])
    small[:, S_NG:S_NG + 16] = _chunks(a["norm_g_2"])
    small[:, S_ON:S_ON + 2] = _chunks(a["hgrn_out_norm"])
    small[:, S_LB:S_LB + 8] = _chunks(a["hgrn_lb_logits"])
    for i, name in enumerate(("glob_q_norm_2", "glob_k_norm_2", "win_q_norm_2", "win_k_norm_2", "nat_q_norm_2",
                              "nat_k_norm_2")):
        small[:, S_QK + i] = np.concatenate([a[name][0]] * 2)
    small[:, S_CW:S_CW + 36] = a["hy_conv_w_2"][0].reshape(3, 12, P).transpose(2, 1, 0).reshape(P, 36)
    small[:, S_CB:S_CB + 12] = _chunks(a["hy_conv_b_2"])
    small[:, S_SINK:S_SINK + 8] = a["win_sink_2"][0][None, :]
    small[:, S_ADA:S_ADA + 48] = _chunks(a["b_ada_2"])
    small[:, S_ROUT:S_ROUT + 64] = a["moe_router"][0].reshape(KD, P, E).transpose(1, 0, 2).reshape(P, 64)
    both = np.stack([a["c_2"][0], a["c_ctx_2"]])
    small[:, S_COND:S_COND + 16] = both.reshape(2, KD, P).transpose(2, 1, 0).reshape(P, 16)
    for i, name in enumerate(("hy_b1_2", "hy_b2_2", "hy_freq_2")):
        small[0:64, S_HYP + i] = a[name][0]

    def tokens(t):
        return np.ascontiguousarray(t[0].reshape(S, KD, P).transpose(2, 1, 0).reshape(P, KD * S))

    arrays = dict(
        panels=panels, x=tokens(a["x"]), ctx=tokens(a["ctx_2"]), consts=constants(), small=small, dft=dft_tables(),
        decay=decay_table(), position=position_table(), w1=a["hy_w1_2"][0], w2=a["hy_w2_2"][0], w3=a["hy_w3_2"][0],
        skip=a["hy_skip_2"].reshape(1024), rpb=a["nat_rpb_2"][0, :, :, ::-1].reshape(-1))
    arrays = {k: np.ascontiguousarray(v) for k, v in arrays.items()}
    nc = _bacc.Bacc("TRN2", target_bir_lowering=False, num_devices=1)
    args = [nc.dram_tensor(k, v.shape, F32, kind="ExternalInput").ap() for k, v in arrays.items()]
    out = nc.dram_tensor("y", (P, KD * S), F32, kind="ExternalOutput").ap()
    two_blocks(nc, *args, out)
    got = _run(nc, [arrays], core_ids=[0]).results[0]["y"]
    return np.ascontiguousarray(got.reshape(P, KD, S).transpose(2, 1, 0).reshape(1, S, D))
```

```python
from contextlib import ExitStack

import numpy as np

import concourse.bass as bass
from concourse import mybir

F32 = mybir.dt.float32
BF16 = mybir.dt.bfloat16
I32 = mybir.dt.int32
ACT = mybir.ActivationFunctionType
ALU = mybir.AluOpType
AX = mybir.AxisListType

P = 128
D = 1024
KD = D // P
S = 256
F = 3584
E = 8
PW = 2048
RING = 6
EPS = 1e-6
PI = float(np.pi)
SLOTS = 128

IN1 = 22
IN2 = 13
ADA = 12
OUTP = 4
FSTEP = F // 256
FFN = 3 * FSTEP
LAYER1 = IN1 + OUTP + OUTP
BLOCK1 = LAYER1 + FFN + LAYER1 + E * FFN
LAYER2 = ADA + IN2 + OUTP
PANELS = BLOCK1 + 2 * LAYER2

HQ, HF, HOG, SQ, SK, GA, GB = 0, 4, 8, 12, 16, 20, 28
HI, SV = 18, 20
C_Q, C_K, C_V, C_HU, C_G, C_HG = 0, 4, 5, 6, 18, 22
C_NQ, C_NK, C_NV = 6, 10, 14

(K_ID, K_ONE, K_1024, K_128, K_BD, K_SWAP, K_TRI, K_NEG, K_LEV, K_STRICT, K_COS, K_SIN, K_WIN, K_NBR,
 K_LOW) = np.cumsum([0, 128, 128, 128, 128, 128, 128, 128, 128, 896, 128, 256, 256, 512, 256]).tolist()
K_EPS = K_LOW + 64
K_IOTA = K_EPS + 1
K_N = K_IOTA + P
S_MIX, S_FFN, S_FIN, S_NG, S_ON, S_LB, S_QK, S_CW, S_CB, S_SINK, S_ADA, S_ROUT, S_COND, S_HYP = np.cumsum(
    [0, 16, 16, 8, 16, 2, 8, 6, 36, 12, 8, 48, 64, 16]).tolist()
S_N = S_HYP + 3


def constants():
    c = np.zeros((P, K_N), np.float32)
    i, j = np.arange(P)[:, None], np.arange(P)[None, :]
    c[:, K_ID:K_ID + P] = i == j
    c[:, K_ONE:K_ONE + P] = 1.0
    c[:, K_1024:K_1024 + P] = 1.0 / D
    c[:, K_128:K_128 + P] = 1.0 / P
    c[:, K_BD:K_BD + P] = (i // 64 == j // 64) / 64.0
    c[:, K_SWAP:K_SWAP + P] = ((j % 2 == 1) & (i == j - 1)) * 1.0 - ((j % 2 == 0) & (i == j + 1)) * 1.0
    c[:, K_TRI:K_TRI + P] = -1.0 * (i >= j)
    c[:, K_NEG:K_NEG + P] = -1.0
    for lv in range(7):
        c[:, K_LEV + lv * P:K_LEV + (lv + 1) * P] = ((i >> lv) % 2 == 0) & ((j >> lv) == (i >> lv) + 1)
    c[:, K_STRICT:K_STRICT + P] = i < j
    t = np.arange(S)
    inv = 10000.0 ** (-np.arange(16, dtype=np.float32) / np.float32(16))
    ang = np.concatenate([(t // 64).astype(np.float32)[:, None] * inv, (t % 64).astype(np.float32)[:, None] * inv], -1)
    pair = (np.arange(P) % 64) // 2
    c[:, K_COS:K_COS + S] = np.cos(ang.astype(np.float32)).T[pair]
    c[:, K_SIN:K_SIN + S] = np.sin(ang.astype(np.float32)).T[pair]
    for qt in range(2):
        q = qt * P + np.arange(P)[:, None]
        c[:, K_WIN + qt * S:K_WIN + (qt + 1) * S] = np.where(np.abs(t[None, :] - q) <= 128, 0.0, -1e30)
    c0 = np.clip(np.arange(P) % 64 - 8, 0, 48)[:, None]
    kc = 63 - (t % 64)[None, :]
    c[:, K_NBR:K_NBR + S] = np.where((kc >= c0) & (kc < c0 + 16), 0.0, -1e30)
    low = (np.arange(8)[None, :] < np.arange(8)[:, None]) * 1.0
    c[:, K_LOW:K_LOW + 64] = low.reshape(1, 64)
    c[:, K_EPS] = EPS
    c[:, K_IOTA:K_IOTA + P] = j
    return c


def dft_tables():
    t = np.arange(S, dtype=np.float64)
    a = np.pi * np.outer(t, 2 * t + 1) / 512.0
    rows = lambda m: m.reshape(2, P, S).transpose(1, 0, 2).reshape(P, 2 * S)
    return np.concatenate([rows(np.cos(a)), rows(np.sin(a)), rows(np.cos(a).T / 256), rows(np.sin(a).T / 256)],
                          1).astype(np.float32)


def decay_table():
    t = np.linspace(0.0, 1.0, S, dtype=np.float32)[:, None]
    deltas = np.linspace(np.log(1e-2) / 1.5, np.log(1e-2) / 0.3, 512, dtype=np.float32)
    d = np.exp(-t * np.abs(deltas)).astype(np.float32)
    return d.reshape(2, P, 512).transpose(1, 0, 2).reshape(P, 1024)


def position_table():
    t = np.linspace(0.0, 1.0, S, dtype=np.float32)[:, None]
    w = (2.0 * np.pi * np.arange(S, dtype=np.float32)[:, None] / S).astype(np.float32)
    f = np.linspace(1e-4, 15, 16, dtype=np.float32)[None, :]
    return np.concatenate([t, np.cos(f * w), -np.sin(f * w)], -1).T.astype(np.float32)


def two_blocks(nc, panels, x_in, ctx_in, consts_in, small_in, dft_in, decay_in, pos_in, w1_in, w2_in, w3_in,
               skip_in, rpb_in, out):
    stack = ExitStack()
    with stack:
        def sb(name, words, parts=P, dt=F32):
            return stack.enter_context(nc.sbuf_tensor(name, [parts, words], dt))

        sems = {}

        def sem(name):
            if name not in sems:
                sems[name] = stack.enter_context(nc.semaphore(name))
            return sems[name]

        seen = {}

        def nth(eng, name, k=1):
            key = (eng.engine, name)
            seen[key] = seen.get(key, 0) + k
            return seen[key]

        ring = sb("ring", RING * PW)
        xT = sb("xT", KD * S)
        cT = sb("cT", KD * S)
        hT = sb("hT", KD * 512)
        proj = sb("proj", 26 * 512)
        yT = sb("yT", KD * 512)
        arena = sb("arena", 9728)
        cst = sb("cst", K_N)
        sml = sb("sml", S_N)
        rstd = sb("rstd", 512)
        ada = sb("ada", 48)
        ada_a = sb("ada_a", 16)
        cond = sb("cond", 16)
        lbs = sb("lbs", 32)
        stat = sb("stat", 16)
        rt = sb("rt", 400)
        zrow = sb("zrow", 640, dt=BF16)
        ps = stack.enter_context(nc.psum_tensor("ps", [P, 8, 512], F32))

        h3 = hT[:, :].rearrange("p (k n) -> p k n", k=KD)
        y3 = yT[:, :].rearrange("p (k n) -> p k n", k=KD)
        x3 = xT[:, :].rearrange("p (k n) -> p k n", k=KD)
        c3 = cT[:, :].rearrange("p (k n) -> p k n", k=KD)
        ones1 = cst[:, K_ONE:K_ONE + 1]
        eps1 = cst[:, K_EPS:K_EPS + 1]

        def K(at, n=P):
            return cst[:, at:at + n]

        def bank(b, n=1):
            return ps[:, b:b + n, :].rearrange("p b n -> p (b n)")

        def slot(p, a, b):
            s = p % RING
            return ring[:, s * PW + a:s * PW + b]

        def qk_chunks(layer):
            if layer == 0:
                return [(C_Q + c, 512, 0, True) for c in range(4)] + [(C_K, 512, 1, True)]
            return ([(C_Q + c, S, 2, True) for c in range(4)] + [(C_K, 512, 3, True)]
                    + [(C_NQ + c, S, 4, False) for c in range(4)] + [(C_NK + c, 512, 5, False) for c in range(4)])

        def attention_units(layer):
            us = []

            def gqa(c, half, qt, stream, kind):
                r = slice(half * 64, half * 64 + 64)
                first = 0 if stream == 0 else 2
                us.append(dict(
                    half=half, keys=512 if stream == 0 else 256, kind=kind,
                    q=proj[r, (C_Q + c) * 512 + stream * S + qt * P:][:, 0:P],
                    k=proj[r, C_K * 512 + stream * S:(C_K + 1) * 512],
                    v=lambda n: proj[:, C_V * 512 + (first + n) * P + half * 64:][:, 0:64],
                    mask=K(K_WIN + qt * S, S).rearrange("p (r c) -> p r c", r=4),
                    sink=sml[:, S_SINK + c + 4 * half:S_SINK + c + 4 * half + 1],
                    gate=proj[r, (C_G + c) * 512 + stream * S + qt * P:][:, 0:P],
                    y=yT[r, c * 512 + stream * S + qt * P:][:, 0:P]))

            def neighbour(h, qt):
                half, c = h % 2, h // 2
                r = slice(half * 64, half * 64 + 64)
                us.append(dict(
                    half=half, keys=512, kind="neighbour",
                    q=proj[r, (C_NQ + c) * 512 + qt * P:][:, 0:P], k=proj[r, (C_NK + c) * 512:(C_NK + c + 1) * 512],
                    v=lambda n: proj[:, (C_NV + 2 * (h // 4)) * 512 + n * S + (h % 4) * 64:][:, 0:64],
                    mask=arena[:, (h * 2 + qt) * S:(h * 2 + qt + 1) * S].rearrange("p (r c) -> p r c", r=4)[:, :, ::-1],
                    gate=proj[r, (C_HG + c) * 512 + qt * P:][:, 0:P],
                    y=yT[r, (4 + c) * 512 + qt * P:][:, 0:P]))

            if layer == 0:
                for c in range(4):
                    for half in range(2):
                        for stream in range(2):
                            for qt in range(2):
                                gqa(c, half, qt, stream, "plain")
            else:
                for c in range(4):
                    for half in range(2):
                        for qt in range(2):
                            gqa(c, half, qt, 0, "window")
                for h in range(8):
                    for qt in range(2):
                        neighbour(h, qt)
            return us

        def qk_root(i):
            return arena[:, 7424:7936] if i % 2 else rstd[:, :]

        def probs(i):
            return arena[:, 6144 + (i % 3) * 520:][:, 0:520]

        def probsT(i):
            return arena[:, 7704 + (i % 2) * 512:][:, 0:512]

        def scores_sb(i):
            return arena[:, 4096 + (i % 2) * 520:4096 + (i % 2) * 520 + 520]

        hN = proj[:, 4096:6144]
        xeT = proj[:, 6144:7168]
        yS = proj[:, 7168:8192]
        G = proj[:, 9216:11520]
        SEL = arena[:, 4096:6144]
        SELW = arena[:, 6144:8192]
        crowded = stack.enter_context(nc.sbuf_tensor("crowded", [1, 1], I32))

        block = stack.enter_context(nc.Block())
        LANDED = [sem(f"panel_landed_{s}") for s in range(RING)]
        DONE = sem("panels_multiplied")

        @block.sync
        def _(sp):
            def load(p, s):
                sp.dma_start(ring[:, s * PW:(s + 1) * PW], panels[bass.ds(p, 1), :, :].rearrange("a p n -> p (a n)")) \
                  .then_inc(LANDED[s], 16)

            sp.dma_start(xT[:, :], x_in).then_inc(sem("inputs_landed"), 16)
            sp.dma_start(sml[:, :], small_in).then_inc(sem("inputs_landed"), 16)
            sp.dma_start(cst[:, :], consts_in).then_inc(sem("inputs_landed"), 16)
            for s in range(RING):
                load(s, s)
            sp.dma_start(cT[:, :], ctx_in).then_inc(sem("context_landed"), 16)
            full = PANELS // RING
            with sp.Fori(1, full) as r:
                for s in range(RING):
                    sp.wait_ge(DONE, r * RING + (s - RING + 1))
                    load(r * RING + s, s)
            for p in range(full * RING, PANELS):
                sp.wait_ge(DONE, p - RING + 1)
                load(p, p % RING)

        @block.tensor
        def _(pe):
            at = [0]

            def mm(o, w, m, start, stop, skip=False):
                return nc.tensor.matmul(o, w, m, start=start, stop=stop, skip_group_check=skip)

            def landed(p, rounds=0):
                pe.wait_ge(LANDED[p % RING], 16 * (p // RING + 1) + rounds * 16)

            def take():
                p = at[0]
                at[0] += 1
                landed(p)
                return p

            def panel_T(p, b, n, rhs):
                for m in range(2):
                    o = bank(b)[:, m * 256:m * 256 + n] if n <= 256 else bank(b + m)
                    for k in range(KD):
                        last = mm(o, slot(p, k * 256 + m * P, k * 256 + (m + 1) * P), rhs(k), k == 0, k == KD - 1)
                return last

            def norm(streams=1):
                pe.wait_ge(sem("squares_ready"), nth(pe, "squares_ready"))
                for s in range(streams):
                    for k in range(KD):
                        last = mm(bank(0)[:, s * S:(s + 1) * S], K(K_1024), h3[:, k, s * S:(s + 1) * S],
                                  k == 0, k == KD - 1)
                last.then_inc(sem("mean_square_ready"), 1)

            def project1():
                pe.wait_ge(sem("h_ready"), nth(pe, "h_ready", KD))
                for p in range(IN1):
                    q = take()
                    if p >= 8:
                        copied = "proj_even_copied" if p % 2 == 0 else "proj_odd_copied"
                        pe.wait_ge(sem(copied), nth(pe, copied))
                    if p < 18:
                        last = panel_T(q, p % 8, S, lambda k: h3[:, k, 0:S])
                    else:
                        for tb in range(2):
                            for k in range(KD):
                                last = mm(bank(p % 8)[:, tb * S:(tb + 1) * S], h3[:, k, tb * P:(tb + 1) * P],
                                          slot(q, k * 256, (k + 1) * 256), k == 0, k == KD - 1)
                    last.then_inc(DONE, 1)
                seen[(pe.engine, "proj_even_copied")] += 4
                seen[(pe.engine, "proj_odd_copied")] += 4

            def hgrn():
                q = arena[:, 0:1024]
                kk = arena[:, 1024:2048]
                X = [arena[:, 5120:6144], arena[:, 6144:7168]]
                pe.wait_ge(sem("hgrn_qk_ready"), nth(pe, "hgrn_qk_ready"))
                for h in range(8):
                    last = mm(bank(0, 2)[:, h * P:(h + 1) * P], kk[:, h * P:(h + 1) * P], q[:, h * P:(h + 1) * P],
                              True, True)
                last.then_inc(sem("level_scores_ready"), 1)
                for lv in range(8):
                    pe.wait_ge(sem("level_q_ready"), nth(pe, "level_q_ready"))
                    pe.wait_ge(sem("level_k_ready"), nth(pe, "level_k_ready"))
                    x = X[lv % 2]
                    if lv >= 1:
                        pe.wait_ge(sem("level_merged"), nth(pe, "level_merged"))
                    if lv < 7:
                        for h in range(8):
                            xs = x[:, h * P:(h + 1) * P]
                            last = mm(bank(2 - 2 * (lv % 2), 2)[:, h * P:(h + 1) * P], xs, xs, True, True)
                    else:
                        for h in range(4):
                            last = mm(bank(4)[:, h * P:(h + 1) * P], x[:, h * S:h * S + P],
                                      x[:, h * S + P:(h + 1) * S], True, True)
                    last.then_inc(sem("level_scores_ready"), 1)
                pe.wait_ge(sem("hgrn_scores_merged"), nth(pe, "hgrn_scores_merged"))
                pe.wait_ge(sem("level_merged"), nth(pe, "level_merged"))
                sc = arena[:, 7168:8192]
                cross = arena[:, 8192:8704]
                for h in range(4):
                    o = bank(5 + h // 2)[:, (h % 2) * S:(h % 2 + 1) * S]
                    v = lambda tb: proj[:, (HI + h // 2) * 512 + tb * S + (h % 2) * P:][:, 0:P]
                    mm(o[:, 0:P], v(0), sc[:, 2 * h * P:(2 * h + 1) * P], True, True)
                    mm(o[:, P:S], v(1), sc[:, (2 * h + 1) * P:(2 * h + 2) * P], True, False)
                    last = mm(o[:, P:S], v(0), cross[:, h * P:(h + 1) * P], False, True)
                last.then_inc(sem("hgrn_o_ready"), 1)
                pe.wait_ge(sem("hgrn_o_squared"), nth(pe, "hgrn_o_squared"))
                for j in range(2):
                    last = mm(bank(7 if j else 4), K(K_128), arena[:, 3072 + j * 512:3072 + (j + 1) * 512], True, True)
                last.then_inc(sem("hgrn_mean_square_ready"), 1)

            def stick():
                pe.wait_ge(sem("hgrn_done"), nth(pe, "hgrn_done"))
                for g in range(2):
                    L = arena[:, g * 3072:g * 3072 + 1536]
                    W = arena[:, g * 3072 + 1536:(g + 1) * 3072]
                    if g:
                        pe.wait_ge(sem("stick_exponent_ready"), nth(pe, "stick_exponent_ready", 1))
                        seen[(pe.engine, "stick_exponent_ready")] += 1
                    for i in range(4):
                        h = 4 * g + i
                        r = slice((h % 2) * 64, (h % 2) * 64 + 64)
                        kh = proj[r, (SK + h // 2) * S:(SK + h // 2 + 1) * S]
                        qh = proj[r, (SQ + h // 2) * S:(SQ + h // 2 + 1) * S]
                        mm(bank(i)[:, 0:S], kh[:, 0:P], qh, True, False, True)
                        last = mm(bank(i)[:, S:S + P], kh[:, P:S], qh[:, P:S], False, False, True)
                    last.then_inc(sem("stick_z_ready"), 1)
                    pe.wait_ge(sem("stick_softplus_ready"), nth(pe, "stick_softplus_ready"))
                    for i in range(4):
                        l = L[:, i * 384:(i + 1) * 384]
                        mm(bank(i)[:, 0:S], K(K_TRI), l[:, 0:S], False, False, True)
                        mm(bank(i)[:, P:S], K(K_NEG), l[:, S:384], False, False, True)
                        last = mm(bank(i)[:, S:384], K(K_TRI), l[:, S:384], False, True, True)
                    last.then_inc(sem("stick_sums_ready"), 1)
                    pe.wait_ge(sem("stick_weights_ready"), nth(pe, "stick_weights_ready"))
                    for i in range(4):
                        h = 4 * g + i
                        o = bank(4 + g)[(h % 2) * 64:(h % 2) * 64 + 64, (i // 2) * S:(i // 2 + 1) * S]
                        v = lambda tb: proj[:, (SV + h // 4) * 512 + tb * S + (h % 4) * 64:][:, 0:64]
                        w = W[:, i * 384:(i + 1) * 384]
                        mm(o, v(0), w[:, 0:S], True, False)
                        last = mm(o[:, P:S], v(1), w[:, S:384], False, True)
                    last.then_inc(sem("stick_o_ready"), 1)

            def mix_out():
                pe.wait_ge(sem("o_a_ready"), nth(pe, "o_a_ready"))
                pe.wait_ge(sem("o_b_ready"), nth(pe, "o_b_ready", 2))
                for j in range(2):
                    for br in range(2):
                        q = take()
                        for m in range(4):
                            o = bank(4 * j + 2 * br + m // 2)[:, (m % 2) * S:(m % 2 + 1) * S]
                            for k in range(4):
                                last = mm(o, slot(q, k * 512 + m * P, k * 512 + (m + 1) * P),
                                          y3[:, 4 * br + k, 0:S], k == 0, k == 3)
                        last.then_inc(DONE, 1)
                pe.wait_ge(sem("mixed_ready"), nth(pe, "mixed_ready", 2))
                for j in range(OUTP):
                    panel_T(take(), j, S, lambda k: h3[:, k, 0:S]).then_inc(DONE, 1)

            def ffn(p0, e=0):
                hb = [arena[:, 1024:1536], arena[:, 1536:2048]]

                def up(p, f, r):
                    for j in range(2):
                        landed(p + j, r)
                        panel_T(p + j, 2 * j + f % 2, S, lambda k: h3[:, k, 0:S]).then_inc(DONE, 1)

                def down(p, f, r, count):
                    landed(p, r)
                    pe.wait_ge(sem("hidden_ready"), count)
                    for k in range(2):
                        for m in range(KD):
                            last = mm(bank(4 + m // 2)[:, (m % 2) * S:(m % 2 + 1) * S],
                                      slot(p, k * D + m * P, k * D + (m + 1) * P),
                                      hb[f % 2][:, k * S:(k + 1) * S], False, True, True)
                    last.then_inc(DONE, 1)

                h0 = hid[0]
                er = e * (FFN // RING)
                up(p0, 0, er)
                pe.wait_ge(sem("accumulators_free"), e + accs[0])
                for b in range(4):
                    mm(bank(4 + b), zrow[:, 0:P], zrow[:, P:640], True, False, True)
                with pe.Fori(0, FSTEP // 2 - 1) as i:
                    up(p0 + 2, 1, er + i)
                    down(p0 + 4, 0, er + i, e * FSTEP + i * 2 + (h0 + 1))
                    up(p0 + 5, 0, er + i)
                    down(p0 + 7, 1, er + i, e * FSTEP + i * 2 + (h0 + 2))
                up(p0 + 38, 1, er)
                down(p0 + 40, 0, er, e * FSTEP + (h0 + FSTEP - 1))
                down(p0 + 41, 1, er, e * FSTEP + (h0 + FSTEP))

            def router():
                pe.wait_ge(sem("h_ready"), nth(pe, "h_ready", KD))
                for tb in range(2):
                    for k in range(KD):
                        last = mm(bank(1)[:, tb * 8:tb * 8 + 8], h3[:, k, tb * P:(tb + 1) * P],
                                  sml[:, S_ROUT + k * 8:S_ROUT + k * 8 + 8], k == 0, k == KD - 1)
                last.then_inc(sem("logits_ready"), 1)
                for j in range(4):
                    tb, half = j // 2, j % 2
                    if j == 1:
                        pe.wait_ge(sem("logits_copied"), nth(pe, "logits_copied"))
                    for c in range(4):
                        last = nc.tensor.transpose(bank(j)[:, c * P:(c + 1) * P],
                                                   h3[:, half * 4 + c, tb * P:(tb + 1) * P], K(K_ID))
                last.then_inc(sem("h_turned"), 1)
                pe.wait_ge(sem("selected_ready"), nth(pe, "selected_ready"))
                s0, s1 = rt[:, 40:48], rt[:, 48:56]
                o = bank(7)
                mm(o[:, 0:8], K(K_STRICT), s0, True, True)
                mm(o[:, 8:16], K(K_ONE), s0, True, False)
                mm(o[:, 8:16], K(K_STRICT), s1, False, True)
                mm(o[:, 16:24], K(K_ONE), s0, True, False)
                mm(o[:, 16:24], K(K_ONE), s1, False, True).then_inc(sem("places_ready"), 1)
                pe.wait_ge(sem("combine_diagonals_ready"), nth(pe, "combine_diagonals_ready"))
                for b in range(4):
                    last = mm(bank(4 + b), K(K_ONE), arena[:, 4096 + b * 512:4096 + (b + 1) * 512], True, True)
                last.then_inc(sem("combine_ready"), 1)
                pe.wait_ge(sem("weighted_selection_ready"), nth(pe, "weighted_selection_ready"))
                for j in range(16):
                    last = nc.tensor.transpose(bank(4, 4)[:, j * P:(j + 1) * P], SELW[:, j * P:(j + 1) * P], K(K_ID))
                last.then_inc(sem("slot_weights_ready"), 1)
                pe.wait_ge(sem("slot_weights_copied"), nth(pe, "slot_weights_copied"))
                pe.wait_ge(sem("h_tokens_copied"), nth(pe, "h_tokens_copied"))
                pe.wait_ge(sem("crowded_ready"), nth(pe, "crowded_ready"))

            def scatter(e, count):
                for j in range(4):
                    if j >= 2:
                        pe.wait_ge(sem("rows_added"), count + (j - 1))
                    for m in range(2):
                        c = 2 * j + m
                        last = mm(bank(6 + j % 2)[:, m * S:(m + 1) * S], yS[:, c * P:(c + 1) * P],
                                  G[:, bass.ds(e * S, S)], True, True)
                    last.then_inc(sem("rows_spread"), 1)

            def compact_expert(p0, e):
                hd = [arena[:, 1024:1280], arena[:, 1536:1792]]
                hT2 = [arena[:, 1280:1536], arena[:, 1792:2048]]
                er = e * (FFN // RING)

                def up(p, b, r):
                    landed(p, r)
                    for k in range(KD):
                        last = mm(bank(b)[:, 0:S], xeT[:, k * P:(k + 1) * P], slot(p, k * 256, (k + 1) * 256),
                                  k == 0, k == KD - 1)
                    last.then_inc(DONE, 1)

                def turn(f, count):
                    pe.wait_ge(sem("c_hidden_ready"), count)
                    for k in range(2):
                        last = nc.tensor.transpose(bank(6)[:, k * P:(k + 1) * P], hd[f % 2][:, k * P:(k + 1) * P],
                                                   K(K_ID))
                    last.then_inc(sem("c_hidden_turned"), 1)

                def down(p, f, r, count):
                    landed(p, r)
                    pe.wait_ge(sem("c_hidden_copied"), count)
                    for k in range(2):
                        for n in range(2):
                            last = mm(bank(4 + n), hT2[f % 2][:, k * P:(k + 1) * P],
                                      slot(p, k * D + n * 512, k * D + (n + 1) * 512), False, True, True)
                    last.then_inc(DONE, 1)

                for half in range(2):
                    for c in range(4):
                        for tb in range(2):
                            last = mm(bank(2 + half)[:, c * P:(c + 1) * P],
                                      hN[:, tb * D + (half * 4 + c) * P:][:, 0:P],
                                      SEL[:, bass.ds(e * S + tb * P, P)], tb == 0, tb == 1)
                last.then_inc(sem("tokens_gathered"), 1)
                pe.wait_ge(sem("rows_copied"), e + 1)
                scatter(e, e * 4)
                pe.wait_ge(sem("tokens_copied"), e * 2 + 2)
                up(p0, 0, er)
                for b in range(2):
                    mm(bank(4 + b), zrow[:, 0:P], zrow[:, P:640], True, False, True)
                pe.wait_ge(sem("rows_added"), e * 4 + 4)
                up(p0 + 1, 2, er)
                with pe.Fori(0, FSTEP // 2 - 1) as i:
                    up(p0 + 2, 1, er + i)
                    turn(0, e * FSTEP + i * 2 + 1)
                    up(p0 + 3, 3, er + i)
                    down(p0 + 4, 0, er + i, e * FSTEP + i * 2 + 1)
                    up(p0 + 5, 0, er + i)
                    turn(1, e * FSTEP + i * 2 + 2)
                    up(p0 + 6, 2, er + i)
                    down(p0 + 7, 1, er + i, e * FSTEP + i * 2 + 2)
                up(p0 + 38, 1, er)
                turn(0, e * FSTEP + (FSTEP - 1))
                up(p0 + 39, 3, er)
                down(p0 + 40, 0, er, e * FSTEP + (FSTEP - 1))
                turn(1, e * FSTEP + FSTEP)
                down(p0 + 41, 1, er, e * FSTEP + FSTEP)

            hid, accs = [0], [1]
            pe.wait_ge(sem("inputs_landed"), 48)
            for layer in range(2):
                norm()
                project1()
                hgrn()
                stick()
                mix_out()
                norm()
                if layer == 0:
                    pe.wait_ge(sem("h_ready"), nth(pe, "h_ready", KD))
                    ffn(at[0])
                    at[0] += FFN
                    hid[0] += FSTEP
                    accs[0] += 2
                else:
                    router()
                    many = pe.value_load(crowded[0:1, 0:1], min_val=0, max_val=1)
                    with pe.If(many == 1):
                        with pe.Fori(0, E) as e:
                            ffn(at[0], e)
                    with pe.Else():
                        with pe.Fori(0, E) as e:
                            compact_expert(at[0], e)
                        pe.wait_ge(sem("rows_copied"), E + 1)
                        scatter(E, 4 * E)
                    at[0] += E * FFN
            norm()

            def hyena_filters():
                h1 = proj[0:64, 2304:2560]
                h2 = proj[0:64, 2560:2816]
                pe.wait_ge(sem("filter_tables_landed"), nth(pe, "filter_tables_landed", 16 * 7))
                mm(bank(1)[0:64, 0:S], proj[0:33, 2816:2880], proj[0:33, 2048:2304], True, True) \
                    .then_inc(sem("filter_hidden_sum"), 1)
                pe.wait_ge(sem("filter_hidden_ready"), nth(pe, "filter_hidden_ready"))
                mm(bank(1)[0:64, 0:S], proj[0:64, 2880:2944], h1, True, True).then_inc(sem("filter_hidden_sum"), 1)
                pe.wait_ge(sem("filter_hidden_ready"), nth(pe, "filter_hidden_ready"))
                for o in range(2):
                    if o:
                        pe.wait_ge(sem("filter_spectrum_ready"), nth(pe, "filter_spectrum_ready"))
                    for tb in range(2):
                        for d in range(2):
                            last = mm(bank(tb * 2 + d), h2[:, tb * P:(tb + 1) * P],
                                      proj[0:64, (o * 2 + d) * 512:(o * 2 + d + 1) * 512], True, True)
                    last.then_inc(sem("filter_taps_sum"), 1)
                    pe.wait_ge(sem("taps_squared"), nth(pe, "taps_squared"))
                    for j in range(4):
                        last = mm(bank(4), K(K_ONE), proj[:, 9216 + j * 512:9216 + (j + 1) * 512], j == 0, j == 3)
                    last.then_inc(sem("taps_energy_ready"), 1)
                    pe.wait_ge(sem("taps_combined"), nth(pe, "taps_combined"))
                    pe.wait_ge(sem("taps_rnorm_ready"), nth(pe, "taps_rnorm_ready"))
                    for m in range(2):
                        for cs in range(2):
                            for tb in range(2):
                                last = mm(bank(4 + 2 * m + cs),
                                          arena[:, 4096 + cs * 512 + tb * S + m * P:][:, 0:P],
                                          proj[:, 6144 + cs * 1024 + tb * 512:][:, 0:512], tb == 0, tb == 1)
                    last.then_inc(sem("spectrum_sum"), 1)
                pe.wait_ge(sem("filter_spectrum_ready"), nth(pe, "filter_spectrum_ready"))

            def adaln():
                if at[0] == BLOCK1:
                    pe.wait_ge(sem("cond_ready"), nth(pe, "cond_ready"))
                else:
                    pe.wait_ge(sem("ada_done"), nth(pe, "ada_done"))
                for p in range(ADA):
                    q = take()
                    for k in range(KD):
                        last = mm(bank(1 + p // 2)[0:2, (p % 2) * 256:(p % 2 + 1) * 256], cond[:, 2 * k:2 * k + 2],
                                  slot(q, k * 256, (k + 1) * 256), k == 0, k == KD - 1)
                    last.then_inc(DONE, 1)
                pe.wait_ge(sem("ada_rows_copied"), nth(pe, "ada_rows_copied"))
                for c in range(24):
                    last = nc.tensor.transpose(bank(7)[:, 2 * c:2 * c + 2], arena[0:2, 6144 + c * P:][:, 0:P],
                                               cst[0:2, K_ID:K_ID + 2])
                last.then_inc(sem("ada_turned"), 1)

            def project2(layer):
                pe.wait_ge(sem("h_mod_ready"), nth(pe, "h_mod_ready", 2 * KD))
                for p in range(IN2):
                    q = take()
                    b = 2 * (p % 4)
                    if p >= 4:
                        pe.wait_ge(sem("pair_copied"), nth(pe, "pair_copied"))
                    wide = layer == 0 or p in (2, 5, 6)
                    n = 512 if wide else S
                    if layer == 1 and p in (7, 8):
                        for tb in range(4):
                            for k in range(KD):
                                last = mm(bank(b, 2)[:, tb * S:(tb + 1) * S], h3[:, k, tb * P:(tb + 1) * P],
                                          slot(q, k * 256, (k + 1) * 256), k == 0, k == KD - 1)
                    elif p == 2:
                        for k in range(KD):
                            mm(bank(b), slot(q, k * 256, k * 256 + P), h3[:, k, :], k == 0, k == KD - 1)
                        for tb in range(4):
                            for k in range(KD):
                                last = mm(bank(b + 1)[:, tb * P:(tb + 1) * P], h3[:, k, tb * P:(tb + 1) * P],
                                          slot(q, k * 256 + P, (k + 1) * 256), k == 0, k == KD - 1)
                    else:
                        for m in range(2):
                            for k in range(KD):
                                last = mm(bank(b + m)[:, 0:n], slot(q, k * 256 + m * P, k * 256 + (m + 1) * P),
                                          h3[:, k, 0:n], k == 0, k == KD - 1)
                    last.then_inc(DONE, 1)
                pe.wait_ge(sem("pair_copied"), nth(pe, "pair_copied", 4))

            def qk_norm(layer):
                chunks = qk_chunks(layer)

                def mean_square(i):
                    n = chunks[i][1]
                    pe.wait_ge(sem("qk_squared"), nth(pe, "qk_squared"))
                    mm(bank(i % 2)[:, 0:n], K(K_BD), arena[:, 6144 + (i % 2) * 512:][:, 0:n], True, True) \
                        .then_inc(sem("qk_mean_square"), 1)

                mean_square(0)
                mean_square(1)
                for i, (c, n, g, rope) in enumerate(chunks):
                    pe.wait_ge(sem("qk_root_ready"), nth(pe, "qk_root_ready"))
                    if i + 2 < len(chunks):
                        mean_square(i + 2)
                    pe.wait_ge(sem("qk_normed"), nth(pe, "qk_normed"))
                    if rope:
                        mm(bank(2 + i % 2)[:, 0:S], K(K_SWAP), proj[:, c * 512:c * 512 + S], True, True) \
                            .then_inc(sem("qk_swapped"), 1)
                pe.wait_ge(sem("qk_done"), nth(pe, "qk_done"))

            def hyena():
                nat = proj[:, (C_HU + 4) * 512:(C_HU + 12) * 512]
                for j in range(8):
                    part, tb = j // 4, j % 4
                    if j == 0:
                        pe.wait_ge(sem("short_conv_done"), nth(pe, "short_conv_done"))
                    if j >= 2:
                        pe.wait_ge(sem("natural_copied"), nth(pe, "natural_copied"))
                    for c in range(4):
                        last = nc.tensor.transpose(bank(j % 2)[:, c * P:(c + 1) * P],
                                                   h3[:, part * 4 + c, tb * P:(tb + 1) * P], K(K_ID))
                    last.then_inc(sem("natural_ready"), 1)
                pe.wait_ge(sem("natural_copied"), nth(pe, "natural_copied", 2))
                for o in range(2):
                    for s in range(2):
                        z = nat[:, s * 1024:(s + 1) * 1024]
                        if o == 1 and s == 0:
                            pe.wait_ge(sem("hyena_z_ready"), nth(pe, "hyena_z_ready"))
                        for m in range(2):
                            for cs in range(2):
                                for tb in range(2):
                                    last = mm(bank(2 * m + cs), arena[:, 4096 + cs * 512 + tb * S + m * P:][:, 0:P],
                                              z[:, tb * 512:(tb + 1) * 512], tb == 0, tb == 1)
                        last.then_inc(sem("z_spectrum_ready"), 1)
                        pe.wait_ge(sem("y_spectrum_ready"), nth(pe, "y_spectrum_ready"))
                        Y = hT[:, s * 2048:(s + 1) * 2048]
                        if o == 0:
                            if s:
                                pe.wait_ge(sem("hyena_z_ready"), nth(pe, "hyena_z_ready"))
                            for tb in range(2):
                                for j in range(4):
                                    kc, cs = j // 2, j % 2
                                    last = mm(bank(4 + tb), arena[:, 5120 + cs * 512 + kc * S + tb * P:][:, 0:P],
                                              Y[:, j * 512:(j + 1) * 512], j == 0, j == 3)
                        else:
                            if s:
                                pe.wait_ge(sem("hyena_y_done"), nth(pe, "hyena_y_done"))
                            for c in range(4):
                                for j in range(4):
                                    kc, cs = j // 2, j % 2
                                    last = mm(bank(4 + c // 2)[:, (c % 2) * S:(c % 2 + 1) * S],
                                              Y[:, j * 512 + c * P:j * 512 + (c + 1) * P],
                                              arena[:, 5120 + cs * 512 + kc * S:][:, 0:S], j == 0, j == 3)
                        last.then_inc(sem("hyena_inverse_ready"), 1)
                pe.wait_ge(sem("hyena_y_done"), nth(pe, "hyena_y_done"))

            def attend(layer):
                us = attention_units(layer)
                n = len(us)
                first_pv = pv_count[0]
                for i in range(n + 3):
                    if i < n:
                        u = us[i]
                        if i >= 2:
                            pe.wait_ge(sem("probs_scaled_exp"), nth(pe, "probs_scaled_exp"))
                        if u["kind"] == "plain":
                            last = mm(bank(i % 2)[:, 0:u["keys"]], u["q"], u["k"], True, True)
                        else:
                            mm(bank(i % 2)[:, 0:S], u["q"], u["k"][:, 0:S], True, True)
                            last = mm(bank(6 + i % 2)[:, 0:S], u["q"], u["k"][:, S:512], True, True)
                        last.then_inc(sem("scores_ready"), 1)
                    if 2 <= i < n + 2:
                        u = us[i - 2]
                        pe.wait_ge(sem("probs_ready"), nth(pe, "probs_ready"))
                        for c in range(u["keys"] // P):
                            last = nc.tensor.transpose(bank(2 + i % 2)[:, c * P:(c + 1) * P],
                                                       probs(i - 2)[:, c * P:(c + 1) * P], K(K_ID))
                        last.then_inc(sem("probs_turned"), 1)
                    if i >= 3:
                        j = i - 3
                        u = us[j]
                        pe.wait_ge(sem("probsT_ready"), nth(pe, "probsT_ready"))
                        if j >= 2:
                            pe.wait_ge(sem("o_gated"), nth(pe, "o_gated"))
                        o = bank(4 + j % 2)[u["half"] * 64:u["half"] * 64 + 64, 0:P]
                        nch = u["keys"] // P
                        for c in range(nch):
                            last = mm(o, u["v"](c), probsT(j)[:, c * P:(c + 1) * P], c == 0, c == nch - 1)
                        last.then_inc(sem("o_ready"), 1)
                pe.wait_ge(sem("o_gated"), nth(pe, "o_gated", 2))
                nth(pe, "probs_scaled_exp", 2)

            def out2(layer):
                n = 512 if layer == 0 else S
                pe.wait_ge(sem("y2_ready"), nth(pe, "y2_ready"))
                for j in range(OUTP):
                    q = take()
                    for m in range(2):
                        for k in range(KD):
                            last = mm(bank(2 * j + m)[:, 0:n], slot(q, k * 256 + m * P, k * 256 + (m + 1) * P),
                                      y3[:, k, 0:n], k == 0, k == KD - 1)
                    last.then_inc(DONE, 1)

            pv_count = [0]
            hyena_filters()
            for layer in range(2):
                adaln()
                norm(2)
                project2(layer)
                qk_norm(layer)
                if layer == 0:
                    hyena()
                attend(layer)
                out2(layer)

        @block.scalar
        def _(act):
            chain = [0]

            def step(ins):
                chain[0] += 1
                ins.then_inc(sem("scalar_steps"), 1)
                act.wait_ge(sem("scalar_steps"), chain[0])

            def f(o, i, fn, **kw):
                return nc.scalar.activation(o, i, fn, **kw)

            panel = [0]

            def multiplied(k):
                panel[0] += k
                act.wait_ge(DONE, panel[0])

            def norm(first=False, streams=1):
                if first:
                    act.wait_ge(sem("inputs_landed"), 48)
                else:
                    act.wait_ge(sem("x_done"), nth(act, "x_done"))
                if streams == 2:
                    act.wait_ge(sem("context_landed"), 16)
                    step(f(h3[:, :, 0:S], x3, ACT.Square))
                    f(h3[:, :, S:512], c3, ACT.Square).then_inc(sem("squares_ready"), 1)
                else:
                    f(h3[:, :, 0:S], x3, ACT.Square).then_inc(sem("squares_ready"), 1)
                act.wait_ge(sem("mean_square_ready"), nth(act, "mean_square_ready"))
                n = streams * S
                f(rstd[:, 0:n], bank(0)[:, 0:n], ACT.Sqrt, bias=eps1).then_inc(sem("root_ready"), 1)

            def project1():
                for p in range(0, IN1, 2):
                    multiplied(1)
                    o = proj[:, p * 512:(p + 1) * 512]
                    f(o, bank(p % 8), ACT.Copy, scale=0.125 if p * 2 in (SQ, SQ + 2) else 1.0) \
                        .then_inc(sem("proj_even_copied"), 1)
                    panel[0] += 1

            def hgrn(layer):
                q, kk = arena[:, 0:1024], arena[:, 1024:2048]
                e0 = arena[:, 3072:4096]
                E = [e0, arena[:, 4096:5120]]
                act.wait_ge(sem("proj_even_copied"), 11 * (layer + 1))
                act.wait_ge(sem("proj_odd_copied"), 11 * (layer + 1))
                step(f(q, proj[:, HQ * S:(HQ + 4) * S], ACT.Silu))
                f(proj[:, HOG * S:(HOG + 4) * S], proj[:, HOG * S:(HOG + 4) * S], ACT.Silu) \
                    .then_inc(sem("q_silu_ready"), 1)
                f(proj[:, GA * S:(GA + 16) * S], proj[:, GA * S:(GA + 16) * S], ACT.Sigmoid) \
                    .then_inc(sem("gates_ready"), 1)
                act.wait_ge(sem("forget_abs_ready"), nth(act, "forget_abs_ready"))
                step(f(e0, e0, ACT.Exp))
                if layer == 1:
                    step(f(lbs[:, 4:8], lbs[:, 4:8], ACT.Exp))
                    step(f(lbs[:, 4:8], lbs[:, 4:8], ACT.Ln, bias=ones1))
                f(e0, e0, ACT.Ln, bias=ones1).then_inc(sem("forget_log_ready"), 1)
                act.wait_ge(sem("key_exponent_ready"), nth(act, "key_exponent_ready"))
                f(kk, e0, ACT.Exp).then_inc(sem("hgrn_key_ready"), 1)
                if layer == 1:
                    act.wait_ge(sem("forget_abs_ready"), nth(act, "forget_abs_ready"))
                    step(f(e0, e0, ACT.Exp))
                    f(e0, e0, ACT.Ln, bias=ones1).then_inc(sem("forget_log_ready"), 1)
                for lv in range(8):
                    act.wait_ge(sem("level_exponent_ready"), nth(act, "level_exponent_ready"))
                    v = E[lv % 2].rearrange("p (n two b) -> p n two b", two=2, b=1 << lv)
                    f(v[:, :, 1, :], v[:, :, 1, :], ACT.Exp)
                    f(v[:, :, 0, :], v[:, :, 0, :], ACT.Exp, scale=-1.0).then_inc(sem("level_decay_ready"), 1)
                act.wait_ge(sem("level_scores_ready"), nth(act, "level_scores_ready", 9))
                f(arena[:, 8192:8704], bank(4), ACT.Copy).then_inc(sem("cross_copied"), 1)
                act.wait_ge(sem("hgrn_o_ready"), nth(act, "hgrn_o_ready"))
                f(e0, bank(5, 2), ACT.Square).then_inc(sem("hgrn_o_squared"), 1)
                act.wait_ge(sem("hgrn_mean_square_ready"), nth(act, "hgrn_mean_square_ready"))
                f(E[1][:, 0:512], bank(4), ACT.Sqrt, bias=eps1)
                f(E[1][:, 512:1024], bank(7), ACT.Sqrt, bias=eps1).then_inc(sem("hgrn_root_ready"), 1)

            def stick():
                for g in range(2):
                    L = arena[:, g * 3072:g * 3072 + 1536]
                    W = arena[:, g * 3072 + 1536:(g + 1) * 3072]
                    act.wait_ge(sem("stick_z_ready"), nth(act, "stick_z_ready"))
                    step(f(L.rearrange("p (h t) -> p h t", h=4), ps[:, 0:4, 0:384], ACT.Abs))
                    step(f(L, L, ACT.Exp, scale=-1.0))
                    f(L, L, ACT.Ln, bias=ones1).then_inc(sem("stick_log_ready"), 1)
                    act.wait_ge(sem("stick_exponent_ready"), nth(act, "stick_exponent_ready"))
                    f(W, W, ACT.Exp).then_inc(sem("stick_exp_ready"), 1)
                    act.wait_ge(sem("stick_o_ready"), nth(act, "stick_o_ready"))
                    for c in range(2):
                        ins = f(y3[:, 4 + 2 * g + c, 0:S], bank(4 + g)[:, c * S:(c + 1) * S], ACT.Copy)
                        if c == 0:
                            step(ins)
                    ins.then_inc(sem("o_b_ready"), 1)

            def ffn(p0, e=0):
                sg = [arena[:, 0:512], arena[:, 512:1024]]

                def silu(p, f_, more):
                    act.wait_ge(DONE, more + (p + 1))
                    f(sg[f_ % 2], bank(f_ % 2), ACT.Silu).then_inc(sem("gate_silu_ready"), 1)

                silu(p0, 0, e * FFN)
                with act.Fori(0, FSTEP // 2 - 1) as i:
                    silu(p0 + 2, 1, e * FFN + i * 6)
                    silu(p0 + 5, 0, e * FFN + i * 6)
                silu(p0 + 38, 1, e * FFN)

            def compact_expert(p0, e):
                sg = [arena[:, 0:256], arena[:, 512:768]]
                hT2 = [arena[:, 1280:1536], arena[:, 1792:2048]]

                def silu(p, f_, more):
                    act.wait_ge(DONE, more + (p + 1))
                    f(sg[f_ % 2], bank(f_ % 2)[:, 0:S], ACT.Silu).then_inc(sem("c_gate_silu_ready"), 1)

                def copy(f_, count):
                    act.wait_ge(sem("c_hidden_turned"), count)
                    f(hT2[f_ % 2], bank(6)[:, 0:S], ACT.Copy).then_inc(sem("c_hidden_copied"), 1)

                act.wait_ge(sem("tokens_gathered"), e + 1)
                f(xeT[:, 0:512], bank(2), ACT.Copy).then_inc(sem("tokens_copied"), 1)
                silu(p0, 0, e * FFN)
                with act.Fori(0, FSTEP // 2 - 1) as i:
                    silu(p0 + 2, 1, e * FFN + i * 6)
                    copy(0, e * FSTEP + i * 2 + 1)
                    silu(p0 + 5, 0, e * FFN + i * 6)
                    copy(1, e * FSTEP + i * 2 + 2)
                silu(p0 + 38, 1, e * FFN)
                copy(0, e * FSTEP + (FSTEP - 1))
                copy(1, e * FSTEP + FSTEP)
                act.wait_ge(DONE, e * FFN + (p0 + FFN))
                f(yS, bank(4, 2), ACT.Copy).then_inc(sem("rows_copied"), 1)

            for layer in range(2):
                norm(first=layer == 0)
                project1()
                hgrn(layer)
                stick()
                panel[0] += 2 * OUTP
                norm()
                if layer == 0:
                    ffn(panel[0])
                    panel[0] += FFN
                else:
                    act.wait_ge(sem("router_max_ready"), nth(act, "router_max_ready"))
                    for tb in range(2):
                        ins = f(rt[:, 16 + 8 * tb:24 + 8 * tb], rt[:, 8 * tb:8 * tb + 8], ACT.Exp,
                                bias=rt[:, 34 + tb:35 + tb])
                        if tb == 0:
                            step(ins)
                    ins.then_inc(sem("router_exp_ready"), 1)
                    act.dma_start(proj[0:64, 0:2048], w3_in).then_inc(sem("filter_tables_landed"), 16)
                    act.dma_start(proj[0:33, 2048:2304], pos_in).then_inc(sem("filter_tables_landed"), 16)
                    act.dma_start(proj[0:33, 2816:2880], w1_in).then_inc(sem("filter_tables_landed"), 16)
                    act.dma_start(proj[0:64, 2880:2944], w2_in).then_inc(sem("filter_tables_landed"), 16)
                    act.dma_start(proj[:, 8192:9216], decay_in).then_inc(sem("filter_tables_landed"), 16)
                    act.dma_start(proj[:, 11776:12800], skip_in.partition_broadcast(P)) \
                       .then_inc(sem("filter_tables_landed"), 16)
                    act.wait_ge(sem("h_turned"), nth(act, "h_turned"))
                    f(hN, bank(0, 4), ACT.Copy).then_inc(sem("h_tokens_copied"), 1)
                    act.wait_ge(sem("slot_weights_ready"), nth(act, "slot_weights_ready"))
                    f(G[:, S:], bank(4, 4), ACT.Copy).then_inc(sem("slot_weights_copied"), 1)
                    act.wait_ge(sem("crowded_ready"), nth(act, "crowded_ready"))
                    many = act.value_load(crowded[0:1, 0:1], min_val=0, max_val=1)
                    with act.If(many == 1):
                        with act.Fori(0, E) as e:
                            ffn(panel[0], e)
                    with act.Else():
                        with act.Fori(0, E) as e:
                            compact_expert(panel[0], e)
                    panel[0] += E * FFN
            norm()

            act.wait_ge(sem("combine_free"), nth(act, "combine_free"))
            act.dma_start(arena[:, 4096:6144], dft_in).then_inc(sem("filter_tables_landed"), 16)
            f(cond[:, :], sml[:, S_COND:S_COND + 16], ACT.Silu).then_inc(sem("cond_ready"), 1)

            def hyena_filters():
                for _ in range(2):
                    act.wait_ge(sem("filter_phase_ready"), nth(act, "filter_phase_ready"))
                    src = proj[0:64, 2944:3200]
                    dst = proj[0:64, 2304:2560] if _ == 0 else proj[0:64, 2560:2816]
                    f(dst, src, ACT.Sin).then_inc(sem("filter_hidden_ready"), 1)
                for o in range(2):
                    act.wait_ge(sem("taps_ready"), nth(act, "taps_ready"))
                    f(proj[:, 9216:11264], proj[:, 4096:6144], ACT.Square).then_inc(sem("taps_squared"), 1)
                    act.wait_ge(sem("taps_energy_ready"), nth(act, "taps_energy_ready"))
                    f(proj[:, 11264:11776], bank(4), ACT.Sqrt, bias=eps1).then_inc(sem("taps_root_ready"), 1)

            def project2(layer):
                for p in range(IN2):
                    multiplied(1)
                    b = 2 * (p % 4)
                    wide = layer == 0 or p in (2, 5, 6, 7, 8)
                    o = proj[:, 2 * p * 512:(2 * p + 2) * 512]
                    i = bank(b, 2)
                    if not wide:
                        o = o.rearrange("q (a n) -> q a n", a=2)[:, :, 0:S]
                        i = i.rearrange("q (a n) -> q a n", a=2)[:, :, 0:S]
                    f(o, i, ACT.Copy).then_inc(sem("pair_copied"), 1)

            def qk_norm(layer):
                act.wait_ge(sem("pair_copied"), IN2 * (layer + 1))
                chunks = qk_chunks(layer)

                def square(i):
                    c, n = chunks[i][0:2]
                    f(arena[:, 6144 + (i % 2) * 512:][:, 0:n], proj[:, c * 512:c * 512 + n], ACT.Square) \
                        .then_inc(sem("qk_squared"), 1)

                square(0)
                square(1)
                for i, (c, n, g, rope) in enumerate(chunks):
                    if i >= 2:
                        act.wait_ge(sem("qk_normed"), nth(act, "qk_normed"))
                    act.wait_ge(sem("qk_mean_square"), nth(act, "qk_mean_square"))
                    f(qk_root(i)[:, 0:n], bank(i % 2)[:, 0:n], ACT.Sqrt, bias=eps1).then_inc(sem("qk_root_ready"), 1)
                    if i + 2 < len(chunks):
                        square(i + 2)
                act.wait_ge(sem("qk_normed"), nth(act, "qk_normed", 2))
                gates = proj[:, C_G * 512:(C_G + 8) * 512]
                f(gates, gates, ACT.Silu).then_inc(sem("y_gates_ready"), 1)

            def hyena():
                nat = proj[:, (C_HU + 4) * 512:(C_HU + 12) * 512]
                for j in range(8):
                    act.wait_ge(sem("natural_ready"), nth(act, "natural_ready"))
                    f(nat[:, j * 512:(j + 1) * 512], bank(j % 2), ACT.Copy).then_inc(sem("natural_copied"), 1)

            def attend(layer):
                us = attention_units(layer)
                n = len(us)

                def turned_copy(j):
                    act.wait_ge(sem("probs_turned"), nth(act, "probs_turned"))
                    if j >= 2:
                        act.wait_ge(sem("o_ready"), nth(act, "o_ready"))
                    kk = us[j]["keys"]
                    f(probsT(j)[:, 0:kk], bank(2 + j % 2)[:, 0:kk], ACT.Copy).then_inc(sem("probsT_ready"), 1)

                for i in range(n + 2):
                    if i < n:
                        u = us[i]
                        pr = probs(i)
                        acc = stat[:, 8 + i % 4:9 + i % 4]
                        nm = stat[:, 4 + i % 4:5 + i % 4]
                        if u["kind"] != "plain":
                            act.wait_ge(sem("scores_ready"), nth(act, "scores_ready"))
                            if i >= 2:
                                act.wait_ge(sem("probs_scaled_exp"), exps[0] - 1)
                            f(scores_sb(i)[:, S:512], bank(6 + i % 2)[:, 0:S], ACT.Copy, scale=0.125) \
                                .then_inc(sem("context_scores_ready"), 1)
                            if i >= 2:
                                turned_copy(i - 2)
                            act.wait_ge(sem("max_ready"), nth(act, "max_ready"))
                            w = 513 if u["kind"] == "window" else 512
                            f(pr[:, 0:w], scores_sb(i)[:, 0:w], ACT.Exp, bias=nm, accum_out=acc) \
                                .then_inc(sem("probs_scaled_exp"), 1)
                        else:
                            nth(act, "scores_ready")
                            act.wait_ge(sem("max_ready"), nth(act, "max_ready"))
                            f(pr[:, 0:u["keys"]], bank(i % 2)[:, 0:u["keys"]], ACT.Exp, bias=nm, scale=0.125,
                              accum_out=acc).then_inc(sem("probs_scaled_exp"), 1)
                            if i >= 2:
                                turned_copy(i - 2)
                        exps[0] += 1
                    else:
                        turned_copy(i - 2)
                act.wait_ge(sem("o_ready"), nth(act, "o_ready", 2))

            exps = [0]
            hyena_filters()
            for layer in range(2):
                panel[0] += ADA
                if layer == 1:
                    act.wait_ge(sem("y2_ready"), nth(act, "y2_ready"))
                    for h in range(8):
                        for r in range(4):
                            src = bass.AP(rpb_in.tensor, h * 465 + (7 - r) * 31 + 15 - 63, [[1, 64], [31, 4], [1, 64]])
                            dst = arena[(r % 2) * 64:(r % 2) * 64 + 64, (h * 2 + r // 2) * S:(h * 2 + r // 2 + 1) * S]
                            act.dma_start(dst.rearrange("p (a b) -> p a b", a=4), src) \
                               .then_inc(sem("position_bias_landed"), 16)
                act.wait_ge(DONE, panel[0])
                f(arena[0:2, 6144:9216], ps[0:2, 1:7, :].rearrange("p b n -> p (b n)"), ACT.Copy) \
                    .then_inc(sem("ada_rows_copied"), 1)
                norm(streams=2)
                project2(layer)
                qk_norm(layer)
                if layer == 0:
                    hyena()
                attend(layer)
                panel[0] += OUTP
            act.wait_ge(sem("x_done"), nth(act, "x_done", 1))
            act.dma_start(out, xT[:, :]).then_inc(sem("out_stored"), 16)
            act.wait_ge(sem("out_stored"), 16)

        @block.gpsimd
        def _(pool):
            pool.memset(zrow[:, :], 0.0).then_inc(sem("accumulators_free"), 1)
            for layer in range(2):
                k = arena[:, 1024:2048]
                for lv in range(8):
                    pool.wait_ge(sem("level_decay_ready"), nth(pool, "level_decay_ready"))
                    if lv == 0:
                        pool.wait_ge(sem("hgrn_key_ready"), nth(pool, "hgrn_key_ready"))
                    if lv >= 2:
                        pool.wait_ge(sem("level_scores_ready"), nth(pool, "level_scores_ready", 2 if lv == 2 else 1))
                    E = arena[:, 3072 + (lv % 2) * 1024:][:, 0:1024]
                    X = arena[:, 5120 + (lv % 2) * 1024:][:, 0:1024]
                    v = lambda a: a.rearrange("p (n two b) -> p n two b", two=2, b=1 << lv)[:, :, 0, :]
                    pool.tensor_tensor(v(X), v(k), v(E), ALU.mult).then_inc(sem("level_k_ready"), 1)
                seen[(pool.engine, "level_scores_ready")] += 2
            for o in range(2):
                pool.wait_ge(sem("taps_ready"), nth(pool, "taps_ready"))
                if o:
                    pool.wait_ge(sem("spectrum_sum"), nth(pool, "spectrum_sum"))
                a = proj[:, 4096:6144].rearrange("p (tb d n) -> p tb d n", tb=2, d=2)
                hp = proj[:, 6144:7168].rearrange("p (tb n) -> p tb n", tb=2)
                hm = proj[:, 7168:8192].rearrange("p (tb n) -> p tb n", tb=2)
                pool.tensor_tensor(hp, a[:, :, 0, :], a[:, :, 1, :], ALU.add)
                pool.tensor_tensor(hm, a[:, :, 0, :], a[:, :, 1, :], ALU.subtract).then_inc(sem("taps_combined"), 1)

        @block.vector
        def _(dve):
            chain = [0]

            def step(ins):
                chain[0] += 1
                ins.then_inc(sem("vector_steps"), 1)
                dve.wait_ge(sem("vector_steps"), chain[0])

            V = nc.vector
            panel = [0]

            def multiplied(k):
                panel[0] += k
                dve.wait_ge(DONE, panel[0])

            def signal(ins, name):
                ins.then_inc(sem(name), 1)
                made[name] = made.get(name, 0) + 1
                dve.wait_ge(sem(name), made[name])

            made = {}

            def announce(name):
                dve.sem_inc(sem(name), 1)
                made[name] = made.get(name, 0) + 1

            def norm(col, out3=None, name="h_ready"):
                dve.wait_ge(sem("root_ready"), nth(dve, "root_ready"))
                step(V.reciprocal(rstd[:, 0:S], rstd[:, 0:S]))
                for k in range(KD):
                    o = h3[:, k, 0:S] if out3 is None else out3[:, k, :]
                    ins = V.scalar_tensor_tensor(o, x3[:, k, :], sml[:, col + k:col + k + 1], rstd[:, 0:S],
                                                 ALU.mult, ALU.mult)
                    if out3 is None:
                        signal(ins, name)
                    elif k < KD - 1:
                        step(ins)
                    else:
                        signal(ins, name)

            def project1():
                for p in range(1, IN1, 2):
                    multiplied(2)
                    o = proj[:, p * 512:(p + 1) * 512]
                    V.tensor_scalar(o, bank(p % 8), 0.125 if p * 2 in (SQ, SQ + 2) else 1.0, None, ALU.mult) \
                        .then_inc(sem("proj_odd_copied"), 1)

            def hgrn(layer):
                q, kk, b = arena[:, 0:1024], arena[:, 1024:2048], arena[:, 2048:3072]
                e0, lf = arena[:, 3072:4096], arena[:, 4096:5120]
                E = [e0, lf]
                sc, cross = arena[:, 7168:8192], arena[:, 8192:8704]
                z = proj[:, HF * S:(HF + 4) * S]
                heads = lambda a: a.rearrange("p (h t) -> p h t", h=4)
                dve.wait_ge(sem("proj_even_copied"), 11 * (layer + 1))
                dve.wait_ge(sem("proj_odd_copied"), 11 * (layer + 1))
                if layer == 1:
                    step(V.tensor_tensor(lbs[:, 0:4], sml[:, S_LB + 4:S_LB + 8], sml[:, S_LB:S_LB + 4], ALU.subtract))
                    step(V.scalar_tensor_tensor(lbs[:, 4:8], lbs[:, 0:4], -1.0, lbs[:, 0:4], ALU.mult, ALU.min))
                signal(V.scalar_tensor_tensor(e0, z, -1.0, z, ALU.mult, ALU.min), "forget_abs_ready")
                step(V.memset(sc, 0.0))
                dve.wait_ge(sem("forget_log_ready"), nth(dve, "forget_log_ready"))
                step(V.scalar_tensor_tensor(lf, z, 0.0, e0, ALU.min, ALU.subtract))
                if layer == 0:
                    signal(V.tensor_tensor(e0, lf, z, ALU.subtract), "key_exponent_ready")
                else:
                    step(V.scalar_tensor_tensor(lbs[:, 8:12], lbs[:, 0:4], 0.0, lbs[:, 4:8], ALU.min, ALU.subtract))
                    step(V.tensor_tensor(lbs[:, 12:16], lbs[:, 8:12], lbs[:, 0:4], ALU.subtract))
                    rest = lbs[:, 12:16].unsqueeze(2).to_broadcast([P, 4, S])
                    step(V.tensor_tensor(e0, lf, z, ALU.subtract))
                    signal(V.tensor_tensor(heads(e0), heads(e0), rest, ALU.add), "key_exponent_ready")
                    less = lbs[:, 0:4].unsqueeze(2).to_broadcast([P, 4, S])
                    step(V.tensor_tensor(heads(lf), heads(lf), less, ALU.subtract))
                    dve.wait_ge(sem("hgrn_key_ready"), nth(dve, "hgrn_key_ready"))
                    signal(V.scalar_tensor_tensor(e0, lf, -1.0, lf, ALU.mult, ALU.min), "forget_abs_ready")
                    dve.wait_ge(sem("forget_log_ready"), nth(dve, "forget_log_ready"))
                    step(V.scalar_tensor_tensor(lf, lf, 0.0, e0, ALU.max, ALU.add))
                    log_lb = lbs[:, 8:12].unsqueeze(2).to_broadcast([P, 4, S])
                    step(V.tensor_tensor(heads(lf), heads(lf), log_lb, ALU.add))
                for h in range(4):
                    step(V.tensor_tensor_scan(b[:, h * S:(h + 1) * S], ones1.to_broadcast([P, S]),
                                              lf[:, h * S:(h + 1) * S], 0.0, ALU.mult, ALU.add))
                if layer == 0:
                    dve.wait_ge(sem("hgrn_key_ready"), nth(dve, "hgrn_key_ready"))
                dve.wait_ge(sem("q_silu_ready"), nth(dve, "q_silu_ready"))
                announce("hgrn_qk_ready")

                def merge(lv):
                    dve.wait_ge(sem("level_scores_ready"), nth(dve, "level_scores_ready"))
                    if lv == 7:
                        return
                    m = K(K_ID) if lv < 0 else K(K_LEV + lv * P)
                    m = m.bitcast(I32).unsqueeze(1).to_broadcast([P, 8, P])
                    i = bank(0 if lv % 2 else 2, 2).rearrange("p (h t) -> p h t", h=8)
                    signal(V.copy_predicated(sc.rearrange("p (h t) -> p h t", h=8), m, i), "level_merged")

                for lv in range(8):
                    B = 1 << lv
                    if lv >= 2:
                        dve.wait_ge(sem("level_k_ready"), nth(dve, "level_k_ready"))
                    v = lambda a: a.rearrange("p (n m) -> p n m", m=2 * B)
                    signal(V.tensor_tensor(v(E[lv % 2]), v(b), v(b)[:, :, B - 1:B].to_broadcast([P, 512 // B, 2 * B]),
                                           ALU.subtract), "level_exponent_ready")
                    if lv >= 1:
                        merge(lv - 2)
                    dve.wait_ge(sem("level_decay_ready"), nth(dve, "level_decay_ready"))
                    w = lambda a: a.rearrange("p (n two b) -> p n two b", two=2, b=B)[:, :, 1, :]
                    X = arena[:, 5120 + (lv % 2) * 1024:][:, 0:1024]
                    signal(V.tensor_tensor(w(X), w(q), w(E[lv % 2]), ALU.mult), "level_q_ready")
                seen[(dve.engine, "level_k_ready")] += 2
                merge(6)
                merge(7)
                dve.wait_ge(sem("cross_copied"), nth(dve, "cross_copied"))
                announce("hgrn_scores_merged")
                dve.wait_ge(sem("hgrn_root_ready"), nth(dve, "hgrn_root_ready"))
                step(V.reciprocal(lf, lf))
                for j in range(2):
                    t = arena[:, 2048 + j * 512:2048 + (j + 1) * 512]
                    step(V.scalar_tensor_tensor(t, bank(5 + j), sml[:, S_ON + layer:S_ON + layer + 1],
                                                lf[:, j * 512:(j + 1) * 512],
                                                ALU.mult, ALU.mult))
                    g = proj[:, HOG * S + j * 512:HOG * S + (j + 1) * 512]
                    ins = V.tensor_tensor(y3[:, 2 * j:2 * j + 2, 0:S], t.rearrange("p (a n) -> p a n", a=2),
                                          g.rearrange("p (a n) -> p a n", a=2), ALU.mult)
                    if j == 0:
                        step(ins)
                    else:
                        signal(ins, "o_a_ready")
                announce("hgrn_done")

            def stick():
                strict = K(K_STRICT).unsqueeze(1).to_broadcast([P, 4, P])
                for g in range(2):
                    L = arena[:, g * 3072:g * 3072 + 1536]
                    W = arena[:, g * 3072 + 1536:(g + 1) * 3072]
                    v = lambda a: a.rearrange("p (h t) -> p h t", h=4)
                    z = ps[:, 0:4, 0:384]
                    dve.wait_ge(sem("stick_log_ready"), nth(dve, "stick_log_ready"))
                    step(V.scalar_tensor_tensor(v(L), z, 0.0, v(L), ALU.max, ALU.add))
                    step(V.tensor_tensor(v(L)[:, :, 0:P], v(L)[:, :, 0:P], strict, ALU.mult))
                    signal(V.tensor_tensor(v(L)[:, :, S:384], v(L)[:, :, S:384], strict, ALU.mult),
                           "stick_softplus_ready")
                    dve.wait_ge(sem("stick_sums_ready"), nth(dve, "stick_sums_ready"))
                    signal(V.tensor_scalar(v(W), z, 0.0, None, ALU.min), "stick_exponent_ready")
                    dve.wait_ge(sem("stick_exp_ready"), nth(dve, "stick_exp_ready"))
                    step(V.tensor_tensor(v(W)[:, :, 0:P], v(W)[:, :, 0:P], strict, ALU.mult))
                    signal(V.tensor_tensor(v(W)[:, :, S:384], v(W)[:, :, S:384], strict, ALU.mult),
                           "stick_weights_ready")

            def mix_out():
                dve.wait_ge(sem("gates_ready"), nth(dve, "gates_ready"))
                for j in range(2):
                    multiplied(2)
                    ga = proj[:, GA * S + j * 1024:GA * S + (j + 1) * 1024]
                    gb = proj[:, GB * S + j * 1024:GB * S + (j + 1) * 1024]
                    step(V.tensor_tensor(ga, ga, bank(4 * j, 2), ALU.mult))
                    step(V.tensor_tensor(gb, gb, bank(4 * j + 2, 2), ALU.mult))
                    v = lambda a: a.rearrange("p (k n) -> p k n", k=4)
                    signal(V.tensor_tensor(h3[:, 4 * j:4 * j + 4, 0:S], v(ga), v(gb), ALU.add), "mixed_ready")
                for j in range(OUTP):
                    multiplied(1)
                    o = xT[:, j * 512:(j + 1) * 512]
                    ins = V.tensor_tensor(o, o, bank(j), ALU.add)
                    if j < OUTP - 1:
                        step(ins)
                    else:
                        signal(ins, "x_done")

            def ffn(p0, e=0):
                sg = [arena[:, 0:512], arena[:, 512:1024]]
                hb = [arena[:, 1024:1536], arena[:, 1536:2048]]

                def gated(p, f, more, count):
                    dve.wait_ge(DONE, more + (p + 2))
                    dve.wait_ge(sem("gate_silu_ready"), count)
                    V.tensor_tensor(hb[f % 2], sg[f % 2], bank(2 + f % 2), ALU.mult).then_inc(sem("hidden_ready"), 1)

                h0 = hid[0]
                gated(p0, 0, e * FFN, e * FSTEP + (h0 + 1))
                with dve.Fori(0, FSTEP // 2 - 1) as i:
                    gated(p0 + 2, 1, e * FFN + i * 6, e * FSTEP + i * 2 + (h0 + 2))
                    gated(p0 + 5, 0, e * FFN + i * 6, e * FSTEP + i * 2 + (h0 + 3))
                gated(p0 + 38, 1, e * FFN, e * FSTEP + (h0 + FSTEP))
                dve.wait_ge(DONE, e * FFN + (p0 + FFN))

            hid = [0]
            dve.wait_ge(sem("inputs_landed"), 48)
            for layer in range(2):
                norm(S_MIX + layer * KD)
                project1()
                hgrn(layer)
                stick()
                mix_out()
                norm(S_FFN + layer * KD)
                if layer == 0:
                    ffn(panel[0])
                    panel[0] += FFN
                    hid[0] += FSTEP
                    for j in range(4):
                        o = xT[:, j * 512:(j + 1) * 512]
                        ins = V.tensor_tensor(o, o, bank(4 + j), ALU.add)
                        if j < 3:
                            step(ins)
                        else:
                            signal(ins, "x_done")
                    made["accumulators_free"] = 1
                    announce("accumulators_free")

            L = rt[:, 0:16]
            dve.wait_ge(sem("logits_ready"), nth(dve, "logits_ready"))
            signal(V.tensor_copy(L, bank(1)[:, 0:16]), "logits_copied")
            L3 = L.rearrange("p (t e) -> p t e", t=2)
            step(V.tensor_reduce(rt[:, 32:34], L3, AX.X, ALU.max))
            signal(V.tensor_scalar(rt[:, 34:36], rt[:, 32:34], -1.0, None, ALU.mult), "router_max_ready")
            for tb in range(2):
                l = rt[:, 8 * tb:8 * tb + 8]
                other = l.unsqueeze(1).to_broadcast([P, 8, 8])
                own = l.unsqueeze(2).to_broadcast([P, 8, 8])
                more = rt[:, 64:128].rearrange("p (a b) -> p a b", a=8)
                tie = rt[:, 128:192].rearrange("p (a b) -> p a b", a=8)
                low = K(K_LOW, 64).rearrange("p (a b) -> p a b", a=8)
                step(V.tensor_tensor(more, other, own, ALU.is_gt))
                step(V.tensor_tensor(tie, other, own, ALU.is_equal))
                step(V.tensor_tensor(tie, tie, low, ALU.mult))
                step(V.tensor_tensor(more, more, tie, ALU.add))
                step(V.tensor_reduce(rt[:, 40 + 8 * tb:48 + 8 * tb], more, AX.X, ALU.add))
            signal(V.tensor_scalar(rt[:, 40:56], rt[:, 40:56], 1.5, None, ALU.is_lt), "selected_ready")
            dve.wait_ge(sem("router_exp_ready"), nth(dve, "router_exp_ready"))
            step(V.tensor_tensor(rt[:, 16:32], rt[:, 16:32], rt[:, 40:56], ALU.mult))
            step(V.tensor_reduce(rt[:, 36:38], rt[:, 16:32].rearrange("p (t e) -> p t e", t=2), AX.X, ALU.add))
            step(V.reciprocal(rt[:, 38:40], rt[:, 36:38]))
            step(V.tensor_tensor(rt[:, 200:216].rearrange("p (t e) -> p t e", t=2),
                                 rt[:, 16:32].rearrange("p (t e) -> p t e", t=2),
                                 rt[:, 38:40].unsqueeze(2).to_broadcast([P, 2, 8]), ALU.mult))
            dve.wait_ge(sem("places_ready"), nth(dve, "places_ready"))
            step(V.tensor_copy(rt[:, 216:240], bank(7)[:, 0:24]))
            dg = arena[:, 4096:6144].rearrange("p (e t n) -> p e t n", e=8, t=2)
            for tb in range(2):
                ins = V.tensor_tensor(dg[:, :, tb, :], K(K_ID).unsqueeze(1).to_broadcast([P, 8, P]),
                                      rt[:, 200 + 8 * tb:208 + 8 * tb].unsqueeze(2).to_broadcast([P, 8, P]), ALU.mult)
                if tb == 0:
                    step(ins)
            signal(ins, "combine_diagonals_ready")
            comb = arena[:, 2048:4096]
            dve.wait_ge(sem("combine_ready"), nth(dve, "combine_ready"))
            step(V.tensor_copy(comb, bank(4, 4)))
            place, sel, total = rt[:, 216:232], rt[:, 40:56], rt[:, 232:240]
            step(V.tensor_scalar(place, place, 1.0, None, ALU.add))
            step(V.tensor_tensor(place, place, sel, ALU.mult))
            step(V.tensor_scalar(place, place, -1.0, None, ALU.add))
            step(V.tensor_reduce(rt[:, 240:241], total, AX.X, ALU.max))
            signal(V.tensor_scalar(crowded[0:1, 0:1], rt[0:1, 240:241], float(SLOTS), None, ALU.is_gt),
                   "crowded_ready")
            sel4 = SEL.rearrange("p (e t n) -> p e t n", e=8, t=2)
            selw4 = SELW.rearrange("p (e t n) -> p e t n", e=8, t=2)
            for tb in range(2):
                step(V.tensor_tensor(sel4[:, :, tb, :], K(K_IOTA).unsqueeze(1).to_broadcast([P, 8, P]),
                                     place[:, 8 * tb:8 * tb + 8].unsqueeze(2).to_broadcast([P, 8, P]), ALU.is_equal))
                step(V.tensor_tensor(selw4[:, :, tb, :], sel4[:, :, tb, :],
                                     rt[:, 200 + 8 * tb:208 + 8 * tb].unsqueeze(2).to_broadcast([P, 8, P]), ALU.mult))
            announce("weighted_selection_ready")
            step(V.memset(G[:, 0:S], 0.0))
            signal(V.memset(yS, 0.0), "rows_copied")
            announce("accumulators_free")

            def compact_expert(p0, e):
                sg = [arena[:, 0:256], arena[:, 512:768]]
                hd = [arena[:, 1024:1280], arena[:, 1536:1792]]

                def gated(p, f, more, count):
                    dve.wait_ge(DONE, more + (p + 2))
                    dve.wait_ge(sem("c_gate_silu_ready"), count)
                    V.tensor_tensor(hd[f % 2], sg[f % 2], bank(2 + f % 2)[:, 0:S], ALU.mult) \
                        .then_inc(sem("c_hidden_ready"), 1)

                dve.wait_ge(sem("tokens_gathered"), e + 1)
                V.tensor_copy(xeT[:, 512:1024], bank(3)).then_inc(sem("tokens_copied"), 1)
                add_rows(e * 4)
                gated(p0, 0, e * FFN, e * FSTEP + 1)
                with dve.Fori(0, FSTEP // 2 - 1) as i:
                    gated(p0 + 2, 1, e * FFN + i * 6, e * FSTEP + i * 2 + 2)
                    gated(p0 + 5, 0, e * FFN + i * 6, e * FSTEP + i * 2 + 3)
                gated(p0 + 38, 1, e * FFN, e * FSTEP + FSTEP)

            def add_rows(count):
                for j in range(4):
                    dve.wait_ge(sem("rows_spread"), count + (j + 1))
                    o = xT[:, j * 512:(j + 1) * 512]
                    V.tensor_tensor(o, o, bank(6 + j % 2), ALU.add).then_inc(sem("rows_added"), 1)
                dve.wait_ge(sem("rows_added"), count + 4)

            def dense_expert(e):
                ffn(panel[0], e)
                w = arena[:, bass.ds(e * S + 2048, S)].unsqueeze(1).to_broadcast([P, 2, S])
                for j in range(4):
                    i = bank(4 + j).rearrange("p (a n) -> p a n", a=2)
                    V.tensor_tensor(arena[:, 6144 + j * 512:6144 + (j + 1) * 512].rearrange("p (a n) -> p a n", a=2),
                                    i, w, ALU.mult).then_inc(sem("expert_weighed"), 1)
                dve.wait_ge(sem("expert_weighed"), e * 4 + 4)
                announce("accumulators_free")
                V.tensor_tensor(xT[:, :], xT[:, :], arena[:, 6144:8192], ALU.add).then_inc(sem("expert_added"), 1)
                dve.wait_ge(sem("expert_added"), e + 1)

            many = dve.value_load(crowded[0:1, 0:1], min_val=0, max_val=1)
            with dve.If(many == 1):
                with dve.Fori(0, E) as e:
                    dense_expert(e)
            with dve.Else():
                with dve.Fori(0, E) as e:
                    compact_expert(panel[0], e)
                add_rows(4 * E)
            panel[0] += E * FFN
            announce("combine_free")
            announce("x_done")
            norm(S_FIN, out3=x3, name="x_done")

            def hyena_filters():
                dve.wait_ge(sem("filter_tables_landed"), nth(dve, "filter_tables_landed", 16 * 7))
                arg = proj[0:64, 2944:3200]
                turn = proj[0:64, 3200:3456]
                for n in range(2):
                    dve.wait_ge(sem("filter_hidden_sum"), nth(dve, "filter_hidden_sum"))
                    step(V.tensor_scalar(arg, bank(1)[0:64, 0:S], sml[0:64, S_HYP + n:S_HYP + n + 1],
                                         sml[0:64, S_HYP + 2:S_HYP + 3], ALU.add, ALU.mult))
                    step(V.tensor_scalar(turn, arg, 1.0 / (2 * PI), None, ALU.mult))
                    step(V.tensor_scalar(turn, turn, 12582912.0, None, ALU.add))
                    step(V.tensor_scalar(turn, turn, 12582912.0, None, ALU.subtract))
                    for part in (6.28125, 0.0019350051879882812, 3.019916050561733e-07):
                        step(V.scalar_tensor_tensor(arg, turn, -part, arg, ALU.mult, ALU.add))
                    signal(V.tensor_scalar(arg, arg, 3.1415925, -3.1415925, ALU.min, ALU.max), "filter_phase_ready")
                for o in range(2):
                    dve.wait_ge(sem("filter_taps_sum"), nth(dve, "filter_taps_sum"))
                    for tb in range(2):
                        d = proj[:, 8192 + tb * 512:8192 + (tb + 1) * 512].unsqueeze(1).to_broadcast([P, 2, 512])
                        step(V.tensor_tensor(proj[:, 4096 + tb * 1024:4096 + (tb + 1) * 1024]
                                             .rearrange("p (d n) -> p d n", d=2), ps[:, 2 * tb:2 * tb + 2, :], d,
                                             ALU.mult))
                    signal(V.memset(proj[0:1, 4608:5120], 0.0), "taps_ready")
                    dve.wait_ge(sem("taps_root_ready"), nth(dve, "taps_root_ready"))
                    rn = proj[:, 11264:11776]
                    signal(V.reciprocal(rn, rn), "taps_rnorm_ready")
                    dve.wait_ge(sem("spectrum_sum"), nth(dve, "spectrum_sum"))
                    for m in range(2):
                        for cs in range(2):
                            t = arena[:, ((o * 2 + m) * 2 + cs) * 512:][:, 0:512]
                            step(V.tensor_tensor(t, bank(4 + 2 * m + cs), rn, ALU.mult))
                            if cs == 0:
                                step(V.tensor_tensor(t, t, proj[:, 11776 + o * 512:11776 + (o + 1) * 512], ALU.add))
                    announce("filter_spectrum_ready")

            def modulate(layer):
                dve.wait_ge(sem("context_landed"), 16)
                panel[0] += ADA
                dve.wait_ge(sem("ada_turned"), nth(dve, "ada_turned"))
                step(V.tensor_tensor(ada[:, :].rearrange("p (c s) -> p c s", s=2),
                                     bank(7)[:, 0:48].rearrange("p (c s) -> p c s", s=2),
                                     sml[:, S_ADA + 24 * layer:S_ADA + 24 * layer + 24].unsqueeze(2)
                                     .to_broadcast([P, 24, 2]), ALU.add))
                g = sml[:, S_NG + layer * KD:S_NG + (layer + 1) * KD].unsqueeze(2).to_broadcast([P, KD, 2])
                step(V.scalar_tensor_tensor(ada_a[:, :].rearrange("p (c s) -> p c s", s=2),
                                            ada[:, 16:32].rearrange("p (c s) -> p c s", s=2), 1.0, g,
                                            ALU.add, ALU.mult))
                dve.wait_ge(sem("root_ready"), nth(dve, "root_ready"))
                step(V.reciprocal(rstd[:, :], rstd[:, :]))
                for k in range(KD):
                    for s, src in enumerate((x3, c3)):
                        o = h3[:, k, s * S:(s + 1) * S]
                        step(V.scalar_tensor_tensor(o, src[:, k, :], ada_a[:, 2 * k + s:2 * k + s + 1],
                                                    rstd[:, s * S:(s + 1) * S], ALU.mult, ALU.mult))
                        signal(V.tensor_scalar(o, o, ada[:, 2 * k + s:2 * k + s + 1], None, ALU.add), "h_mod_ready")

            def qk_norm(layer):
                for i, (c, n, g, rope) in enumerate(qk_chunks(layer)):
                    dve.wait_ge(sem("qk_root_ready"), nth(dve, "qk_root_ready"))
                    r = qk_root(i)[:, 0:n]
                    q = proj[:, c * 512:c * 512 + n]
                    step(V.reciprocal(r, r))
                    signal(V.scalar_tensor_tensor(q, q, sml[:, S_QK + g:S_QK + g + 1], r, ALU.mult, ALU.mult),
                           "qk_normed")
                    if not rope:
                        continue
                    dve.wait_ge(sem("qk_swapped"), nth(dve, "qk_swapped"))
                    t = arena[:, 7168:7168 + S]
                    qx = proj[:, c * 512:c * 512 + S]
                    step(V.tensor_tensor(t, bank(2 + i % 2)[:, 0:S], K(K_SIN, S), ALU.mult))
                    step(V.tensor_tensor(qx, qx, K(K_COS, S), ALU.mult))
                    step(V.tensor_tensor(qx, qx, t, ALU.add))
                announce("qk_done")

            def hyena():
                dve.wait_ge(sem("y_gates_ready"), nth(dve, "y_gates_ready"))
                for j in range(12):
                    src = proj[:, (C_HU + j) * 512:(C_HU + j + 1) * 512].rearrange("p (s t) -> p s t", s=2)
                    dst = hT[:, j * 512:(j + 1) * 512] if j < 8 else proj[:, (C_HU + j - 8) * 512:(C_HU + j - 7) * 512]
                    dst = dst.rearrange("p (s t) -> p s t", s=2)
                    w = lambda n: sml[:, S_CW + 3 * j + n:S_CW + 3 * j + n + 1]
                    step(V.tensor_scalar(dst, src, w(1), sml[:, S_CB + j:S_CB + j + 1], ALU.mult, ALU.add))
                    step(V.scalar_tensor_tensor(dst[:, :, 1:S], src[:, :, 0:S - 1], w(0), dst[:, :, 1:S],
                                                ALU.mult, ALU.add))
                    step(V.scalar_tensor_tensor(dst[:, :, 0:S - 1], src[:, :, 1:S], w(2), dst[:, :, 0:S - 1],
                                                ALU.mult, ALU.add))
                announce("short_conv_done")
                dve.wait_ge(sem("natural_copied"), nth(dve, "natural_copied", 8))
                nat = proj[:, (C_HU + 4) * 512:(C_HU + 12) * 512]
                for o in range(2):
                    for s in range(2):
                        dve.wait_ge(sem("z_spectrum_ready"), nth(dve, "z_spectrum_ready"))
                        Y = hT[:, s * 2048:(s + 1) * 2048]
                        for m in range(2):
                            T = lambda cs: arena[:, ((o * 2 + m) * 2 + cs) * 512:][:, 0:512]
                            A, Bk = bank(2 * m), bank(2 * m + 1)
                            t0 = arena[:, 6144:6656]
                            re, im = Y[:, 2 * m * 512:(2 * m + 1) * 512], Y[:, (2 * m + 1) * 512:(2 * m + 2) * 512]
                            step(V.tensor_tensor(re, A, T(0), ALU.mult))
                            step(V.tensor_tensor(t0, Bk, T(1), ALU.mult))
                            step(V.tensor_tensor(re, re, t0, ALU.subtract))
                            step(V.tensor_tensor(im, A, T(1), ALU.mult))
                            step(V.tensor_tensor(t0, Bk, T(0), ALU.mult))
                            step(V.tensor_tensor(im, im, t0, ALU.add))
                        announce("y_spectrum_ready")
                        dve.wait_ge(sem("hyena_inverse_ready"), nth(dve, "hyena_inverse_ready"))
                        if o == 0:
                            part1 = nat[:, 2048 + s * 1024:2048 + (s + 1) * 1024]
                            signal(V.tensor_tensor(nat[:, s * 1024:(s + 1) * 1024], bank(4, 2), part1, ALU.mult),
                                   "hyena_z_ready")
                        else:
                            p2 = proj[:, C_HU * 512:(C_HU + 4) * 512].rearrange("p (c n) -> p c n", c=4)
                            g = proj[:, C_HG * 512:(C_HG + 4) * 512].rearrange("p (c n) -> p c n", c=4)
                            a = slice(s * S, (s + 1) * S)
                            step(V.tensor_tensor(p2[:, :, a], p2[:, :, a], g[:, :, a], ALU.mult))
                            signal(V.tensor_tensor(y3[:, 4:8, a], bank(4, 2).rearrange("p (c n) -> p c n", c=4),
                                                   p2[:, :, a], ALU.mult), "hyena_y_done")

            def attend(layer):
                us = attention_units(layer)
                n = len(us)
                if layer == 1:
                    dve.wait_ge(sem("y_gates_ready"), nth(dve, "y_gates_ready"))
                    dve.wait_ge(sem("position_bias_landed"), 16 * 32)
                    m = K(K_NBR, S).unsqueeze(1).to_broadcast([P, 16, S])
                    b = arena[:, 0:4096].rearrange("p (a n) -> p a n", a=16)
                    step(V.tensor_tensor(b, b, m, ALU.add))
                for i in range(n + 4):
                    if i < n:
                        u = us[i]
                        dve.wait_ge(sem("scores_ready"), nth(dve, "scores_ready"))
                        mx = stat[:, i % 4:i % 4 + 1]
                        nm = stat[:, 4 + i % 4:5 + i % 4]
                        if u["kind"] == "plain":
                            step(V.tensor_reduce(mx, bank(i % 2)[:, 0:u["keys"]], AX.X, ALU.max))
                            signal(V.tensor_scalar(nm, mx, -0.125, None, ALU.mult), "max_ready")
                        else:
                            sc = scores_sb(i)
                            rows = lambda a: a.rearrange("p (r c) -> p r c", r=4)
                            step(V.scalar_tensor_tensor(rows(sc[:, 0:S]), rows(bank(i % 2)[:, 0:S]), 0.125,
                                                        u["mask"], ALU.mult, ALU.add))
                            w = 512
                            if u["kind"] == "window":
                                step(V.tensor_copy(sc[:, 512:513], u["sink"]))
                                w = 513
                            dve.wait_ge(sem("context_scores_ready"), nth(dve, "context_scores_ready"))
                            step(V.tensor_reduce(mx, sc[:, 0:w], AX.X, ALU.max))
                            signal(V.tensor_scalar(nm, mx, -1.0, None, ALU.mult), "max_ready")
                    if 1 <= i <= n:
                        j = i - 1
                        dve.wait_ge(sem("probs_scaled_exp"), nth(dve, "probs_scaled_exp"))
                        pr = probs(j)[:, 0:us[j]["keys"]]
                        rs = stat[:, 12 + j % 4:13 + j % 4]
                        step(V.reciprocal(rs, stat[:, 8 + j % 4:9 + j % 4]))
                        signal(V.tensor_scalar(pr, pr, rs, None, ALU.mult), "probs_ready")
                    if i >= 4:
                        u = us[i - 4]
                        dve.wait_ge(sem("o_ready"), nth(dve, "o_ready"))
                        o = bank(4 + (i - 4) % 2)[u["half"] * 64:u["half"] * 64 + 64, 0:P]
                        signal(V.tensor_tensor(u["y"], o, u["gate"], ALU.mult), "o_gated")
                announce("y2_ready")

            def out2(layer):
                for j in range(OUTP):
                    multiplied(1)
                    for m in range(2):
                        for s, dst in enumerate((x3, c3)[:2 - layer]):
                            c = 2 * j + m
                            step(V.scalar_tensor_tensor(
                                dst[:, c, :], bank(c)[:, s * S:(s + 1) * S],
                                ada[:, 32 + 2 * c + s:33 + 2 * c + s], dst[:, c, :], ALU.mult, ALU.add))
                announce("x_done")
                announce("ada_done")

            hyena_filters()
            for layer in range(2):
                modulate(layer)
                panel[0] += IN2
                qk_norm(layer)
                if layer == 0:
                    hyena()
                attend(layer)
                out2(layer)


def _columns(w):
    n = w.shape[1] // 256
    return w.reshape(KD, P, n, 256).transpose(2, 1, 0, 3).reshape(n, P, PW)


def _branch(w):
    return w.reshape(4, P, 2, 512).transpose(2, 1, 0, 3).reshape(2, P, PW)


def _rows(w):
    return w.reshape(FSTEP, 2, P, D).transpose(0, 2, 1, 3).reshape(FSTEP, P, PW)


def _chunks(v):
    return v.reshape(-1, P).T


def kernel(**inputs):
    import concourse.bacc as _bacc
    from concourse.bass_utils import run_bass_kernel_spmd as _run

    a = {k: np.asarray(v) for k, v in inputs.items()}
    panels = np.empty((PANELS, P, PW), np.float32)
    at = 0

    def put(block):
        nonlocal at
        panels[at:at + len(block)] = block
        at += len(block)

    def put_ffn(gate, up, down):
        g, u, d = _columns(gate), _columns(up), _rows(down)
        put(g[0:1])
        put(u[0:1])
        for f in range(1, FSTEP):
            put(g[f:f + 1])
            put(u[f:f + 1])
            put(d[f - 1:f])
        put(d[FSTEP - 1:])

    for layer in range(2):
        w = a["w_in"][layer]
        hq, hf, hi, hog, sq, sk, sv, ga, gb = np.split(w, [512, 1024, 1536, 2048, 2560, 3072, 3584, 4608], 1)
        for part in (hq, hf, hog, sq, sk, ga, gb, hi, sv):
            put(_columns(part))
        A, B = _branch(a["w_branch_hgrn"][layer]), _branch(a["w_branch_sb"][layer])
        for j in range(2):
            put(A[j:j + 1])
            put(B[j:j + 1])
        put(_columns(a["w_out"][layer]))
        if layer == 0:
            put_ffn(a["dense_w_gate"][0], a["dense_w_up"][0], a["dense_w_down"][0])
        else:
            for e in range(E):
                put_ffn(a["moe_w_gate"][0, e], a["moe_w_up"][0, e], a["moe_w_down"][0, e])
    heads = np.arange(512).reshape(2, 4, 64).transpose(1, 0, 2).reshape(-1)
    for layer in range(2):
        put(_columns(a["w_ada_2"][layer]))
        cols = np.arange(3328)
        cols[0:512] = heads
        cols[2304:2816] = 2304 + heads
        put(_columns(a["w_in_2"][layer][:, cols]))
        rows = np.arange(1024)
        rows[0:512] = heads
        put(_columns(a["w_out_2"][layer][rows]))
    assert at == PANELS

    small = np.zeros((P, S_N), np.float32)
    small[:, S_MIX:S_MIX + 16] = _chunks(a["mix_norm"])
    small[:, S_FFN:S_FFN + 16] = _chunks(a["ffn_norm"])
    small[:, S_FIN:S_FIN + 8] = _chunks(a["final_norm"])
    small[:, S_NG:S_NG + 16] = _chunks(a["norm_g_2"])
    small[:, S_ON:S_ON + 2] = _chunks(a["hgrn_out_norm"])
    small[:, S_LB:S_LB + 8] = _chunks(a["hgrn_lb_logits"])
    for i, name in enumerate(("glob_q_norm_2", "glob_k_norm_2", "win_q_norm_2", "win_k_norm_2", "nat_q_norm_2",
                              "nat_k_norm_2")):
        small[:, S_QK + i] = np.concatenate([a[name][0]] * 2)
    small[:, S_CW:S_CW + 36] = a["hy_conv_w_2"][0].reshape(3, 12, P).transpose(2, 1, 0).reshape(P, 36)
    small[:, S_CB:S_CB + 12] = _chunks(a["hy_conv_b_2"])
    small[:, S_SINK:S_SINK + 8] = a["win_sink_2"][0][None, :]
    small[:, S_ADA:S_ADA + 48] = _chunks(a["b_ada_2"])
    small[:, S_ROUT:S_ROUT + 64] = a["moe_router"][0].reshape(KD, P, E).transpose(1, 0, 2).reshape(P, 64)
    both = np.stack([a["c_2"][0], a["c_ctx_2"]])
    small[:, S_COND:S_COND + 16] = both.reshape(2, KD, P).transpose(2, 1, 0).reshape(P, 16)
    for i, name in enumerate(("hy_b1_2", "hy_b2_2", "hy_freq_2")):
        small[0:64, S_HYP + i] = a[name][0]

    def tokens(t):
        return np.ascontiguousarray(t[0].reshape(S, KD, P).transpose(2, 1, 0).reshape(P, KD * S))

    arrays = dict(
        panels=panels, x=tokens(a["x"]), ctx=tokens(a["ctx_2"]), consts=constants(), small=small, dft=dft_tables(),
        decay=decay_table(), position=position_table(), w1=a["hy_w1_2"][0], w2=a["hy_w2_2"][0], w3=a["hy_w3_2"][0],
        skip=a["hy_skip_2"].reshape(1024), rpb=a["nat_rpb_2"][0, :, :, ::-1].reshape(-1))
    arrays = {k: np.ascontiguousarray(v) for k, v in arrays.items()}
    nc = _bacc.Bacc("TRN2", target_bir_lowering=False, num_devices=1)
    args = [nc.dram_tensor(k, v.shape, F32, kind="ExternalInput").ap() for k, v in arrays.items()]
    out = nc.dram_tensor("y", (P, KD * S), F32, kind="ExternalOutput").ap()
    two_blocks(nc, *args, out)
    got = _run(nc, [arrays], core_ids=[0]).results[0]["y"]
    return np.ascontiguousarray(got.reshape(P, KD, S).transpose(2, 1, 0).reshape(1, S, D))
```

```python
from contextlib import ExitStack

import numpy as np

import concourse.bass as bass
from concourse import mybir

F32 = mybir.dt.float32
F32R = mybir.dt.float32r
BF16 = mybir.dt.bfloat16
I32 = mybir.dt.int32
ACT = mybir.ActivationFunctionType
ALU = mybir.AluOpType
AX = mybir.AxisListType

P = 128
D = 1024
KD = D // P
S = 256
F = 3584
E = 8
PW = 2048
RING = 6
SPLIT = 3
EPS = 1e-6
PI = float(np.pi)
SLOTS = 128

IN1 = 22
IN2 = 13
ADA = 12
OUTP = 4
FSTEP = F // 256
FFN = 3 * FSTEP
LAYER1 = IN1 + OUTP + OUTP
BLOCK1 = LAYER1 + FFN + LAYER1 + E * FFN
LAYER2 = ADA + IN2 + OUTP
PANELS = BLOCK1 + 2 * LAYER2

HQ, HF, HOG, SQ, SK, GA, GB = 0, 4, 8, 12, 16, 20, 28
HI, SV = 18, 20
C_Q, C_K, C_V, C_HU, C_G, C_HG = 0, 4, 5, 6, 18, 22
C_NQ, C_NK, C_NV = 6, 10, 14

(K_ID, K_ONE, K_1024, K_128, K_BD, K_SWAP, K_TRI, K_NEG, K_LEV, K_STRICT, K_COS, K_SIN, K_WIN, K_NBR,
 K_LOW) = np.cumsum([0, 128, 128, 128, 128, 128, 128, 128, 128, 896, 128, 256, 256, 512, 256]).tolist()
K_EPS = K_LOW + 64
K_IOTA = K_EPS + 1
K_N = K_IOTA + P
S_MIX, S_FFN, S_FIN, S_NG, S_ON, S_LB, S_QK, S_CW, S_CB, S_SINK, S_ADA, S_ROUT, S_COND, S_HYP = np.cumsum(
    [0, 16, 16, 8, 16, 2, 8, 6, 36, 12, 8, 48, 64, 16]).tolist()
S_N = S_HYP + 3


def constants():
    c = np.zeros((P, K_N), np.float32)
    i, j = np.arange(P)[:, None], np.arange(P)[None, :]
    c[:, K_ID:K_ID + P] = i == j
    c[:, K_ONE:K_ONE + P] = 1.0
    c[:, K_1024:K_1024 + P] = 1.0 / D
    c[:, K_128:K_128 + P] = 1.0 / P
    c[:, K_BD:K_BD + P] = (i // 64 == j // 64) / 64.0
    c[:, K_SWAP:K_SWAP + P] = ((j % 2 == 1) & (i == j - 1)) * 1.0 - ((j % 2 == 0) & (i == j + 1)) * 1.0
    c[:, K_TRI:K_TRI + P] = -1.0 * (i >= j)
    c[:, K_NEG:K_NEG + P] = -1.0
    for lv in range(7):
        c[:, K_LEV + lv * P:K_LEV + (lv + 1) * P] = ((i >> lv) % 2 == 0) & ((j >> lv) == (i >> lv) + 1)
    c[:, K_STRICT:K_STRICT + P] = i < j
    t = np.arange(S)
    inv = 10000.0 ** (-np.arange(16, dtype=np.float32) / np.float32(16))
    ang = np.concatenate([(t // 64).astype(np.float32)[:, None] * inv, (t % 64).astype(np.float32)[:, None] * inv], -1)
    pair = (np.arange(P) % 64) // 2
    c[:, K_COS:K_COS + S] = np.cos(ang.astype(np.float32)).T[pair]
    c[:, K_SIN:K_SIN + S] = np.sin(ang.astype(np.float32)).T[pair]
    for qt in range(2):
        q = qt * P + np.arange(P)[:, None]
        c[:, K_WIN + qt * S:K_WIN + (qt + 1) * S] = np.where(np.abs(t[None, :] - q) <= 128, 0.0, -1e30)
    c0 = np.clip(np.arange(P) % 64 - 8, 0, 48)[:, None]
    kc = 63 - (t % 64)[None, :]
    c[:, K_NBR:K_NBR + S] = np.where((kc >= c0) & (kc < c0 + 16), 0.0, -1e30)
    low = (np.arange(8)[None, :] < np.arange(8)[:, None]) * 1.0
    c[:, K_LOW:K_LOW + 64] = low.reshape(1, 64)
    c[:, K_EPS] = EPS
    c[:, K_IOTA:K_IOTA + P] = j
    return c


def dft_tables():
    t = np.arange(S, dtype=np.float64)
    a = np.pi * np.outer(t, 2 * t + 1) / 512.0
    rows = lambda m: m.reshape(2, P, S).transpose(1, 0, 2).reshape(P, 2 * S)
    return np.concatenate([rows(np.cos(a)), rows(np.sin(a)), rows(np.cos(a).T / 256), rows(np.sin(a).T / 256)],
                          1).astype(np.float32)


def decay_table():
    t = np.linspace(0.0, 1.0, S, dtype=np.float32)[:, None]
    deltas = np.linspace(np.log(1e-2) / 1.5, np.log(1e-2) / 0.3, 512, dtype=np.float32)
    d = np.exp(-t * np.abs(deltas)).astype(np.float32)
    return d.reshape(2, P, 512).transpose(1, 0, 2).reshape(P, 1024)


def position_table():
    t = np.linspace(0.0, 1.0, S, dtype=np.float32)[:, None]
    w = (2.0 * np.pi * np.arange(S, dtype=np.float32)[:, None] / S).astype(np.float32)
    f = np.linspace(1e-4, 15, 16, dtype=np.float32)[None, :]
    return np.concatenate([t, np.cos(f * w), -np.sin(f * w)], -1).T.astype(np.float32)


def two_blocks(nc, panels, x_in, ctx_in, consts_in, small_in, dft_in, decay_in, pos_in, w1_in, w2_in, w3_in,
               skip_in, rpb_in, out):
    stack = ExitStack()
    with stack:
        def sb(name, words, parts=P, dt=F32):
            return stack.enter_context(nc.sbuf_tensor(name, [parts, words], dt))

        sems = {}

        def sem(name):
            if name not in sems:
                sems[name] = stack.enter_context(nc.semaphore(name))
            return sems[name]

        seen = {}

        def nth(eng, name, k=1):
            key = (eng.engine, name)
            seen[key] = seen.get(key, 0) + k
            return seen[key]

        ring = sb("ring", RING * PW)
        at_ring = nc.sbuf_base - 4 * RING * PW
        xT = sb("xT", KD * S)
        cT = sb("cT", KD * S)
        at_hT = nc.sbuf_base
        hT = sb("hT", KD * 512)
        at_proj = nc.sbuf_base
        proj = sb("proj", 26 * 512)
        at_yT = nc.sbuf_base
        yT = sb("yT", KD * 512)
        at_arena = nc.sbuf_base
        arena = sb("arena", 9728)
        cst = sb("cst", K_N)
        sml = sb("sml", S_N)
        rstd = sb("rstd", 512)
        ada = sb("ada", 48)
        ada_a = sb("ada_a", 16)
        cond = sb("cond", 16)
        lbs = sb("lbs", 32)
        stat = sb("stat", 16)
        rt = sb("rt", 400)
        zrow = sb("zrow", 640, dt=BF16)
        ps = stack.enter_context(nc.psum_tensor("ps", [P, 8, 512], F32))

        def over(name, at, first, words):
            return nc.alloc_sbuf_tensor_at(name, [P, words], F32R, offset=at + 4 * first)[:, :]

        W_high = over("W_high", at_proj, 0, SPLIT * PW)
        W_low = over("W_low", at_proj, SPLIT * PW, SPLIT * PW)
        h_high = over("h_high", at_yT, 0, KD * S)
        h_low = over("h_low", at_yT, KD * S, KD * S)
        xe_high = over("xe_high", at_hT, 0, KD * P)
        xe_low = over("xe_low", at_hT, KD * P, KD * P)
        hid_high = over("hid_high", at_arena, 2048, 1024)
        hid_low = over("hid_low", at_arena, 3072, 1024)

        P_high = over("P_high", at_arena, 0, 4 * PW)
        ring_low = over("ring_low", at_ring, 0, RING * PW)
        h_parts = over("h_parts", at_hT, 0, KD * 512).rearrange("p (k n) -> p k n", k=KD)
        y_parts = over("y_parts", at_yT, 0, KD * 512).rearrange("p (k n) -> p k n", k=KD)

        N_high = (over("N_high_even", at_arena, 6144, PW), over("N_high_odd", at_proj, 22 * 512, PW))

        def wide_high(p, a, b):
            at = (1, 3, 0)[p % 3] * PW
            return P_high[:, at + a:at + b]

        def wide_low(p, a, b):
            s = p % RING
            return ring_low[:, s * PW + a:s * PW + b]

        h3 = hT[:, :].rearrange("p (k n) -> p k n", k=KD)
        y3 = yT[:, :].rearrange("p (k n) -> p k n", k=KD)
        x3 = xT[:, :].rearrange("p (k n) -> p k n", k=KD)
        c3 = cT[:, :].rearrange("p (k n) -> p k n", k=KD)
        ones1 = cst[:, K_ONE:K_ONE + 1]
        eps1 = cst[:, K_EPS:K_EPS + 1]

        def K(at, n=P):
            return cst[:, at:at + n]

        def bank(b, n=1):
            return ps[:, b:b + n, :].rearrange("p b n -> p (b n)")

        def slot(p, a, b):
            s = p % RING
            return ring[:, s * PW + a:s * PW + b]

        def qk_chunks(layer):
            if layer == 0:
                return [(C_Q + c, 512, 0, True) for c in range(4)] + [(C_K, 512, 1, True)]
            return ([(C_Q + c, S, 2, True) for c in range(4)] + [(C_K, 512, 3, True)]
                    + [(C_NQ + c, S, 4, False) for c in range(4)] + [(C_NK + c, 512, 5, False) for c in range(4)])

        def attention_units(layer):
            us = []

            def gqa(c, half, qt, stream, kind):
                r = slice(half * 64, half * 64 + 64)
                first = 0 if stream == 0 else 2
                us.append(dict(
                    half=half, keys=512 if stream == 0 else 256, kind=kind,
                    q=proj[r, (C_Q + c) * 512 + stream * S + qt * P:][:, 0:P],
                    k=proj[r, C_K * 512 + stream * S:(C_K + 1) * 512],
                    v=lambda n: proj[:, C_V * 512 + (first + n) * P + half * 64:][:, 0:64],
                    mask=K(K_WIN + qt * S, S).rearrange("p (r c) -> p r c", r=4),
                    sink=sml[:, S_SINK + c + 4 * half:S_SINK + c + 4 * half + 1],
                    gate=proj[r, (C_G + c) * 512 + stream * S + qt * P:][:, 0:P],
                    y=yT[r, c * 512 + stream * S + qt * P:][:, 0:P]))

            def neighbour(h, qt):
                half, c = h % 2, h // 2
                r = slice(half * 64, half * 64 + 64)
                us.append(dict(
                    half=half, keys=512, kind="neighbour",
                    q=proj[r, (C_NQ + c) * 512 + qt * P:][:, 0:P], k=proj[r, (C_NK + c) * 512:(C_NK + c + 1) * 512],
                    v=lambda n: proj[:, (C_NV + 2 * (h // 4)) * 512 + n * S + (h % 4) * 64:][:, 0:64],
                    mask=arena[:, (h * 2 + qt) * S:(h * 2 + qt + 1) * S].rearrange("p (r c) -> p r c", r=4)[:, :, ::-1],
                    gate=proj[r, (C_HG + c) * 512 + qt * P:][:, 0:P],
                    y=yT[r, (4 + c) * 512 + qt * P:][:, 0:P]))

            if layer == 0:
                for c in range(4):
                    for half in range(2):
                        for stream in range(2):
                            for qt in range(2):
                                gqa(c, half, qt, stream, "plain")
            else:
                for c in range(4):
                    for half in range(2):
                        for qt in range(2):
                            gqa(c, half, qt, 0, "window")
                for h in range(8):
                    for qt in range(2):
                        neighbour(h, qt)
            return us

        def qk_root(i):
            return arena[:, 7424:7936] if i % 2 else rstd[:, :]

        def probs(i):
            return arena[:, 6144 + (i % 3) * 520:][:, 0:520]

        def probsT(i):
            return arena[:, 7704 + (i % 2) * 512:][:, 0:512]

        def scores_sb(i):
            return arena[:, 4096 + (i % 2) * 520:4096 + (i % 2) * 520 + 520]

        hN = yT[:, 0:2048]
        yS = yT[:, 2048:3072]
        G = arena[:, 6144:8448]
        SEL = arena[:, 4096:6144]
        SELW = arena[:, 6144:8192]
        crowded = stack.enter_context(nc.sbuf_tensor("crowded", [1, 1], I32))

        block = stack.enter_context(nc.Block())
        LANDED = [sem(f"panel_landed_{s}") for s in range(RING)]
        DONE = sem("panels_multiplied")

        def split(t, p, a, b):
            s = p % SPLIT
            return t[:, s * PW + a:s * PW + b]

        @block.sync
        def _(sp):
            def load(p, s):
                sp.dma_start(ring[:, s * PW:(s + 1) * PW], panels[bass.ds(p, 1), :, :].rearrange("a p n -> p (a n)")) \
                  .then_inc(LANDED[s], 16)

            sp.dma_start(xT[:, :], x_in).then_inc(sem("inputs_landed"), 16)
            sp.dma_start(sml[:, :], small_in).then_inc(sem("inputs_landed"), 16)
            sp.dma_start(cst[:, :], consts_in).then_inc(sem("inputs_landed"), 16)
            for s in range(RING):
                load(s, s)
            sp.dma_start(cT[:, :], ctx_in).then_inc(sem("context_landed"), 16)
            full = PANELS // RING
            with sp.Fori(1, full) as r:
                for s in range(RING):
                    sp.wait_ge(DONE, r * RING + (s - RING + 1))
                    load(r * RING + s, s)
            for p in range(full * RING, PANELS):
                sp.wait_ge(DONE, p - RING + 1)
                load(p, p % RING)

        @block.tensor
        def _(pe):
            at = [0]

            def mm(o, w, m, start, stop, skip=False):
                return nc.tensor.matmul(o, w, m, start=start, stop=stop, skip_group_check=skip)

            def landed(p, rounds=0):
                pe.wait_ge(LANDED[p % RING], 16 * (p // RING + 1) + rounds * 16)

            def take():
                p = at[0]
                at[0] += 1
                landed(p)
                return p

            def panel_T(p, b, n, rhs):
                for m in range(2):
                    o = bank(b)[:, m * 256:m * 256 + n] if n <= 256 else bank(b + m)
                    for k in range(KD):
                        last = mm(o, slot(p, k * 256 + m * P, k * 256 + (m + 1) * P), rhs(k), k == 0, k == KD - 1)
                return last

            def norm(streams=1):
                pe.wait_ge(sem("squares_ready"), nth(pe, "squares_ready"))
                for s in range(streams):
                    for k in range(KD):
                        last = mm(bank(0)[:, s * S:(s + 1) * S], K(K_1024), h3[:, k, s * S:(s + 1) * S],
                                  k == 0, k == KD - 1)
                last.then_inc(sem("mean_square_ready"), 1)

            def mm3(o, w, m, start, stop, skip=False):
                mm(o, w[0], m[0], start, False, skip)
                mm(o, w[0], m[1], False, False, skip)
                return mm(o, w[1], m[0], False, stop, skip)

            def W1(q, a, b):
                return wide_high(q, a, b), wide_low(q, a, b)

            def parts(t, k, a=0, b=S):
                return t[:, k, S + a:S + b], t[:, k, a:b]

            def take_split():
                p = at[0]
                at[0] += 1
                pe.wait_ge(sem("wide_panel_split"), nth(pe, "wide_panel_split"))
                return p

            def project1():
                pe.wait_ge(sem("h_parts_ready"), nth(pe, "h_parts_ready", 2))
                for p in range(IN1):
                    q = take_split()
                    if p >= 8:
                        copied = "proj_even_copied" if p % 2 == 0 else "proj_odd_copied"
                        pe.wait_ge(sem(copied), nth(pe, copied))
                    for m in range(2):
                        for k in range(KD):
                            if p < 18:
                                w, x = W1(q, k * 256 + m * P, k * 256 + (m + 1) * P), parts(h_parts, k)
                            else:
                                w, x = parts(h_parts, k, m * P, (m + 1) * P), W1(q, k * 256, (k + 1) * 256)
                            last = mm3(bank(p % 8)[:, m * S:(m + 1) * S], w, x, k == 0, k == KD - 1)
                    last.then_inc(DONE, 1)
                seen[(pe.engine, "proj_even_copied")] += 4
                seen[(pe.engine, "proj_odd_copied")] += 4

            def hgrn():
                q = arena[:, 0:1024]
                kk = arena[:, 1024:2048]
                X = [arena[:, 5120:6144], arena[:, 6144:7168]]
                pe.wait_ge(sem("hgrn_qk_ready"), nth(pe, "hgrn_qk_ready"))
                for h in range(8):
                    last = mm(bank(0, 2)[:, h * P:(h + 1) * P], kk[:, h * P:(h + 1) * P], q[:, h * P:(h + 1) * P],
                              True, True)
                last.then_inc(sem("level_scores_ready"), 1)
                for lv in range(8):
                    pe.wait_ge(sem("level_q_ready"), nth(pe, "level_q_ready"))
                    pe.wait_ge(sem("level_k_ready"), nth(pe, "level_k_ready"))
                    x = X[lv % 2]
                    if lv >= 1:
                        pe.wait_ge(sem("level_merged"), nth(pe, "level_merged"))
                    if lv < 7:
                        for h in range(8):
                            xs = x[:, h * P:(h + 1) * P]
                            last = mm(bank(2 - 2 * (lv % 2), 2)[:, h * P:(h + 1) * P], xs, xs, True, True)
                    else:
                        for h in range(4):
                            last = mm(bank(4)[:, h * P:(h + 1) * P], x[:, h * S:h * S + P],
                                      x[:, h * S + P:(h + 1) * S], True, True)
                    last.then_inc(sem("level_scores_ready"), 1)
                pe.wait_ge(sem("hgrn_scores_merged"), nth(pe, "hgrn_scores_merged"))
                pe.wait_ge(sem("level_merged"), nth(pe, "level_merged"))
                sc = arena[:, 7168:8192]
                cross = arena[:, 8192:8704]
                for h in range(4):
                    o = bank(5 + h // 2)[:, (h % 2) * S:(h % 2 + 1) * S]
                    v = lambda tb: proj[:, (HI + h // 2) * 512 + tb * S + (h % 2) * P:][:, 0:P]
                    mm(o[:, 0:P], v(0), sc[:, 2 * h * P:(2 * h + 1) * P], True, True)
                    mm(o[:, P:S], v(1), sc[:, (2 * h + 1) * P:(2 * h + 2) * P], True, False)
                    last = mm(o[:, P:S], v(0), cross[:, h * P:(h + 1) * P], False, True)
                last.then_inc(sem("hgrn_o_ready"), 1)
                pe.wait_ge(sem("hgrn_o_squared"), nth(pe, "hgrn_o_squared"))
                for j in range(2):
                    last = mm(bank(7 if j else 4), K(K_128), arena[:, 3072 + j * 512:3072 + (j + 1) * 512], True, True)
                last.then_inc(sem("hgrn_mean_square_ready"), 1)

            def stick():
                pe.wait_ge(sem("hgrn_done"), nth(pe, "hgrn_done"))
                for g in range(2):
                    L = arena[:, g * 3072:g * 3072 + 1536]
                    W = arena[:, g * 3072 + 1536:(g + 1) * 3072]
                    if g:
                        pe.wait_ge(sem("stick_exponent_ready"), nth(pe, "stick_exponent_ready", 1))
                        seen[(pe.engine, "stick_exponent_ready")] += 1
                    for i in range(4):
                        h = 4 * g + i
                        r = slice((h % 2) * 64, (h % 2) * 64 + 64)
                        kh = proj[r, (SK + h // 2) * S:(SK + h // 2 + 1) * S]
                        qh = proj[r, (SQ + h // 2) * S:(SQ + h // 2 + 1) * S]
                        mm(bank(i)[:, 0:S], kh[:, 0:P], qh, True, False, True)
                        last = mm(bank(i)[:, S:S + P], kh[:, P:S], qh[:, P:S], False, False, True)
                    last.then_inc(sem("stick_z_ready"), 1)
                    pe.wait_ge(sem("stick_softplus_ready"), nth(pe, "stick_softplus_ready"))
                    for i in range(4):
                        l = L[:, i * 384:(i + 1) * 384]
                        mm(bank(i)[:, 0:S], K(K_TRI), l[:, 0:S], False, False, True)
                        mm(bank(i)[:, P:S], K(K_NEG), l[:, S:384], False, False, True)
                        last = mm(bank(i)[:, S:384], K(K_TRI), l[:, S:384], False, True, True)
                    last.then_inc(sem("stick_sums_ready"), 1)
                    pe.wait_ge(sem("stick_weights_ready"), nth(pe, "stick_weights_ready"))
                    for i in range(4):
                        h = 4 * g + i
                        o = bank(4 + g)[(h % 2) * 64:(h % 2) * 64 + 64, (i // 2) * S:(i // 2 + 1) * S]
                        v = lambda tb: proj[:, (SV + h // 4) * 512 + tb * S + (h % 4) * 64:][:, 0:64]
                        w = W[:, i * 384:(i + 1) * 384]
                        mm(o, v(0), w[:, 0:S], True, False)
                        last = mm(o[:, P:S], v(1), w[:, S:384], False, True)
                    last.then_inc(sem("stick_o_ready"), 1)

            def mix_out():
                pe.wait_ge(sem("y_parts_ready"), nth(pe, "y_parts_ready", 3))
                for j in range(2):
                    for br in range(2):
                        q = take_split()
                        for m in range(4):
                            o = bank(4 * j + 2 * br + m // 2)[:, (m % 2) * S:(m % 2 + 1) * S]
                            for k in range(4):
                                last = mm3(o, W1(q, k * 512 + m * P, k * 512 + (m + 1) * P),
                                           parts(y_parts, 4 * br + k), k == 0, k == 3)
                        last.then_inc(DONE, 1)
                pe.wait_ge(sem("h_parts_ready"), nth(pe, "h_parts_ready", 2))
                for j in range(OUTP):
                    q = take_split()
                    for m in range(2):
                        for k in range(KD):
                            last = mm3(bank(j)[:, m * S:(m + 1) * S], W1(q, k * 256 + m * P, k * 256 + (m + 1) * P),
                                       parts(h_parts, k), k == 0, k == KD - 1)
                    last.then_inc(DONE, 1)

            def ffn(p0, e=0):
                hb = [arena[:, 1024:1536], arena[:, 1536:2048]]

                def up(p, f, r):
                    for j in range(2):
                        landed(p + j, r)
                        panel_T(p + j, 2 * j + f % 2, S, lambda k: h3[:, k, 0:S]).then_inc(DONE, 1)

                def down(p, f, r, count):
                    landed(p, r)
                    pe.wait_ge(sem("hidden_ready"), count)
                    for k in range(2):
                        for m in range(KD):
                            last = mm(bank(4 + m // 2)[:, (m % 2) * S:(m % 2 + 1) * S],
                                      slot(p, k * D + m * P, k * D + (m + 1) * P),
                                      hb[f % 2][:, k * S:(k + 1) * S], False, True, True)
                    last.then_inc(DONE, 1)

                er = e * (FFN // RING)
                up(p0, 0, er)
                pe.wait_ge(sem("accumulators_free"), e + accs[0])
                for b in range(4):
                    mm(bank(4 + b), zrow[:, 0:P], zrow[:, P:640], True, False, True)
                with pe.Fori(0, FSTEP // 2 - 1) as i:
                    up(p0 + 2, 1, er + i)
                    down(p0 + 4, 0, er + i, e * FSTEP + i * 2 + 1)
                    up(p0 + 5, 0, er + i)
                    down(p0 + 7, 1, er + i, e * FSTEP + i * 2 + 2)
                up(p0 + 38, 1, er)
                down(p0 + 40, 0, er, e * FSTEP + (FSTEP - 1))
                down(p0 + 41, 1, er, e * FSTEP + FSTEP)

            def W(p, a, b):
                return split(W_high, p, a, b), split(W_low, p, a, b)

            def dense_layer(p0):
                def up(p, b, count):
                    pe.wait_ge(sem("panel_split"), count)
                    for m in range(2):
                        for k in range(KD):
                            last = mm3(bank(b)[:, m * S:(m + 1) * S], W(p, k * 256 + m * P, k * 256 + (m + 1) * P),
                                       (h_high[:, k * S:(k + 1) * S], h_low[:, k * S:(k + 1) * S]),
                                       k == 0, k == KD - 1)
                    last.then_inc(DONE, 1)

                def down(p, f, count, hidden):
                    pe.wait_ge(sem("panel_split"), count)
                    pe.wait_ge(sem("hidden_split"), hidden)
                    for k in range(2):
                        a = (f % 2) * 512 + k * S
                        for m in range(KD):
                            last = mm3(bank(4 + m // 2)[:, (m % 2) * S:(m % 2 + 1) * S],
                                       W(p, k * D + m * P, k * D + (m + 1) * P),
                                       (hid_high[:, a:a + S], hid_low[:, a:a + S]), False, True, True)
                    last.then_inc(DONE, 1)

                pe.wait_ge(sem("h_split"), nth(pe, "h_split", KD))
                up(p0, 0, 1)
                up(p0 + 1, 2, 2)
                pe.wait_ge(sem("accumulators_free"), 1)
                for b in range(4):
                    mm(bank(4 + b), zrow[:, 0:P], zrow[:, P:640], True, False, True)
                with pe.Fori(0, FSTEP // 2 - 1) as i:
                    up(p0 + 2, 1, i * 6 + 3)
                    up(p0 + 3, 3, i * 6 + 4)
                    down(p0 + 4, 0, i * 6 + 5, i * 2 + 1)
                    up(p0 + 5, 0, i * 6 + 6)
                    up(p0 + 6, 2, i * 6 + 7)
                    down(p0 + 7, 1, i * 6 + 8, i * 2 + 2)
                up(p0 + 38, 1, 39)
                up(p0 + 39, 3, 40)
                down(p0 + 40, 0, 41, FSTEP - 1)
                down(p0 + 41, 1, 42, FSTEP)

            def router():
                pe.wait_ge(sem("h_ready"), nth(pe, "h_ready", 4 * KD))
                for tb in range(2):
                    for k in range(KD):
                        last = mm(bank(1)[:, tb * 8:tb * 8 + 8], h3[:, k, tb * P:(tb + 1) * P],
                                  sml[:, S_ROUT + k * 8:S_ROUT + k * 8 + 8], k == 0, k == KD - 1)
                last.then_inc(sem("logits_ready"), 1)
                for j in range(4):
                    tb, half = j // 2, j % 2
                    if j == 1:
                        pe.wait_ge(sem("logits_copied"), nth(pe, "logits_copied"))
                    for c in range(4):
                        last = nc.tensor.transpose(bank(j)[:, c * P:(c + 1) * P],
                                                   h3[:, half * 4 + c, tb * P:(tb + 1) * P], K(K_ID))
                last.then_inc(sem("h_turned"), 1)
                pe.wait_ge(sem("selected_ready"), nth(pe, "selected_ready"))
                s0, s1 = rt[:, 40:48], rt[:, 48:56]
                o = bank(7)
                mm(o[:, 0:8], K(K_STRICT), s0, True, True)
                mm(o[:, 8:16], K(K_ONE), s0, True, False)
                mm(o[:, 8:16], K(K_STRICT), s1, False, True)
                mm(o[:, 16:24], K(K_ONE), s0, True, False)
                mm(o[:, 16:24], K(K_ONE), s1, False, True).then_inc(sem("places_ready"), 1)
                pe.wait_ge(sem("combine_diagonals_ready"), nth(pe, "combine_diagonals_ready"))
                for b in range(4):
                    last = mm(bank(4 + b), K(K_ONE), arena[:, 4096 + b * 512:4096 + (b + 1) * 512], True, True)
                last.then_inc(sem("combine_ready"), 1)
                pe.wait_ge(sem("weighted_selection_ready"), nth(pe, "weighted_selection_ready"))
                for j in range(16):
                    last = nc.tensor.transpose(bank(4, 4)[:, j * P:(j + 1) * P], SELW[:, j * P:(j + 1) * P], K(K_ID))
                last.then_inc(sem("slot_weights_ready"), 1)
                pe.wait_ge(sem("slot_weights_copied"), nth(pe, "slot_weights_copied"))
                pe.wait_ge(sem("h_tokens_copied"), nth(pe, "h_tokens_copied"))
                pe.wait_ge(sem("crowded_ready"), nth(pe, "crowded_ready"))

            def scatter(e, count):
                for j in range(4):
                    if j >= 2:
                        pe.wait_ge(sem("rows_added"), count + (j - 1))
                    for m in range(2):
                        c = 2 * j + m
                        last = mm(bank(6 + j % 2)[:, m * S:(m + 1) * S], yS[:, c * P:(c + 1) * P],
                                  G[:, bass.ds(e * S, S)], True, True)
                    last.then_inc(sem("rows_spread"), 1)

            def compact_expert(p0, e):
                hd = [arena[:, 1024:1280], arena[:, 1536:1792]]
                e1 = e * FFN + FFN
                f1 = e * FSTEP + FSTEP

                def up(p, b, count):
                    pe.wait_ge(sem("panel_split"), count)
                    for k in range(KD):
                        last = mm3(bank(b)[:, 0:S], (xe_high[:, k * P:(k + 1) * P], xe_low[:, k * P:(k + 1) * P]),
                                   W(p, k * 256, (k + 1) * 256), k == 0, k == KD - 1)
                    last.then_inc(DONE, 1)

                def turn(f, count):
                    pe.wait_ge(sem("hidden_made"), count)
                    for k in range(2):
                        last = nc.tensor.transpose(bank(6)[:, k * P:(k + 1) * P], hd[f % 2][:, k * P:(k + 1) * P],
                                                   K(K_ID))
                    last.then_inc(sem("hidden_turned"), 1)

                def down(p, f, count, hidden):
                    pe.wait_ge(sem("panel_split"), count)
                    pe.wait_ge(sem("hidden_split"), hidden)
                    for k in range(2):
                        a = (f % 2) * 512 + k * P
                        for n in range(2):
                            last = mm3(bank(4 + n), (hid_high[:, a:a + P], hid_low[:, a:a + P]),
                                       W(p, k * D + n * 512, k * D + (n + 1) * 512), False, True, True)
                    last.then_inc(DONE, 1)

                for half in range(2):
                    for c in range(4):
                        for tb in range(2):
                            last = mm(bank(2 + half)[:, c * P:(c + 1) * P],
                                      hN[:, tb * D + (half * 4 + c) * P:][:, 0:P],
                                      SEL[:, bass.ds(e * S + tb * P, P)], tb == 0, tb == 1)
                last.then_inc(sem("tokens_gathered"), 1)
                pe.wait_ge(sem("rows_copied"), e + 1)
                scatter(e, e * 4)
                pe.wait_ge(sem("tokens_split"), e + 1)
                up(p0, 0, e1 + 1)
                for b in range(2):
                    mm(bank(4 + b), zrow[:, 0:P], zrow[:, P:640], True, False, True)
                pe.wait_ge(sem("rows_added"), e * 4 + 4)
                up(p0 + 1, 2, e1 + 2)
                with pe.Fori(0, FSTEP // 2 - 1) as i:
                    s, h = e1 + i * 6, f1 + i * 2
                    up(p0 + 2, 1, s + 3)
                    turn(0, h + 1)
                    up(p0 + 3, 3, s + 4)
                    down(p0 + 4, 0, s + 5, h + 1)
                    up(p0 + 5, 0, s + 6)
                    turn(1, h + 2)
                    up(p0 + 6, 2, s + 7)
                    down(p0 + 7, 1, s + 8, h + 2)
                up(p0 + 38, 1, e1 + 39)
                turn(0, f1 + (FSTEP - 1))
                up(p0 + 39, 3, e1 + 40)
                down(p0 + 40, 0, e1 + 41, f1 + (FSTEP - 1))
                turn(1, f1 + FSTEP)
                down(p0 + 41, 1, e1 + 42, f1 + FSTEP)

            accs = [1]
            pe.wait_ge(sem("inputs_landed"), 48)
            for layer in range(2):
                norm()
                project1()
                hgrn()
                stick()
                mix_out()
                norm()
                if layer == 0:
                    dense_layer(at[0])
                    at[0] += FFN
                    accs[0] += 2
                else:
                    router()
                    many = pe.value_load(crowded[0:1, 0:1], min_val=0, max_val=1)
                    with pe.If(many == 1):
                        with pe.Fori(0, E) as e:
                            ffn(at[0], e)
                    with pe.Else():
                        with pe.Fori(0, E) as e:
                            compact_expert(at[0], e)
                        pe.wait_ge(sem("rows_copied"), E + 1)
                        scatter(E, 4 * E)
                    at[0] += E * FFN
            norm()

            def hyena_filters():
                h1 = proj[0:64, 2304:2560]
                h2 = proj[0:64, 2560:2816]
                pe.wait_ge(sem("filter_tables_landed"), nth(pe, "filter_tables_landed", 16 * 7))
                mm(bank(1)[0:64, 0:S], proj[0:33, 2816:2880], proj[0:33, 2048:2304], True, True) \
                    .then_inc(sem("filter_hidden_sum"), 1)
                pe.wait_ge(sem("filter_hidden_ready"), nth(pe, "filter_hidden_ready"))
                mm(bank(1)[0:64, 0:S], proj[0:64, 2880:2944], h1, True, True).then_inc(sem("filter_hidden_sum"), 1)
                pe.wait_ge(sem("filter_hidden_ready"), nth(pe, "filter_hidden_ready"))
                for o in range(2):
                    if o:
                        pe.wait_ge(sem("filter_spectrum_ready"), nth(pe, "filter_spectrum_ready"))
                    for tb in range(2):
                        for d in range(2):
                            last = mm(bank(tb * 2 + d), h2[:, tb * P:(tb + 1) * P],
                                      proj[0:64, (o * 2 + d) * 512:(o * 2 + d + 1) * 512], True, True)
                    last.then_inc(sem("filter_taps_sum"), 1)
                    pe.wait_ge(sem("taps_squared"), nth(pe, "taps_squared"))
                    for j in range(4):
                        last = mm(bank(4), K(K_ONE), proj[:, 9216 + j * 512:9216 + (j + 1) * 512], j == 0, j == 3)
                    last.then_inc(sem("taps_energy_ready"), 1)
                    pe.wait_ge(sem("taps_combined"), nth(pe, "taps_combined"))
                    pe.wait_ge(sem("taps_rnorm_ready"), nth(pe, "taps_rnorm_ready"))
                    for m in range(2):
                        for cs in range(2):
                            for tb in range(2):
                                last = mm(bank(4 + 2 * m + cs),
                                          arena[:, 4096 + cs * 512 + tb * S + m * P:][:, 0:P],
                                          proj[:, 6144 + cs * 1024 + tb * 512:][:, 0:512], tb == 0, tb == 1)
                    last.then_inc(sem("spectrum_sum"), 1)
                pe.wait_ge(sem("filter_spectrum_ready"), nth(pe, "filter_spectrum_ready"))

            def adaln():
                if at[0] == BLOCK1:
                    pe.wait_ge(sem("cond_ready"), nth(pe, "cond_ready"))
                else:
                    pe.wait_ge(sem("ada_done"), nth(pe, "ada_done"))
                for p in range(ADA):
                    if p == ADA // 2:
                        norm(2)
                    q = take()
                    for k in range(KD):
                        last = mm(bank(1 + p // 2)[0:2, (p % 2) * 256:(p % 2 + 1) * 256], cond[:, 2 * k:2 * k + 2],
                                  slot(q, k * 256, (k + 1) * 256), k == 0, k == KD - 1)
                    last.then_inc(DONE, 1)
                pe.wait_ge(sem("ada_rows_copied"), nth(pe, "ada_rows_copied"))
                for c in range(24):
                    last = nc.tensor.transpose(bank(7)[:, 2 * c:2 * c + 2], arena[0:2, 6144 + c * P:][:, 0:P],
                                               cst[0:2, K_ID:K_ID + 2])
                last.then_inc(sem("ada_turned"), 1)

            def project2(layer):
                def X(k, a, b):
                    return y_parts[:, k, a:b], h_parts[:, k, a:b]

                pe.wait_ge(sem("h_mod_split"), nth(pe, "h_mod_split", 2 * KD))
                for p in range(IN2):
                    q = at[0]
                    at[0] += 1
                    if p != 1:
                        pe.wait_ge(sem("wide_panel_split"), nth(pe, "wide_panel_split", 1 if p else 2))
                    W2 = lambda a, b: (N_high[p % 2][:, a:b], wide_low(q, a, b))
                    b = 2 * (p % 4)
                    if p >= 4:
                        pe.wait_ge(sem("pair_copied"), nth(pe, "pair_copied"))
                    wide = layer == 0 or p in (2, 5, 6)
                    n = 512 if wide else S
                    if layer == 1 and p in (7, 8):
                        for tb in range(4):
                            for k in range(KD):
                                last = mm3(bank(b, 2)[:, tb * S:(tb + 1) * S], X(k, tb * P, (tb + 1) * P),
                                           W2(k * 256, (k + 1) * 256), k == 0, k == KD - 1)
                    elif p == 2:
                        for k in range(KD):
                            mm3(bank(b), W2(k * 256, k * 256 + P), X(k, 0, 512), k == 0, k == KD - 1)
                        for tb in range(4):
                            for k in range(KD):
                                last = mm3(bank(b + 1)[:, tb * P:(tb + 1) * P], X(k, tb * P, (tb + 1) * P),
                                           W2(k * 256 + P, (k + 1) * 256), k == 0, k == KD - 1)
                    else:
                        for m in range(2):
                            for k in range(KD):
                                last = mm3(bank(b + m)[:, 0:n], W2(k * 256 + m * P, k * 256 + (m + 1) * P),
                                           X(k, 0, n), k == 0, k == KD - 1)
                    last.then_inc(DONE, 1)
                pe.wait_ge(sem("pair_copied"), nth(pe, "pair_copied", 4))

            def qk_norm(layer):
                chunks = qk_chunks(layer)

                def mean_square(i):
                    n = chunks[i][1]
                    pe.wait_ge(sem("qk_squared"), nth(pe, "qk_squared"))
                    mm(bank(i % 2)[:, 0:n], K(K_BD), arena[:, 6144 + (i % 2) * 512:][:, 0:n], True, True) \
                        .then_inc(sem("qk_mean_square"), 1)

                mean_square(0)
                mean_square(1)
                for i, (c, n, g, rope) in enumerate(chunks):
                    pe.wait_ge(sem("qk_root_ready"), nth(pe, "qk_root_ready"))
                    if i + 2 < len(chunks):
                        mean_square(i + 2)
                    pe.wait_ge(sem("qk_normed"), nth(pe, "qk_normed"))
                    if rope:
                        mm(bank(2 + i % 2)[:, 0:S], K(K_SWAP), proj[:, c * 512:c * 512 + S], True, True) \
                            .then_inc(sem("qk_swapped"), 1)
                pe.wait_ge(sem("qk_done"), nth(pe, "qk_done"))

            def hyena():
                nat = yT[:, :]
                for j in range(8):
                    part, tb = j // 4, j % 4
                    if j == 0:
                        pe.wait_ge(sem("short_conv_done"), nth(pe, "short_conv_done"))
                    if j >= 2:
                        pe.wait_ge(sem("natural_copied"), nth(pe, "natural_copied"))
                    for c in range(4):
                        last = nc.tensor.transpose(bank(j % 2)[:, c * P:(c + 1) * P],
                                                   proj[:, (C_HU + part * 4 + c) * 512 + tb * P:][:, 0:P], K(K_ID))
                    last.then_inc(sem("natural_ready"), 1)
                pe.wait_ge(sem("natural_copied"), nth(pe, "natural_copied", 2))
                for o in range(2):
                    for s in range(2):
                        z = nat[:, s * 1024:(s + 1) * 1024]
                        if o == 1 and s == 0:
                            pe.wait_ge(sem("hyena_z_ready"), nth(pe, "hyena_z_ready"))
                        for m in range(2):
                            for cs in range(2):
                                for tb in range(2):
                                    last = mm(bank(2 * m + cs), arena[:, 4096 + cs * 512 + tb * S + m * P:][:, 0:P],
                                              z[:, tb * 512:(tb + 1) * 512], tb == 0, tb == 1)
                        last.then_inc(sem("z_spectrum_ready"), 1)
                        pe.wait_ge(sem("y_spectrum_ready"), nth(pe, "y_spectrum_ready"))
                        Y = hT[:, s * 2048:(s + 1) * 2048]
                        if o == 0:
                            if s:
                                pe.wait_ge(sem("hyena_z_ready"), nth(pe, "hyena_z_ready"))
                            for tb in range(2):
                                for j in range(4):
                                    kc, cs = j // 2, j % 2
                                    last = mm(bank(4 + tb), arena[:, 5120 + cs * 512 + kc * S + tb * P:][:, 0:P],
                                              Y[:, j * 512:(j + 1) * 512], j == 0, j == 3)
                        else:
                            if s:
                                pe.wait_ge(sem("hyena_y_done"), nth(pe, "hyena_y_done"))
                            for c in range(4):
                                for j in range(4):
                                    kc, cs = j // 2, j % 2
                                    last = mm(bank(4 + c // 2)[:, (c % 2) * S:(c % 2 + 1) * S],
                                              Y[:, j * 512 + c * P:j * 512 + (c + 1) * P],
                                              arena[:, 5120 + cs * 512 + kc * S:][:, 0:S], j == 0, j == 3)
                        last.then_inc(sem("hyena_inverse_ready"), 1)
                pe.wait_ge(sem("hyena_y_done"), nth(pe, "hyena_y_done"))

            def attend(layer):
                us = attention_units(layer)
                n = len(us)
                first_pv = pv_count[0]
                for i in range(n + 3):
                    if i < n:
                        u = us[i]
                        if i >= 2:
                            pe.wait_ge(sem("probs_scaled_exp"), nth(pe, "probs_scaled_exp"))
                        if u["kind"] == "plain":
                            last = mm(bank(i % 2)[:, 0:u["keys"]], u["q"], u["k"], True, True)
                        else:
                            mm(bank(i % 2)[:, 0:S], u["q"], u["k"][:, 0:S], True, True)
                            last = mm(bank(6 + i % 2)[:, 0:S], u["q"], u["k"][:, S:512], True, True)
                        last.then_inc(sem("scores_ready"), 1)
                    if 2 <= i < n + 2:
                        u = us[i - 2]
                        pe.wait_ge(sem("probs_ready"), nth(pe, "probs_ready"))
                        for c in range(u["keys"] // P):
                            last = nc.tensor.transpose(bank(2 + i % 2)[:, c * P:(c + 1) * P],
                                                       probs(i - 2)[:, c * P:(c + 1) * P], K(K_ID))
                        last.then_inc(sem("probs_turned"), 1)
                    if i >= 3:
                        j = i - 3
                        u = us[j]
                        pe.wait_ge(sem("probsT_ready"), nth(pe, "probsT_ready"))
                        if j >= 2:
                            pe.wait_ge(sem("o_gated"), nth(pe, "o_gated"))
                        o = bank(4 + j % 2)[u["half"] * 64:u["half"] * 64 + 64, 0:P]
                        nch = u["keys"] // P
                        for c in range(nch):
                            last = mm(o, u["v"](c), probsT(j)[:, c * P:(c + 1) * P], c == 0, c == nch - 1)
                        last.then_inc(sem("o_ready"), 1)
                pe.wait_ge(sem("o_gated"), nth(pe, "o_gated", 2))
                nth(pe, "probs_scaled_exp", 2)

            def out2(layer):
                n = 512 if layer == 0 else S
                pe.wait_ge(sem("y2_ready"), nth(pe, "y2_ready"))
                for j in range(OUTP):
                    q = take()
                    for m in range(2):
                        for k in range(KD):
                            last = mm(bank(2 * j + m)[:, 0:n], slot(q, k * 256 + m * P, k * 256 + (m + 1) * P),
                                      y3[:, k, 0:n], k == 0, k == KD - 1)
                    last.then_inc(DONE, 1)

            pv_count = [0]
            hyena_filters()
            for layer in range(2):
                adaln()
                project2(layer)
                qk_norm(layer)
                if layer == 0:
                    hyena()
                attend(layer)
                out2(layer)

        @block.scalar
        def _(act):
            chain = [0]

            def step(ins):
                chain[0] += 1
                ins.then_inc(sem("scalar_steps"), 1)
                act.wait_ge(sem("scalar_steps"), chain[0])

            def f(o, i, fn, **kw):
                return nc.scalar.activation(o, i, fn, **kw)

            panel = [0]

            def multiplied(k):
                panel[0] += k
                act.wait_ge(DONE, panel[0])

            def norm(first=False, streams=1, between=None):
                if first:
                    act.wait_ge(sem("inputs_landed"), 48)
                else:
                    act.wait_ge(sem("x_done"), nth(act, "x_done"))
                if streams == 2:
                    act.wait_ge(sem("context_landed"), 16)
                    step(f(h3[:, :, 0:S], x3, ACT.Square))
                    f(h3[:, :, S:512], c3, ACT.Square).then_inc(sem("squares_ready"), 1)
                else:
                    f(h3[:, :, 0:S], x3, ACT.Square).then_inc(sem("squares_ready"), 1)
                if between:
                    between()
                act.wait_ge(sem("mean_square_ready"), nth(act, "mean_square_ready"))
                n = streams * S
                f(rstd[:, 0:n], bank(0)[:, 0:n], ACT.Sqrt, bias=eps1).then_inc(sem("root_ready"), 1)

            def wide_part(p):
                act.wait_ge(LANDED[p % RING], 16 * (p // RING + 1))
                if p > 2:
                    act.wait_ge(DONE, p - 2)
                f(wide_high(p, 0, PW), ring[:, (p % RING) * PW:(p % RING + 1) * PW], ACT.Copy) \
                    .then_inc(sem("wide_panel_high"), 1)

            def half_parts(j):
                f(h_parts[:, 4 * j:4 * j + 4, S:512], h3[:, 4 * j:4 * j + 4, 0:S], ACT.Copy) \
                    .then_inc(sem("h_parts_high"), 1)

            def project1():
                p0 = panel[0]
                for j in range(2):
                    act.wait_ge(sem("h_ready"), nth(act, "h_ready", 4))
                    half_parts(j)
                wide_part(p0 + 1)
                wide_part(p0 + 2)
                for p in range(IN1):
                    multiplied(1)
                    if p + 3 < IN1:
                        wide_part(p0 + p + 3)
                    if p % 2 == 0:
                        o = proj[:, p * 512:(p + 1) * 512]
                        f(o, bank(p % 8), ACT.Copy, scale=0.125 if p * 2 in (SQ, SQ + 2) else 1.0) \
                            .then_inc(sem("proj_even_copied"), 1)

            def mix_out():
                p0 = panel[0]
                wide_part(p0 + 2)
                wide_part(p0 + 3)
                wide_part(p0 + 4)
                for j in range(2):
                    act.wait_ge(sem("mixed_ready"), nth(act, "mixed_ready"))
                    half_parts(j)
                    if j == 0:
                        wide_part(p0 + 5)
                        wide_part(p0 + 6)
                wide_part(p0 + 7)
                panel[0] += 2 * OUTP

            def hgrn(layer):
                q, kk = arena[:, 0:1024], arena[:, 1024:2048]
                e0 = arena[:, 3072:4096]
                E = [e0, arena[:, 4096:5120]]
                act.wait_ge(sem("proj_even_copied"), 11 * (layer + 1))
                act.wait_ge(sem("proj_odd_copied"), 11 * (layer + 1))
                step(f(q, proj[:, HQ * S:(HQ + 4) * S], ACT.Silu))
                f(proj[:, HOG * S:(HOG + 4) * S], proj[:, HOG * S:(HOG + 4) * S], ACT.Silu) \
                    .then_inc(sem("q_silu_ready"), 1)
                act.wait_ge(sem("forget_abs_ready"), nth(act, "forget_abs_ready"))
                step(f(e0, e0, ACT.Exp))
                if layer == 1:
                    step(f(lbs[:, 4:8], lbs[:, 4:8], ACT.Exp))
                    step(f(lbs[:, 4:8], lbs[:, 4:8], ACT.Ln, bias=ones1))
                f(e0, e0, ACT.Ln, bias=ones1).then_inc(sem("forget_log_ready"), 1)
                act.wait_ge(sem("key_exponent_ready"), nth(act, "key_exponent_ready"))
                f(kk, e0, ACT.Exp).then_inc(sem("hgrn_key_ready"), 1)
                if layer == 1:
                    act.wait_ge(sem("forget_abs_ready"), nth(act, "forget_abs_ready"))
                    step(f(e0, e0, ACT.Exp))
                    f(e0, e0, ACT.Ln, bias=ones1).then_inc(sem("forget_log_ready"), 1)
                for lv in range(8):
                    act.wait_ge(sem("level_exponent_ready"), nth(act, "level_exponent_ready"))
                    v = E[lv % 2].rearrange("p (n two b) -> p n two b", two=2, b=1 << lv)
                    f(v[:, :, 1, :], v[:, :, 1, :], ACT.Exp)
                    f(v[:, :, 0, :], v[:, :, 0, :], ACT.Exp, scale=-1.0).then_inc(sem("level_decay_ready"), 1)
                act.wait_ge(sem("level_scores_ready"), nth(act, "level_scores_ready", 9))
                f(arena[:, 8192:8704], bank(4), ACT.Copy).then_inc(sem("cross_copied"), 1)
                act.wait_ge(sem("hgrn_o_ready"), nth(act, "hgrn_o_ready"))
                f(e0, bank(5, 2), ACT.Square).then_inc(sem("hgrn_o_squared"), 1)
                act.wait_ge(sem("hgrn_mean_square_ready"), nth(act, "hgrn_mean_square_ready"))
                f(E[1][:, 0:512], bank(4), ACT.Sqrt, bias=eps1)
                f(E[1][:, 512:1024], bank(7), ACT.Sqrt, bias=eps1).then_inc(sem("hgrn_root_ready"), 1)
                f(proj[:, GA * S:(GA + 16) * S], proj[:, GA * S:(GA + 16) * S], ACT.Sigmoid) \
                    .then_inc(sem("gates_ready"), 1)

            def stick():
                act.wait_ge(sem("hgrn_done"), nth(act, "hgrn_done"))
                f(y_parts[:, 0:4, S:512], y3[:, 0:4, 0:S], ACT.Copy).then_inc(sem("y_parts_high"), 1)
                for g in range(2):
                    L = arena[:, g * 3072:g * 3072 + 1536]
                    W = arena[:, g * 3072 + 1536:(g + 1) * 3072]
                    act.wait_ge(sem("stick_z_ready"), nth(act, "stick_z_ready"))
                    step(f(L.rearrange("p (h t) -> p h t", h=4), ps[:, 0:4, 0:384], ACT.Abs))
                    step(f(L, L, ACT.Exp, scale=-1.0))
                    f(L, L, ACT.Ln, bias=ones1).then_inc(sem("stick_log_ready"), 1)
                    act.wait_ge(sem("stick_exponent_ready"), nth(act, "stick_exponent_ready"))
                    f(W, W, ACT.Exp).then_inc(sem("stick_exp_ready"), 1)
                    wide_part(panel[0] + g)
                    act.wait_ge(sem("stick_o_ready"), nth(act, "stick_o_ready"))
                    f(y_parts[:, 4 + 2 * g:6 + 2 * g, S:512], bank(4 + g).rearrange("p (c n) -> p c n", c=2),
                      ACT.Copy).then_inc(sem("y_parts_high"), 1)

            def ffn(p0, e=0):
                sg = [arena[:, 0:512], arena[:, 512:1024]]

                def silu(p, f_, more):
                    act.wait_ge(DONE, more + (p + 1))
                    f(sg[f_ % 2], bank(f_ % 2), ACT.Silu).then_inc(sem("gate_silu_ready"), 1)

                silu(p0, 0, e * FFN)
                with act.Fori(0, FSTEP // 2 - 1) as i:
                    silu(p0 + 2, 1, e * FFN + i * 6)
                    silu(p0 + 5, 0, e * FFN + i * 6)
                silu(p0 + 38, 1, e * FFN)

            def high_part(p, before, rounds):
                act.wait_ge(LANDED[p % RING], rounds * 16 + 16 * (p // RING + 1))
                act.wait_ge(DONE, before + (p - 2))
                f(split(W_high, p, 0, PW), ring[:, (p % RING) * PW:(p % RING + 1) * PW], ACT.Copy) \
                    .then_inc(sem("panel_high"), 1)

            def silu_and_high(p0, e, before, n, src, made):
                sg = [arena[:, 0:n], arena[:, 512:512 + n]]
                eF, eR = e * FFN, e * (FFN // RING)

                def silu(p, f_, more):
                    act.wait_ge(DONE, more + (p + 1))
                    f(sg[f_ % 2], bank(f_ % 2)[:, 0:n], ACT.Silu).then_inc(sem("gate_activated"), 1)

                def hidden(f_, count):
                    act.wait_ge(sem(made), count)
                    a = (f_ % 2) * 512
                    f(hid_high[:, a:a + n], src(f_), ACT.Copy).then_inc(sem("hidden_high"), 1)

                silu(p0, 0, eF)
                for p in range(2, 5):
                    high_part(p0 + p, eF, eR)
                with act.Fori(0, FSTEP // 2 - 1) as i:
                    for j in range(1, 3):
                        silu(p0 + 3 * j - 1, j, eF + i * 6)
                        hidden(j - 1, before + i * 2 + j)
                        for p in range(3 * j + 2, 3 * j + 5):
                            high_part(p0 + p, eF + i * 6, eR + i)
                silu(p0 + 38, 1, eF)
                hidden(0, before + (FSTEP - 1))
                high_part(p0 + 41, eF, eR)
                hidden(1, before + FSTEP)

            def dense_layer(p0):
                for k in range(KD):
                    act.wait_ge(sem("h_ready"), nth(act, "h_ready"))
                    f(h_high[:, k * S:(k + 1) * S], h3[:, k, 0:S], ACT.Copy).then_inc(sem("h_high_ready"), 1)
                high_part(p0 + 1, 0, 0)
                hb = [arena[:, 1024:1536], arena[:, 1536:2048]]
                silu_and_high(p0, 0, 0, 512, lambda f_: hb[f_ % 2], "hidden_made")

            def compact_expert(p0, e):
                act.wait_ge(sem("tokens_gathered"), e + 1)
                f(xe_high[:, :], bank(2, 2), ACT.Copy).then_inc(sem("tokens_high"), 1)
                high_part(p0 + 1, e * FFN, e * (FFN // RING))
                silu_and_high(p0, e, e * FSTEP, 256, lambda f_: bank(6)[:, 0:S], "hidden_turned")
                high_part(p0 + FFN, e * FFN, e * (FFN // RING))
                act.wait_ge(DONE, e * FFN + (p0 + FFN))
                f(yS, bank(4, 2), ACT.Copy).then_inc(sem("rows_copied"), 1)

            for layer in range(2):
                norm(first=layer == 0, between=lambda: wide_part(panel[0]))
                project1()
                hgrn(layer)
                stick()
                mix_out()
                norm(between=None if layer else lambda: high_part(panel[0], 0, 0))
                if layer == 0:
                    dense_layer(panel[0])
                    panel[0] += FFN
                else:
                    act.wait_ge(sem("router_max_ready"), nth(act, "router_max_ready"))
                    for tb in range(2):
                        ins = f(rt[:, 16 + 8 * tb:24 + 8 * tb], rt[:, 8 * tb:8 * tb + 8], ACT.Exp,
                                bias=rt[:, 34 + tb:35 + tb])
                        if tb == 0:
                            step(ins)
                    ins.then_inc(sem("router_exp_ready"), 1)
                    act.wait_ge(sem("h_turned"), nth(act, "h_turned"))
                    f(hN, bank(0, 4), ACT.Copy).then_inc(sem("h_tokens_copied"), 1)
                    act.wait_ge(sem("slot_weights_ready"), nth(act, "slot_weights_ready"))
                    f(G[:, S:], bank(4, 4), ACT.Copy).then_inc(sem("slot_weights_copied"), 1)
                    act.wait_ge(sem("crowded_ready"), nth(act, "crowded_ready"))
                    many = act.value_load(crowded[0:1, 0:1], min_val=0, max_val=1)
                    with act.If(many == 1):
                        with act.Fori(0, E) as e:
                            ffn(panel[0], e)
                    with act.Else():
                        high_part(panel[0], 0, 0)
                        with act.Fori(0, E) as e:
                            compact_expert(panel[0], e)
                    panel[0] += E * FFN
            norm()

            act.wait_ge(sem("combine_free"), nth(act, "combine_free"))
            act.dma_start(proj[0:64, 0:2048], w3_in).then_inc(sem("filter_tables_landed"), 16)
            act.dma_start(proj[0:33, 2048:2304], pos_in).then_inc(sem("filter_tables_landed"), 16)
            act.dma_start(proj[0:33, 2816:2880], w1_in).then_inc(sem("filter_tables_landed"), 16)
            act.dma_start(proj[0:64, 2880:2944], w2_in).then_inc(sem("filter_tables_landed"), 16)
            act.dma_start(proj[:, 8192:9216], decay_in).then_inc(sem("filter_tables_landed"), 16)
            act.dma_start(proj[:, 11776:12800], skip_in.partition_broadcast(P)) \
               .then_inc(sem("filter_tables_landed"), 16)
            act.dma_start(arena[:, 4096:6144], dft_in).then_inc(sem("filter_tables_landed"), 16)
            f(cond[:, :], sml[:, S_COND:S_COND + 16], ACT.Silu).then_inc(sem("cond_ready"), 1)

            def hyena_filters():
                for _ in range(2):
                    act.wait_ge(sem("filter_phase_ready"), nth(act, "filter_phase_ready"))
                    src = proj[0:64, 2944:3200]
                    dst = proj[0:64, 2304:2560] if _ == 0 else proj[0:64, 2560:2816]
                    f(dst, src, ACT.Sin).then_inc(sem("filter_hidden_ready"), 1)
                for o in range(2):
                    act.wait_ge(sem("taps_ready"), nth(act, "taps_ready"))
                    f(proj[:, 9216:11264], proj[:, 4096:6144], ACT.Square).then_inc(sem("taps_squared"), 1)
                    act.wait_ge(sem("taps_energy_ready"), nth(act, "taps_energy_ready"))
                    f(proj[:, 11264:11776], bank(4), ACT.Sqrt, bias=eps1).then_inc(sem("taps_root_ready"), 1)

            def narrow_part(p0, p):
                q = p0 + p
                act.wait_ge(LANDED[q % RING], 16 * (q // RING + 1))
                act.wait_ge(DONE, q - 1)
                f(N_high[p % 2], ring[:, (q % RING) * PW:(q % RING + 1) * PW], ACT.Copy) \
                    .then_inc(sem("wide_panel_high"), 1)

            def project2(layer):
                p0 = panel[0]
                narrow_part(p0, 1)
                act.wait_ge(sem("ada_turned"), nth(act, "ada_turned"))
                narrow_part(p0, 0)
                for k in range(KD):
                    for s in range(2):
                        act.wait_ge(sem("h_scaled"), nth(act, "h_scaled"))
                        f(y_parts[:, k, s * S:(s + 1) * S], h3[:, k, s * S:(s + 1) * S], ACT.Identity,
                          bias=ada[:, 2 * k + s:2 * k + s + 1]).then_inc(sem("h_mod_high"), 1)
                for p in range(IN2):
                    multiplied(1)
                    if p + 2 < IN2:
                        narrow_part(p0, p + 2)
                    b = 2 * (p % 4)
                    wide = layer == 0 or p in (2, 5, 6, 7, 8)
                    o = proj[:, 2 * p * 512:(2 * p + 2) * 512]
                    i = bank(b, 2)
                    if not wide:
                        o = o.rearrange("q (a n) -> q a n", a=2)[:, :, 0:S]
                        i = i.rearrange("q (a n) -> q a n", a=2)[:, :, 0:S]
                    f(o, i, ACT.Copy).then_inc(sem("pair_copied"), 1)

            def qk_norm(layer):
                act.wait_ge(sem("pair_copied"), IN2 * (layer + 1))
                chunks = qk_chunks(layer)

                def square(i):
                    c, n = chunks[i][0:2]
                    f(arena[:, 6144 + (i % 2) * 512:][:, 0:n], proj[:, c * 512:c * 512 + n], ACT.Square) \
                        .then_inc(sem("qk_squared"), 1)

                square(0)
                square(1)
                for i, (c, n, g, rope) in enumerate(chunks):
                    if i >= 2:
                        act.wait_ge(sem("qk_normed"), nth(act, "qk_normed"))
                    act.wait_ge(sem("qk_mean_square"), nth(act, "qk_mean_square"))
                    f(qk_root(i)[:, 0:n], bank(i % 2)[:, 0:n], ACT.Sqrt, bias=eps1).then_inc(sem("qk_root_ready"), 1)
                    if i + 2 < len(chunks):
                        square(i + 2)
                act.wait_ge(sem("qk_normed"), nth(act, "qk_normed", 2))
                n = 512 if layer == 0 else S
                gates = proj[:, C_G * 512:(C_G + 8) * 512].rearrange("p (c n) -> p c n", c=8)[:, :, 0:n]
                f(gates, gates, ACT.Silu).then_inc(sem("y_gates_ready"), 1)

            def hyena():
                nat = yT[:, :]
                for j in range(8):
                    act.wait_ge(sem("natural_ready"), nth(act, "natural_ready"))
                    f(nat[:, j * 512:(j + 1) * 512], bank(j % 2), ACT.Copy).then_inc(sem("natural_copied"), 1)

            def attend(layer):
                us = attention_units(layer)
                n = len(us)

                def turned_copy(j):
                    act.wait_ge(sem("probs_turned"), nth(act, "probs_turned"))
                    if j >= 2:
                        act.wait_ge(sem("o_ready"), nth(act, "o_ready"))
                    kk = us[j]["keys"]
                    f(probsT(j)[:, 0:kk], bank(2 + j % 2)[:, 0:kk], ACT.Copy).then_inc(sem("probsT_ready"), 1)

                for i in range(n + 2):
                    if i < n:
                        u = us[i]
                        pr = probs(i)
                        acc = stat[:, 8 + i % 4:9 + i % 4]
                        nm = stat[:, 4 + i % 4:5 + i % 4]
                        if u["kind"] != "plain":
                            act.wait_ge(sem("scores_ready"), nth(act, "scores_ready"))
                            if i >= 2:
                                act.wait_ge(sem("probs_scaled_exp"), exps[0] - 1)
                            f(scores_sb(i)[:, S:512], bank(6 + i % 2)[:, 0:S], ACT.Copy, scale=0.125) \
                                .then_inc(sem("context_scores_ready"), 1)
                            if i >= 2:
                                turned_copy(i - 2)
                            act.wait_ge(sem("max_ready"), nth(act, "max_ready"))
                            w = 513 if u["kind"] == "window" else 512
                            f(pr[:, 0:w], scores_sb(i)[:, 0:w], ACT.Exp, bias=nm, accum_out=acc) \
                                .then_inc(sem("probs_scaled_exp"), 1)
                        else:
                            nth(act, "scores_ready")
                            act.wait_ge(sem("max_ready"), nth(act, "max_ready"))
                            f(pr[:, 0:u["keys"]], bank(i % 2)[:, 0:u["keys"]], ACT.Exp, bias=nm, scale=0.125,
                              accum_out=acc).then_inc(sem("probs_scaled_exp"), 1)
                            if i >= 2:
                                turned_copy(i - 2)
                        exps[0] += 1
                    else:
                        turned_copy(i - 2)
                act.wait_ge(sem("o_ready"), nth(act, "o_ready", 2))

            exps = [0]
            hyena_filters()
            for layer in range(2):
                panel[0] += ADA
                if layer == 1:
                    act.wait_ge(sem("y2_ready"), nth(act, "y2_ready"))
                    for h in range(8):
                        for r in range(4):
                            src = bass.AP(rpb_in.tensor, h * 465 + (7 - r) * 31 + 15 - 63, [[1, 64], [31, 4], [1, 64]])
                            dst = arena[(r % 2) * 64:(r % 2) * 64 + 64, (h * 2 + r // 2) * S:(h * 2 + r // 2 + 1) * S]
                            act.dma_start(dst.rearrange("p (a b) -> p a b", a=4), src) \
                               .then_inc(sem("position_bias_landed"), 16)
                norm(streams=2)
                act.wait_ge(DONE, panel[0])
                f(arena[0:2, 6144:9216], ps[0:2, 1:7, :].rearrange("p b n -> p (b n)"), ACT.Copy) \
                    .then_inc(sem("ada_rows_copied"), 1)
                project2(layer)
                qk_norm(layer)
                if layer == 0:
                    hyena()
                attend(layer)
                panel[0] += OUTP
            act.wait_ge(sem("x_done"), nth(act, "x_done", 1))
            act.dma_start(out, xT[:, :]).then_inc(sem("out_stored"), 16)
            act.wait_ge(sem("out_stored"), 16)

        @block.gpsimd
        def _(pool):
            pool.memset(zrow[:, :], 0.0).then_inc(sem("accumulators_free"), 1)
            for layer in range(2):
                k = arena[:, 1024:2048]
                for lv in range(8):
                    pool.wait_ge(sem("level_decay_ready"), nth(pool, "level_decay_ready"))
                    if lv == 0:
                        pool.wait_ge(sem("hgrn_key_ready"), nth(pool, "hgrn_key_ready"))
                    if lv >= 2:
                        pool.wait_ge(sem("level_scores_ready"), nth(pool, "level_scores_ready", 2 if lv == 2 else 1))
                    E = arena[:, 3072 + (lv % 2) * 1024:][:, 0:1024]
                    X = arena[:, 5120 + (lv % 2) * 1024:][:, 0:1024]
                    v = lambda a: a.rearrange("p (n two b) -> p n two b", two=2, b=1 << lv)[:, :, 0, :]
                    pool.tensor_tensor(v(X), v(k), v(E), ALU.mult).then_inc(sem("level_k_ready"), 1)
                seen[(pool.engine, "level_scores_ready")] += 2
            for o in range(2):
                pool.wait_ge(sem("taps_ready"), nth(pool, "taps_ready"))
                if o:
                    pool.wait_ge(sem("spectrum_sum"), nth(pool, "spectrum_sum"))
                a = proj[:, 4096:6144].rearrange("p (tb d n) -> p tb d n", tb=2, d=2)
                hp = proj[:, 6144:7168].rearrange("p (tb n) -> p tb n", tb=2)
                hm = proj[:, 7168:8192].rearrange("p (tb n) -> p tb n", tb=2)
                pool.tensor_tensor(hp, a[:, :, 0, :], a[:, :, 1, :], ALU.add)
                pool.tensor_tensor(hm, a[:, :, 0, :], a[:, :, 1, :], ALU.subtract).then_inc(sem("taps_combined"), 1)

        @block.vector
        def _(dve):
            chain = [0]

            def step(ins):
                chain[0] += 1
                ins.then_inc(sem("vector_steps"), 1)
                dve.wait_ge(sem("vector_steps"), chain[0])

            V = nc.vector
            panel = [0]

            def multiplied(k):
                panel[0] += k
                dve.wait_ge(DONE, panel[0])

            def signal(ins, name):
                ins.then_inc(sem(name), 1)
                made[name] = made.get(name, 0) + 1
                dve.wait_ge(sem(name), made[name])

            made = {}

            def announce(name):
                dve.sem_inc(sem(name), 1)
                made[name] = made.get(name, 0) + 1

            def norm(col, out3=None, name="h_ready", between=None):
                if between:
                    between()
                dve.wait_ge(sem("root_ready"), nth(dve, "root_ready"))
                step(V.reciprocal(rstd[:, 0:S], rstd[:, 0:S]))
                for k in range(KD):
                    o = h3[:, k, 0:S] if out3 is None else out3[:, k, :]
                    ins = V.scalar_tensor_tensor(o, x3[:, k, :], sml[:, col + k:col + k + 1], rstd[:, 0:S],
                                                 ALU.mult, ALU.mult)
                    if out3 is None:
                        signal(ins, name)
                    elif k < KD - 1:
                        step(ins)
                    else:
                        signal(ins, name)

            def wide_part(p):
                dve.wait_ge(sem("wide_panel_high"), nth(dve, "wide_panel_high"))
                V.tensor_tensor(wide_low(p, 0, PW), ring[:, (p % RING) * PW:(p % RING + 1) * PW],
                                wide_high(p, 0, PW).bitcast(F32), ALU.subtract).then_inc(sem("wide_panel_split"), 1)

            def half_parts(j):
                dve.wait_ge(sem("h_parts_high"), nth(dve, "h_parts_high"))
                V.tensor_tensor(h_parts[:, 4 * j:4 * j + 4, 0:S], h3[:, 4 * j:4 * j + 4, 0:S],
                                h_parts[:, 4 * j:4 * j + 4, S:512].bitcast(F32), ALU.subtract) \
                    .then_inc(sem("h_parts_ready"), 1)

            def project1():
                p0 = panel[0]
                for j in range(2):
                    half_parts(j)
                wide_part(p0 + 1)
                wide_part(p0 + 2)
                for p in range(IN1):
                    if p + 3 < IN1:
                        wide_part(p0 + p + 3)
                    if p % 2 == 1:
                        multiplied(2)
                        o = proj[:, p * 512:(p + 1) * 512]
                        V.tensor_scalar(o, bank(p % 8), 0.125 if p * 2 in (SQ, SQ + 2) else 1.0, None, ALU.mult) \
                            .then_inc(sem("proj_odd_copied"), 1)

            def hgrn(layer):
                q, kk, b = arena[:, 0:1024], arena[:, 1024:2048], arena[:, 2048:3072]
                e0, lf = arena[:, 3072:4096], arena[:, 4096:5120]
                E = [e0, lf]
                sc, cross = arena[:, 7168:8192], arena[:, 8192:8704]
                z = proj[:, HF * S:(HF + 4) * S]
                heads = lambda a: a.rearrange("p (h t) -> p h t", h=4)
                dve.wait_ge(sem("proj_even_copied"), 11 * (layer + 1))
                dve.wait_ge(sem("proj_odd_copied"), 11 * (layer + 1))
                if layer == 1:
                    step(V.tensor_tensor(lbs[:, 0:4], sml[:, S_LB + 4:S_LB + 8], sml[:, S_LB:S_LB + 4], ALU.subtract))
                    step(V.scalar_tensor_tensor(lbs[:, 4:8], lbs[:, 0:4], -1.0, lbs[:, 0:4], ALU.mult, ALU.min))
                signal(V.scalar_tensor_tensor(e0, z, -1.0, z, ALU.mult, ALU.min), "forget_abs_ready")
                step(V.memset(sc, 0.0))
                dve.wait_ge(sem("forget_log_ready"), nth(dve, "forget_log_ready"))
                step(V.scalar_tensor_tensor(lf, z, 0.0, e0, ALU.min, ALU.subtract))
                if layer == 0:
                    signal(V.tensor_tensor(e0, lf, z, ALU.subtract), "key_exponent_ready")
                else:
                    step(V.scalar_tensor_tensor(lbs[:, 8:12], lbs[:, 0:4], 0.0, lbs[:, 4:8], ALU.min, ALU.subtract))
                    step(V.tensor_tensor(lbs[:, 12:16], lbs[:, 8:12], lbs[:, 0:4], ALU.subtract))
                    rest = lbs[:, 12:16].unsqueeze(2).to_broadcast([P, 4, S])
                    step(V.tensor_tensor(e0, lf, z, ALU.subtract))
                    signal(V.tensor_tensor(heads(e0), heads(e0), rest, ALU.add), "key_exponent_ready")
                    less = lbs[:, 0:4].unsqueeze(2).to_broadcast([P, 4, S])
                    step(V.tensor_tensor(heads(lf), heads(lf), less, ALU.subtract))
                    dve.wait_ge(sem("hgrn_key_ready"), nth(dve, "hgrn_key_ready"))
                    signal(V.scalar_tensor_tensor(e0, lf, -1.0, lf, ALU.mult, ALU.min), "forget_abs_ready")
                    dve.wait_ge(sem("forget_log_ready"), nth(dve, "forget_log_ready"))
                    step(V.scalar_tensor_tensor(lf, lf, 0.0, e0, ALU.max, ALU.add))
                    log_lb = lbs[:, 8:12].unsqueeze(2).to_broadcast([P, 4, S])
                    step(V.tensor_tensor(heads(lf), heads(lf), log_lb, ALU.add))
                for h in range(4):
                    step(V.tensor_tensor_scan(b[:, h * S:(h + 1) * S], ones1.to_broadcast([P, S]),
                                              lf[:, h * S:(h + 1) * S], 0.0, ALU.mult, ALU.add))
                if layer == 0:
                    dve.wait_ge(sem("hgrn_key_ready"), nth(dve, "hgrn_key_ready"))
                dve.wait_ge(sem("q_silu_ready"), nth(dve, "q_silu_ready"))
                announce("hgrn_qk_ready")

                def merge(lv):
                    dve.wait_ge(sem("level_scores_ready"), nth(dve, "level_scores_ready"))
                    if lv == 7:
                        return
                    m = K(K_ID) if lv < 0 else K(K_LEV + lv * P)
                    m = m.bitcast(I32).unsqueeze(1).to_broadcast([P, 8, P])
                    i = bank(0 if lv % 2 else 2, 2).rearrange("p (h t) -> p h t", h=8)
                    signal(V.copy_predicated(sc.rearrange("p (h t) -> p h t", h=8), m, i), "level_merged")

                for lv in range(8):
                    B = 1 << lv
                    if lv >= 2:
                        dve.wait_ge(sem("level_k_ready"), nth(dve, "level_k_ready"))
                    v = lambda a: a.rearrange("p (n m) -> p n m", m=2 * B)
                    signal(V.tensor_tensor(v(E[lv % 2]), v(b), v(b)[:, :, B - 1:B].to_broadcast([P, 512 // B, 2 * B]),
                                           ALU.subtract), "level_exponent_ready")
                    if lv >= 1:
                        merge(lv - 2)
                    dve.wait_ge(sem("level_decay_ready"), nth(dve, "level_decay_ready"))
                    w = lambda a: a.rearrange("p (n two b) -> p n two b", two=2, b=B)[:, :, 1, :]
                    X = arena[:, 5120 + (lv % 2) * 1024:][:, 0:1024]
                    signal(V.tensor_tensor(w(X), w(q), w(E[lv % 2]), ALU.mult), "level_q_ready")
                seen[(dve.engine, "level_k_ready")] += 2
                merge(6)
                merge(7)
                dve.wait_ge(sem("cross_copied"), nth(dve, "cross_copied"))
                announce("hgrn_scores_merged")
                dve.wait_ge(sem("hgrn_root_ready"), nth(dve, "hgrn_root_ready"))
                step(V.reciprocal(lf, lf))
                for j in range(2):
                    t = arena[:, 2048 + j * 512:2048 + (j + 1) * 512]
                    step(V.scalar_tensor_tensor(t, bank(5 + j), sml[:, S_ON + layer:S_ON + layer + 1],
                                                lf[:, j * 512:(j + 1) * 512],
                                                ALU.mult, ALU.mult))
                    g = proj[:, HOG * S + j * 512:HOG * S + (j + 1) * 512]
                    ins = V.tensor_tensor(y3[:, 2 * j:2 * j + 2, 0:S], t.rearrange("p (a n) -> p a n", a=2),
                                          g.rearrange("p (a n) -> p a n", a=2), ALU.mult)
                    if j == 0:
                        step(ins)
                    else:
                        signal(ins, "o_a_ready")
                announce("hgrn_done")

            def stick():
                dve.wait_ge(sem("y_parts_high"), nth(dve, "y_parts_high"))
                V.tensor_tensor(y_parts[:, 0:4, 0:S], y3[:, 0:4, 0:S], y_parts[:, 0:4, S:512].bitcast(F32),
                                ALU.subtract).then_inc(sem("y_parts_ready"), 1)
                strict = K(K_STRICT).unsqueeze(1).to_broadcast([P, 4, P])
                for g in range(2):
                    L = arena[:, g * 3072:g * 3072 + 1536]
                    W = arena[:, g * 3072 + 1536:(g + 1) * 3072]
                    v = lambda a: a.rearrange("p (h t) -> p h t", h=4)
                    z = ps[:, 0:4, 0:384]
                    dve.wait_ge(sem("stick_log_ready"), nth(dve, "stick_log_ready"))
                    step(V.scalar_tensor_tensor(v(L), z, 0.0, v(L), ALU.max, ALU.add))
                    step(V.tensor_tensor(v(L)[:, :, 0:P], v(L)[:, :, 0:P], strict, ALU.mult))
                    signal(V.tensor_tensor(v(L)[:, :, S:384], v(L)[:, :, S:384], strict, ALU.mult),
                           "stick_softplus_ready")
                    dve.wait_ge(sem("stick_sums_ready"), nth(dve, "stick_sums_ready"))
                    signal(V.tensor_scalar(v(W), z, 0.0, None, ALU.min), "stick_exponent_ready")
                    dve.wait_ge(sem("stick_exp_ready"), nth(dve, "stick_exp_ready"))
                    step(V.tensor_tensor(v(W)[:, :, 0:P], v(W)[:, :, 0:P], strict, ALU.mult))
                    signal(V.tensor_tensor(v(W)[:, :, S:384], v(W)[:, :, S:384], strict, ALU.mult),
                           "stick_weights_ready")
                    wide_part(panel[0] + g)
                    dve.wait_ge(sem("y_parts_high"), nth(dve, "y_parts_high"))
                    V.tensor_tensor(y_parts[:, 4 + 2 * g:6 + 2 * g, 0:S],
                                    bank(4 + g).rearrange("p (c n) -> p c n", c=2),
                                    y_parts[:, 4 + 2 * g:6 + 2 * g, S:512].bitcast(F32), ALU.subtract) \
                        .then_inc(sem("y_parts_ready"), 1)

            def mix_out():
                dve.wait_ge(sem("gates_ready"), nth(dve, "gates_ready"))
                p0 = panel[0]
                wide_part(p0 + 2)
                wide_part(p0 + 3)
                wide_part(p0 + 4)
                for j in range(2):
                    multiplied(2)
                    ga = proj[:, GA * S + j * 1024:GA * S + (j + 1) * 1024]
                    gb = proj[:, GB * S + j * 1024:GB * S + (j + 1) * 1024]
                    step(V.tensor_tensor(ga, ga, bank(4 * j, 2), ALU.mult))
                    step(V.tensor_tensor(gb, gb, bank(4 * j + 2, 2), ALU.mult))
                    v = lambda a: a.rearrange("p (k n) -> p k n", k=4)
                    signal(V.tensor_tensor(h3[:, 4 * j:4 * j + 4, 0:S], v(ga), v(gb), ALU.add), "mixed_ready")
                    half_parts(j)
                    if j == 0:
                        wide_part(p0 + 5)
                        wide_part(p0 + 6)
                wide_part(p0 + 7)
                for j in range(OUTP):
                    multiplied(1)
                    o = xT[:, j * 512:(j + 1) * 512]
                    ins = V.tensor_tensor(o, o, bank(j), ALU.add)
                    if j < OUTP - 1:
                        step(ins)
                    else:
                        signal(ins, "x_done")

            def ffn(p0, e=0):
                sg = [arena[:, 0:512], arena[:, 512:1024]]
                hb = [arena[:, 1024:1536], arena[:, 1536:2048]]

                def gated(p, f, more, count):
                    dve.wait_ge(DONE, more + (p + 2))
                    dve.wait_ge(sem("gate_silu_ready"), count)
                    V.tensor_tensor(hb[f % 2], sg[f % 2], bank(2 + f % 2), ALU.mult).then_inc(sem("hidden_ready"), 1)

                gated(p0, 0, e * FFN, e * FSTEP + 1)
                with dve.Fori(0, FSTEP // 2 - 1) as i:
                    gated(p0 + 2, 1, e * FFN + i * 6, e * FSTEP + i * 2 + 2)
                    gated(p0 + 5, 0, e * FFN + i * 6, e * FSTEP + i * 2 + 3)
                gated(p0 + 38, 1, e * FFN, e * FSTEP + FSTEP)
                dve.wait_ge(DONE, e * FFN + (p0 + FFN))

            def low_part(p, count):
                dve.wait_ge(sem("panel_high"), count)
                V.tensor_tensor(split(W_low, p, 0, PW), ring[:, (p % RING) * PW:(p % RING + 1) * PW],
                                split(W_high, p, 0, PW).bitcast(F32), ALU.subtract).then_inc(sem("panel_split"), 1)

            def hidden_and_low(p0, more, first, before, n, src):
                sg = [arena[:, 0:n], arena[:, 512:512 + n]]
                hb = [arena[:, 1024:1024 + n], arena[:, 1536:1536 + n]]

                def hidden(p, f, more, count):
                    dve.wait_ge(DONE, more + (p + 2))
                    dve.wait_ge(sem("gate_activated"), count)
                    V.tensor_tensor(hb[f % 2], sg[f % 2], bank(2 + f % 2)[:, 0:n], ALU.mult) \
                        .then_inc(sem("hidden_made"), 1)

                def hidden_low(f, count):
                    dve.wait_ge(sem("hidden_high"), count)
                    a = (f % 2) * 512
                    V.tensor_tensor(hid_low[:, a:a + n], src(f), hid_high[:, a:a + n].bitcast(F32), ALU.subtract) \
                        .then_inc(sem("hidden_split"), 1)

                low_part(p0 + 2, first + 3)
                hidden(p0, 0, more, before + 1)
                low_part(p0 + 3, first + 4)
                low_part(p0 + 4, first + 5)
                with dve.Fori(0, FSTEP // 2 - 1) as i:
                    for j in range(1, 3):
                        hidden_low(j - 1, before + i * 2 + j)
                        low_part(p0 + 3 * j + 2, first + i * 6 + (3 * j + 3))
                        hidden(p0 + 3 * j - 1, j, more + i * 6, before + i * 2 + (j + 1))
                        low_part(p0 + 3 * j + 3, first + i * 6 + (3 * j + 4))
                        low_part(p0 + 3 * j + 4, first + i * 6 + (3 * j + 5))
                hidden_low(0, before + (FSTEP - 1))
                low_part(p0 + 41, first + 42)
                hidden(p0 + 38, 1, more, before + FSTEP)
                hidden_low(1, before + FSTEP)

            def dense_layer(p0):
                for k in range(KD):
                    dve.wait_ge(sem("h_high_ready"), nth(dve, "h_high_ready"))
                    V.tensor_tensor(h_low[:, k * S:(k + 1) * S], h3[:, k, 0:S], h_high[:, k * S:(k + 1) * S].bitcast(F32),
                                    ALU.subtract).then_inc(sem("h_split"), 1)
                low_part(p0 + 1, 2)
                hb = [arena[:, 1024:1536], arena[:, 1536:2048]]
                hidden_and_low(p0, 0, 0, 0, 512, lambda f: hb[f % 2])
                dve.wait_ge(DONE, p0 + FFN)

            dve.wait_ge(sem("inputs_landed"), 48)
            for layer in range(2):
                norm(S_MIX + layer * KD, between=lambda: wide_part(panel[0]))
                project1()
                hgrn(layer)
                stick()
                mix_out()
                norm(S_FFN + layer * KD, between=None if layer else lambda: low_part(panel[0], 1))
                if layer == 0:
                    dense_layer(panel[0])
                    panel[0] += FFN
                    for j in range(4):
                        o = xT[:, j * 512:(j + 1) * 512]
                        ins = V.tensor_tensor(o, o, bank(4 + j), ALU.add)
                        if j < 3:
                            step(ins)
                        else:
                            signal(ins, "x_done")
                    made["accumulators_free"] = 1
                    announce("accumulators_free")

            L = rt[:, 0:16]
            dve.wait_ge(sem("logits_ready"), nth(dve, "logits_ready"))
            signal(V.tensor_copy(L, bank(1)[:, 0:16]), "logits_copied")
            L3 = L.rearrange("p (t e) -> p t e", t=2)
            step(V.tensor_reduce(rt[:, 32:34], L3, AX.X, ALU.max))
            signal(V.tensor_scalar(rt[:, 34:36], rt[:, 32:34], -1.0, None, ALU.mult), "router_max_ready")
            for tb in range(2):
                l = rt[:, 8 * tb:8 * tb + 8]
                other = l.unsqueeze(1).to_broadcast([P, 8, 8])
                own = l.unsqueeze(2).to_broadcast([P, 8, 8])
                more = rt[:, 64:128].rearrange("p (a b) -> p a b", a=8)
                tie = rt[:, 128:192].rearrange("p (a b) -> p a b", a=8)
                low = K(K_LOW, 64).rearrange("p (a b) -> p a b", a=8)
                step(V.tensor_tensor(more, other, own, ALU.is_gt))
                step(V.tensor_tensor(tie, other, own, ALU.is_equal))
                step(V.tensor_tensor(tie, tie, low, ALU.mult))
                step(V.tensor_tensor(more, more, tie, ALU.add))
                step(V.tensor_reduce(rt[:, 40 + 8 * tb:48 + 8 * tb], more, AX.X, ALU.add))
            signal(V.tensor_scalar(rt[:, 40:56], rt[:, 40:56], 1.5, None, ALU.is_lt), "selected_ready")
            dve.wait_ge(sem("router_exp_ready"), nth(dve, "router_exp_ready"))
            step(V.tensor_tensor(rt[:, 16:32], rt[:, 16:32], rt[:, 40:56], ALU.mult))
            step(V.tensor_reduce(rt[:, 36:38], rt[:, 16:32].rearrange("p (t e) -> p t e", t=2), AX.X, ALU.add))
            step(V.reciprocal(rt[:, 38:40], rt[:, 36:38]))
            step(V.tensor_tensor(rt[:, 200:216].rearrange("p (t e) -> p t e", t=2),
                                 rt[:, 16:32].rearrange("p (t e) -> p t e", t=2),
                                 rt[:, 38:40].unsqueeze(2).to_broadcast([P, 2, 8]), ALU.mult))
            dve.wait_ge(sem("places_ready"), nth(dve, "places_ready"))
            step(V.tensor_copy(rt[:, 216:240], bank(7)[:, 0:24]))
            dg = arena[:, 4096:6144].rearrange("p (e t n) -> p e t n", e=8, t=2)
            for tb in range(2):
                ins = V.tensor_tensor(dg[:, :, tb, :], K(K_ID).unsqueeze(1).to_broadcast([P, 8, P]),
                                      rt[:, 200 + 8 * tb:208 + 8 * tb].unsqueeze(2).to_broadcast([P, 8, P]), ALU.mult)
                if tb == 0:
                    step(ins)
            signal(ins, "combine_diagonals_ready")
            comb = arena[:, 2048:4096]
            dve.wait_ge(sem("combine_ready"), nth(dve, "combine_ready"))
            step(V.tensor_copy(comb, bank(4, 4)))
            place, sel, total = rt[:, 216:232], rt[:, 40:56], rt[:, 232:240]
            step(V.tensor_scalar(place, place, 1.0, None, ALU.add))
            step(V.tensor_tensor(place, place, sel, ALU.mult))
            step(V.tensor_scalar(place, place, -1.0, None, ALU.add))
            step(V.tensor_reduce(rt[:, 240:241], total, AX.X, ALU.max))
            signal(V.tensor_scalar(crowded[0:1, 0:1], rt[0:1, 240:241], float(SLOTS), None, ALU.is_gt),
                   "crowded_ready")
            sel4 = SEL.rearrange("p (e t n) -> p e t n", e=8, t=2)
            selw4 = SELW.rearrange("p (e t n) -> p e t n", e=8, t=2)
            for tb in range(2):
                step(V.tensor_tensor(sel4[:, :, tb, :], K(K_IOTA).unsqueeze(1).to_broadcast([P, 8, P]),
                                     place[:, 8 * tb:8 * tb + 8].unsqueeze(2).to_broadcast([P, 8, P]), ALU.is_equal))
                step(V.tensor_tensor(selw4[:, :, tb, :], sel4[:, :, tb, :],
                                     rt[:, 200 + 8 * tb:208 + 8 * tb].unsqueeze(2).to_broadcast([P, 8, P]), ALU.mult))
            announce("weighted_selection_ready")
            dve.wait_ge(sem("slot_weights_ready"), nth(dve, "slot_weights_ready"))
            step(V.memset(G[:, 0:S], 0.0))
            signal(V.memset(yS, 0.0), "rows_copied")
            announce("accumulators_free")

            def compact_expert(p0, e):
                first = e * FFN + FFN
                dve.wait_ge(sem("tokens_high"), e + 1)
                V.tensor_tensor(xe_low[:, :], bank(2, 2), xe_high[:, :].bitcast(F32), ALU.subtract) \
                    .then_inc(sem("tokens_split"), 1)
                add_rows(e * 4)
                low_part(p0 + 1, first + 2)
                hidden_and_low(p0, e * FFN, first, e * FSTEP + FSTEP, 256, lambda f: bank(6)[:, 0:S])
                low_part(p0 + FFN, first + (FFN + 1))

            def add_rows(count):
                for j in range(4):
                    dve.wait_ge(sem("rows_spread"), count + (j + 1))
                    o = xT[:, j * 512:(j + 1) * 512]
                    V.tensor_tensor(o, o, bank(6 + j % 2), ALU.add).then_inc(sem("rows_added"), 1)
                dve.wait_ge(sem("rows_added"), count + 4)

            def dense_expert(e):
                ffn(panel[0], e)
                w = arena[:, bass.ds(e * S + 2048, S)].unsqueeze(1).to_broadcast([P, 2, S])
                for j in range(4):
                    i = bank(4 + j).rearrange("p (a n) -> p a n", a=2)
                    V.tensor_tensor(arena[:, 6144 + j * 512:6144 + (j + 1) * 512].rearrange("p (a n) -> p a n", a=2),
                                    i, w, ALU.mult).then_inc(sem("expert_weighed"), 1)
                dve.wait_ge(sem("expert_weighed"), e * 4 + 4)
                announce("accumulators_free")
                V.tensor_tensor(xT[:, :], xT[:, :], arena[:, 6144:8192], ALU.add).then_inc(sem("expert_added"), 1)
                dve.wait_ge(sem("expert_added"), e + 1)

            many = dve.value_load(crowded[0:1, 0:1], min_val=0, max_val=1)
            with dve.If(many == 1):
                with dve.Fori(0, E) as e:
                    dense_expert(e)
            with dve.Else():
                low_part(panel[0], FFN + 1)
                with dve.Fori(0, E) as e:
                    compact_expert(panel[0], e)
                add_rows(4 * E)
                dve.wait_ge(sem("panel_split"), (E + 1) * FFN + 1)
            panel[0] += E * FFN
            announce("combine_free")
            announce("x_done")
            norm(S_FIN, out3=x3, name="x_done")

            def hyena_filters():
                dve.wait_ge(sem("filter_tables_landed"), nth(dve, "filter_tables_landed", 16 * 7))
                arg = proj[0:64, 2944:3200]
                turn = proj[0:64, 3200:3456]
                for n in range(2):
                    dve.wait_ge(sem("filter_hidden_sum"), nth(dve, "filter_hidden_sum"))
                    step(V.tensor_scalar(arg, bank(1)[0:64, 0:S], sml[0:64, S_HYP + n:S_HYP + n + 1],
                                         sml[0:64, S_HYP + 2:S_HYP + 3], ALU.add, ALU.mult))
                    step(V.tensor_scalar(turn, arg, 1.0 / (2 * PI), None, ALU.mult))
                    step(V.tensor_scalar(turn, turn, 12582912.0, None, ALU.add))
                    step(V.tensor_scalar(turn, turn, 12582912.0, None, ALU.subtract))
                    for part in (6.28125, 0.0019350051879882812, 3.019916050561733e-07):
                        step(V.scalar_tensor_tensor(arg, turn, -part, arg, ALU.mult, ALU.add))
                    signal(V.tensor_scalar(arg, arg, 3.1415925, -3.1415925, ALU.min, ALU.max), "filter_phase_ready")
                for o in range(2):
                    dve.wait_ge(sem("filter_taps_sum"), nth(dve, "filter_taps_sum"))
                    for tb in range(2):
                        d = proj[:, 8192 + tb * 512:8192 + (tb + 1) * 512].unsqueeze(1).to_broadcast([P, 2, 512])
                        step(V.tensor_tensor(proj[:, 4096 + tb * 1024:4096 + (tb + 1) * 1024]
                                             .rearrange("p (d n) -> p d n", d=2), ps[:, 2 * tb:2 * tb + 2, :], d,
                                             ALU.mult))
                    signal(V.memset(proj[0:1, 4608:5120], 0.0), "taps_ready")
                    dve.wait_ge(sem("taps_root_ready"), nth(dve, "taps_root_ready"))
                    rn = proj[:, 11264:11776]
                    signal(V.reciprocal(rn, rn), "taps_rnorm_ready")
                    dve.wait_ge(sem("spectrum_sum"), nth(dve, "spectrum_sum"))
                    for m in range(2):
                        for cs in range(2):
                            t = arena[:, ((o * 2 + m) * 2 + cs) * 512:][:, 0:512]
                            step(V.tensor_tensor(t, bank(4 + 2 * m + cs), rn, ALU.mult))
                            if cs == 0:
                                step(V.tensor_tensor(t, t, proj[:, 11776 + o * 512:11776 + (o + 1) * 512], ALU.add))
                    announce("filter_spectrum_ready")

            def modulate(layer):
                dve.wait_ge(sem("context_landed"), 16)
                panel[0] += ADA
                p0 = panel[0]
                dve.wait_ge(sem("root_ready"), nth(dve, "root_ready"))
                step(V.reciprocal(rstd[:, :], rstd[:, :]))
                narrow_part(p0, 1)
                dve.wait_ge(sem("ada_turned"), nth(dve, "ada_turned"))
                step(V.tensor_tensor(ada[:, :].rearrange("p (c s) -> p c s", s=2),
                                     bank(7)[:, 0:48].rearrange("p (c s) -> p c s", s=2),
                                     sml[:, S_ADA + 24 * layer:S_ADA + 24 * layer + 24].unsqueeze(2)
                                     .to_broadcast([P, 24, 2]), ALU.add))
                g = sml[:, S_NG + layer * KD:S_NG + (layer + 1) * KD].unsqueeze(2).to_broadcast([P, KD, 2])
                step(V.scalar_tensor_tensor(ada_a[:, :].rearrange("p (c s) -> p c s", s=2),
                                            ada[:, 16:32].rearrange("p (c s) -> p c s", s=2), 1.0, g,
                                            ALU.add, ALU.mult))
                for k in range(KD):
                    for s, src in enumerate((x3, c3)):
                        V.scalar_tensor_tensor(h3[:, k, s * S:(s + 1) * S], src[:, k, :],
                                               ada_a[:, 2 * k + s:2 * k + s + 1], rstd[:, s * S:(s + 1) * S],
                                               ALU.mult, ALU.mult).then_inc(sem("h_scaled"), 1)
                narrow_part(p0, 0)
                for k in range(KD):
                    for s in range(2):
                        dve.wait_ge(sem("h_mod_high"), nth(dve, "h_mod_high"))
                        a = slice(s * S, (s + 1) * S)
                        V.scalar_tensor_tensor(h_parts[:, k, a], h3[:, k, a], ada[:, 2 * k + s:2 * k + s + 1],
                                               y_parts[:, k, a].bitcast(F32), ALU.add, ALU.subtract) \
                            .then_inc(sem("h_mod_split"), 1)
                for p in range(2, IN2):
                    narrow_part(p0, p)
                    if layer == 0 and 6 <= p < 12:
                        dve.wait_ge(sem("pair_copied"), p - 2)
                        short_conv(2 * (p - 6))
                        short_conv(2 * (p - 6) + 1)
                if layer == 0:
                    announce("short_conv_done")

            def short_conv(j):
                hu = proj[:, (C_HU + j) * 512:(C_HU + j + 1) * 512]
                t = arena[:, 8192 + (j % 2) * 512:8704 + (j % 2) * 512]
                src, dst = (a.rearrange("p (s t) -> p s t", s=2) for a in (hu, t))
                w = lambda n: sml[:, S_CW + 3 * j + n:S_CW + 3 * j + n + 1]
                step(V.tensor_scalar(dst, src, w(1), sml[:, S_CB + j:S_CB + j + 1], ALU.mult, ALU.add))
                step(V.scalar_tensor_tensor(dst[:, :, 1:S], src[:, :, 0:S - 1], w(0), dst[:, :, 1:S],
                                            ALU.mult, ALU.add))
                step(V.scalar_tensor_tensor(dst[:, :, 0:S - 1], src[:, :, 1:S], w(2), dst[:, :, 0:S - 1],
                                            ALU.mult, ALU.add))
                step(V.tensor_copy(hu, t))

            def narrow_part(p0, p):
                q = p0 + p
                dve.wait_ge(sem("wide_panel_high"), nth(dve, "wide_panel_high"))
                V.tensor_tensor(wide_low(q, 0, PW), ring[:, (q % RING) * PW:(q % RING + 1) * PW],
                                N_high[p % 2].bitcast(F32), ALU.subtract).then_inc(sem("wide_panel_split"), 1)

            def qk_norm(layer):
                for i, (c, n, g, rope) in enumerate(qk_chunks(layer)):
                    dve.wait_ge(sem("qk_root_ready"), nth(dve, "qk_root_ready"))
                    r = qk_root(i)[:, 0:n]
                    q = proj[:, c * 512:c * 512 + n]
                    step(V.reciprocal(r, r))
                    signal(V.scalar_tensor_tensor(q, q, sml[:, S_QK + g:S_QK + g + 1], r, ALU.mult, ALU.mult),
                           "qk_normed")
                    if not rope:
                        continue
                    dve.wait_ge(sem("qk_swapped"), nth(dve, "qk_swapped"))
                    t = arena[:, 7168:7168 + S]
                    qx = proj[:, c * 512:c * 512 + S]
                    step(V.tensor_tensor(t, bank(2 + i % 2)[:, 0:S], K(K_SIN, S), ALU.mult))
                    step(V.tensor_tensor(qx, qx, K(K_COS, S), ALU.mult))
                    step(V.tensor_tensor(qx, qx, t, ALU.add))
                announce("qk_done")

            def hyena():
                dve.wait_ge(sem("y_gates_ready"), nth(dve, "y_gates_ready"))
                dve.wait_ge(sem("natural_copied"), nth(dve, "natural_copied", 8))
                nat = yT[:, :]
                for o in range(2):
                    for s in range(2):
                        dve.wait_ge(sem("z_spectrum_ready"), nth(dve, "z_spectrum_ready"))
                        Y = hT[:, s * 2048:(s + 1) * 2048]
                        for m in range(2):
                            T = lambda cs: arena[:, ((o * 2 + m) * 2 + cs) * 512:][:, 0:512]
                            A, Bk = bank(2 * m), bank(2 * m + 1)
                            t0 = arena[:, 6144:6656]
                            re, im = Y[:, 2 * m * 512:(2 * m + 1) * 512], Y[:, (2 * m + 1) * 512:(2 * m + 2) * 512]
                            step(V.tensor_tensor(re, A, T(0), ALU.mult))
                            step(V.tensor_tensor(t0, Bk, T(1), ALU.mult))
                            step(V.tensor_tensor(re, re, t0, ALU.subtract))
                            step(V.tensor_tensor(im, A, T(1), ALU.mult))
                            step(V.tensor_tensor(t0, Bk, T(0), ALU.mult))
                            step(V.tensor_tensor(im, im, t0, ALU.add))
                        announce("y_spectrum_ready")
                        dve.wait_ge(sem("hyena_inverse_ready"), nth(dve, "hyena_inverse_ready"))
                        if o == 0:
                            part1 = nat[:, 2048 + s * 1024:2048 + (s + 1) * 1024]
                            signal(V.tensor_tensor(nat[:, s * 1024:(s + 1) * 1024], bank(4, 2), part1, ALU.mult),
                                   "hyena_z_ready")
                        else:
                            p2 = proj[:, (C_HU + 8) * 512:(C_HU + 12) * 512].rearrange("p (c n) -> p c n", c=4)
                            g = proj[:, C_HG * 512:(C_HG + 4) * 512].rearrange("p (c n) -> p c n", c=4)
                            a = slice(s * S, (s + 1) * S)
                            step(V.tensor_tensor(p2[:, :, a], p2[:, :, a], g[:, :, a], ALU.mult))
                            signal(V.tensor_tensor(y3[:, 4:8, a], bank(4, 2).rearrange("p (c n) -> p c n", c=4),
                                                   p2[:, :, a], ALU.mult), "hyena_y_done")

            def attend(layer):
                us = attention_units(layer)
                n = len(us)
                if layer == 1:
                    dve.wait_ge(sem("y_gates_ready"), nth(dve, "y_gates_ready"))
                    dve.wait_ge(sem("position_bias_landed"), 16 * 32)
                    m = K(K_NBR, S).unsqueeze(1).to_broadcast([P, 16, S])
                    b = arena[:, 0:4096].rearrange("p (a n) -> p a n", a=16)
                    step(V.tensor_tensor(b, b, m, ALU.add))
                for i in range(n + 4):
                    if i < n:
                        u = us[i]
                        dve.wait_ge(sem("scores_ready"), nth(dve, "scores_ready"))
                        mx = stat[:, i % 4:i % 4 + 1]
                        nm = stat[:, 4 + i % 4:5 + i % 4]
                        if u["kind"] == "plain":
                            step(V.tensor_reduce(mx, bank(i % 2)[:, 0:u["keys"]], AX.X, ALU.max))
                            signal(V.tensor_scalar(nm, mx, -0.125, None, ALU.mult), "max_ready")
                        else:
                            sc = scores_sb(i)
                            rows = lambda a: a.rearrange("p (r c) -> p r c", r=4)
                            step(V.scalar_tensor_tensor(rows(sc[:, 0:S]), rows(bank(i % 2)[:, 0:S]), 0.125,
                                                        u["mask"], ALU.mult, ALU.add))
                            w = 512
                            if u["kind"] == "window":
                                step(V.tensor_copy(sc[:, 512:513], u["sink"]))
                                w = 513
                            dve.wait_ge(sem("context_scores_ready"), nth(dve, "context_scores_ready"))
                            step(V.tensor_reduce(mx, sc[:, 0:w], AX.X, ALU.max))
                            signal(V.tensor_scalar(nm, mx, -1.0, None, ALU.mult), "max_ready")
                    if 1 <= i <= n:
                        j = i - 1
                        dve.wait_ge(sem("probs_scaled_exp"), nth(dve, "probs_scaled_exp"))
                        pr = probs(j)[:, 0:us[j]["keys"]]
                        rs = stat[:, 12 + j % 4:13 + j % 4]
                        step(V.reciprocal(rs, stat[:, 8 + j % 4:9 + j % 4]))
                        signal(V.tensor_scalar(pr, pr, rs, None, ALU.mult), "probs_ready")
                    if i >= 4:
                        u = us[i - 4]
                        dve.wait_ge(sem("o_ready"), nth(dve, "o_ready"))
                        o = bank(4 + (i - 4) % 2)[u["half"] * 64:u["half"] * 64 + 64, 0:P]
                        signal(V.tensor_tensor(u["y"], o, u["gate"], ALU.mult), "o_gated")
                announce("y2_ready")

            def out2(layer):
                for j in range(OUTP):
                    multiplied(1)
                    for m in range(2):
                        for s, dst in enumerate((x3, c3)[:2 - layer]):
                            c = 2 * j + m
                            step(V.scalar_tensor_tensor(
                                dst[:, c, :], bank(c)[:, s * S:(s + 1) * S],
                                ada[:, 32 + 2 * c + s:33 + 2 * c + s], dst[:, c, :], ALU.mult, ALU.add))
                announce("x_done")
                announce("ada_done")

            hyena_filters()
            for layer in range(2):
                modulate(layer)
                panel[0] += IN2
                qk_norm(layer)
                if layer == 0:
                    hyena()
                attend(layer)
                out2(layer)


def _columns(w):
    n = w.shape[1] // 256
    return w.reshape(KD, P, n, 256).transpose(2, 1, 0, 3).reshape(n, P, PW)


def _branch(w):
    return w.reshape(4, P, 2, 512).transpose(2, 1, 0, 3).reshape(2, P, PW)


def _rows(w):
    return w.reshape(FSTEP, 2, P, D).transpose(0, 2, 1, 3).reshape(FSTEP, P, PW)


def _chunks(v):
    return v.reshape(-1, P).T


def kernel(**inputs):
    import concourse.bacc as _bacc
    from concourse.bass_utils import run_bass_kernel_spmd as _run

    a = {k: np.asarray(v) for k, v in inputs.items()}
    panels = np.empty((PANELS, P, PW), np.float32)
    at = 0

    def put(block):
        nonlocal at
        panels[at:at + len(block)] = block
        at += len(block)

    def put_ffn(gate, up, down):
        g, u, d = _columns(gate), _columns(up), _rows(down)
        put(g[0:1])
        put(u[0:1])
        for f in range(1, FSTEP):
            put(g[f:f + 1])
            put(u[f:f + 1])
            put(d[f - 1:f])
        put(d[FSTEP - 1:])

    for layer in range(2):
        w = a["w_in"][layer]
        hq, hf, hi, hog, sq, sk, sv, ga, gb = np.split(w, [512, 1024, 1536, 2048, 2560, 3072, 3584, 4608], 1)
        for part in (hq, hf, hog, sq, sk, ga, gb, hi, sv):
            put(_columns(part))
        A, B = _branch(a["w_branch_hgrn"][layer]), _branch(a["w_branch_sb"][layer])
        for j in range(2):
            put(A[j:j + 1])
            put(B[j:j + 1])
        put(_columns(a["w_out"][layer]))
        if layer == 0:
            put_ffn(a["dense_w_gate"][0], a["dense_w_up"][0], a["dense_w_down"][0])
        else:
            for e in range(E):
                put_ffn(a["moe_w_gate"][0, e], a["moe_w_up"][0, e], a["moe_w_down"][0, e])
    heads = np.arange(512).reshape(2, 4, 64).transpose(1, 0, 2).reshape(-1)
    for layer in range(2):
        put(_columns(a["w_ada_2"][layer]))
        cols = np.arange(3328)
        cols[0:512] = heads
        cols[2304:2816] = 2304 + heads
        put(_columns(a["w_in_2"][layer][:, cols]))
        rows = np.arange(1024)
        rows[0:512] = heads
        put(_columns(a["w_out_2"][layer][rows]))
    assert at == PANELS

    small = np.zeros((P, S_N), np.float32)
    small[:, S_MIX:S_MIX + 16] = _chunks(a["mix_norm"])
    small[:, S_FFN:S_FFN + 16] = _chunks(a["ffn_norm"])
    small[:, S_FIN:S_FIN + 8] = _chunks(a["final_norm"])
    small[:, S_NG:S_NG + 16] = _chunks(a["norm_g_2"])
    small[:, S_ON:S_ON + 2] = _chunks(a["hgrn_out_norm"])
    small[:, S_LB:S_LB + 8] = _chunks(a["hgrn_lb_logits"])
    for i, name in enumerate(("glob_q_norm_2", "glob_k_norm_2", "win_q_norm_2", "win_k_norm_2", "nat_q_norm_2",
                              "nat_k_norm_2")):
        small[:, S_QK + i] = np.concatenate([a[name][0]] * 2)
    small[:, S_CW:S_CW + 36] = a["hy_conv_w_2"][0].reshape(3, 12, P).transpose(2, 1, 0).reshape(P, 36)
    small[:, S_CB:S_CB + 12] = _chunks(a["hy_conv_b_2"])
    small[:, S_SINK:S_SINK + 8] = a["win_sink_2"][0][None, :]
    small[:, S_ADA:S_ADA + 48] = _chunks(a["b_ada_2"])
    small[:, S_ROUT:S_ROUT + 64] = a["moe_router"][0].reshape(KD, P, E).transpose(1, 0, 2).reshape(P, 64)
    both = np.stack([a["c_2"][0], a["c_ctx_2"]])
    small[:, S_COND:S_COND + 16] = both.reshape(2, KD, P).transpose(2, 1, 0).reshape(P, 16)
    for i, name in enumerate(("hy_b1_2", "hy_b2_2", "hy_freq_2")):
        small[0:64, S_HYP + i] = a[name][0]

    def tokens(t):
        return np.ascontiguousarray(t[0].reshape(S, KD, P).transpose(2, 1, 0).reshape(P, KD * S))

    arrays = dict(
        panels=panels, x=tokens(a["x"]), ctx=tokens(a["ctx_2"]), consts=constants(), small=small, dft=dft_tables(),
        decay=decay_table(), position=position_table(), w1=a["hy_w1_2"][0], w2=a["hy_w2_2"][0], w3=a["hy_w3_2"][0],
        skip=a["hy_skip_2"].reshape(1024), rpb=a["nat_rpb_2"][0, :, :, ::-1].reshape(-1))
    arrays = {k: np.ascontiguousarray(v) for k, v in arrays.items()}
    nc = _bacc.Bacc("TRN2", target_bir_lowering=False, num_devices=1)
    args = [nc.dram_tensor(k, v.shape, F32, kind="ExternalInput").ap() for k, v in arrays.items()]
    out = nc.dram_tensor("y", (P, KD * S), F32, kind="ExternalOutput").ap()
    two_blocks(nc, *args, out)
    got = _run(nc, [arrays], core_ids=[0]).results[0]["y"]
    return np.ascontiguousarray(got.reshape(P, KD, S).transpose(2, 1, 0).reshape(1, S, D))
```
